# Optimizing a Trainium2 kernel written in Bass

```python
import functools
import jax, jax.numpy as jnp
from jax import lax
import numpy as np

D_MODEL = 1024
BATCH = 1
SEQ = 1024
DEPTH = 1
DEC_BATCH = 8
DEC_SEQ = 1
PAST_LEN = 2048
PAGE_SIZE = 128

SSM_EXPAND = 2
D_INNER = SSM_EXPAND * D_MODEL
SSM_HEAD_DIM = 64
SSM_HEADS = D_INNER // SSM_HEAD_DIM
SSM_GROUPS = 4
SSM_HPG = SSM_HEADS // SSM_GROUPS
D_STATE = 128
CONV_W = 4
CONV_DIM = D_INNER + 2 * SSM_GROUPS * D_STATE
SSD_CHUNK = 128
SB_HEAD_DIM = 64
SB_HEADS = D_MODEL // SB_HEAD_DIM
SB_KV_HEADS = 4
SB_REP = SB_HEADS // SB_KV_HEADS
SB_Q_BLOCK = 128
SB_SCALE = SB_HEAD_DIM ** -0.5
SB_BIAS_INIT = -7.0
D_FF = 4 * D_MODEL
DEEPNORM_ALPHA = (2.0 * DEPTH) ** 0.25
DEEPNORM_BETA = (8.0 * DEPTH) ** -0.25
LN_EPS = 1e-5
RMS_EPS = 1e-5
IN_SIZES = (D_INNER, CONV_DIM, SSM_HEADS, SB_HEADS * SB_HEAD_DIM,
            SB_KV_HEADS * SB_HEAD_DIM, SB_KV_HEADS * SB_HEAD_DIM, 2 * D_MODEL)
IN_DIM = sum(IN_SIZES)
IN_SPLITS = tuple(int(s) for s in np.cumsum(IN_SIZES)[:-1])

kernel_name = "hybrid_ssd_stickbreak_deepnorm_step"

def layer_norm(x, g, b):
    xf = x.astype(jnp.float32)
    mu = jnp.mean(xf, -1, keepdims=True)
    var = jnp.mean(jnp.square(xf - mu), -1, keepdims=True)
    return ((xf - mu) * lax.rsqrt(var + LN_EPS) * g + b).astype(x.dtype)

def gated_rms_norm(y, z, w):
    h = y.astype(jnp.float32) * jax.nn.silu(z.astype(jnp.float32))
    h = h * lax.rsqrt(jnp.mean(h * h, -1, keepdims=True) + RMS_EPS)
    return (h * w).astype(z.dtype)

def causal_dwconv(xbc, prev, w, b):
    seqlen = xbc.shape[1]
    xp = jnp.concatenate([prev.astype(xbc.dtype), xbc], axis=1)
    out = b + xp[:, 0:seqlen] * w[0]
    for tap in range(1, CONV_W):
        out = out + xp[:, tap:tap + seqlen] * w[tap]
    return jax.nn.silu(out), xp[:, -(CONV_W - 1):]

def ssd_scan(x, dt, a, bm, cm, h0):
    bsz, seqlen = x.shape[:2]
    q = min(SSD_CHUNK, seqlen)
    nc = seqlen // q
    xc = x.reshape(bsz, nc, q, SSM_GROUPS, SSM_HPG, SSM_HEAD_DIM)
    dtc = dt.reshape(bsz, nc, q, SSM_GROUPS, SSM_HPG)
    bc = bm.reshape(bsz, nc, q, SSM_GROUPS, D_STATE)
    cc = cm.reshape(bsz, nc, q, SSM_GROUPS, D_STATE)
    cum = jnp.cumsum(dtc * a.reshape(SSM_GROUPS, SSM_HPG), axis=2)
    cum_t = jnp.moveaxis(cum, 2, -1)
    causal = jnp.tril(jnp.ones((q, q), dtype=bool))
    seg = cum_t[..., :, None] - cum_t[..., None, :]
    decay = jnp.exp(jnp.where(causal, seg, -jnp.inf))
    xdt = xc * dtc[..., None]
    cb = jnp.einsum('bclgn,bcsgn->bcgls', cc, bc)
    y_diag = jnp.einsum('bcgrls,bcsgrp->bclgrp', decay * cb[:, :, :, None], xdt)
    to_end = jnp.exp(cum[:, :, -1:] - cum)
    st = jnp.einsum('bclgn,bclgrp->bcgrpn', bc, xdt * to_end[..., None])
    chunk_decay = jnp.exp(cum[:, :, -1])

    def carry(h, inp):
        s_c, d_c = inp
        return h * d_c[..., None, None] + s_c, h

    h_last, h_in = lax.scan(
        carry, h0.reshape(bsz, SSM_GROUPS, SSM_HPG, SSM_HEAD_DIM, D_STATE),
        (jnp.moveaxis(st, 1, 0), jnp.moveaxis(chunk_decay, 1, 0)))
    h_in = jnp.moveaxis(h_in, 0, 1)
    y_off = jnp.einsum('bclgn,bcgrpn->bclgrp', cc, h_in) * jnp.exp(cum)[..., None]
    y = (y_diag + y_off).reshape(bsz, seqlen, SSM_HEADS, SSM_HEAD_DIM)
    return y, h_last.reshape(bsz, SSM_HEADS, SSM_HEAD_DIM, D_STATE)

def stick_breaking(q, k, v, bias, q_pos, k_pos):
    z = jnp.einsum('bqgrd,bkgd->bgrqk', q, k).astype(jnp.float32) * SB_SCALE
    z = z + bias.astype(jnp.float32).reshape(SB_KV_HEADS, SB_REP)[:, :, None, None]
    mask = k_pos[None, :] < q_pos[:, None]
    log_beta = jax.nn.log_sigmoid(z)
    log_keep = jnp.where(mask, log_beta - z, 0.0)
    after = lax.cumsum(log_keep, axis=4, reverse=True) - log_keep
    w = jnp.where(mask, jnp.exp(log_beta + after), 0.0)
    return jnp.einsum('bgrqk,bkgd->bqgrd', w.astype(v.dtype), v)

def sb_prompt(q, k, v, bias):
    bsz, seqlen = q.shape[:2]
    nb = seqlen // SB_Q_BLOCK
    qb = jnp.moveaxis(q.reshape(bsz, nb, SB_Q_BLOCK, SB_KV_HEADS, SB_REP, SB_HEAD_DIM), 1, 0)
    k_pos = jnp.arange(seqlen)

    def block(args):
        q_blk, i = args
        q_pos = i * SB_Q_BLOCK + jnp.arange(SB_Q_BLOCK)
        return stick_breaking(q_blk, k, v, bias, q_pos, k_pos)

    o = lax.map(block, (qb, jnp.arange(nb)))
    return jnp.moveaxis(o, 0, 1).reshape(bsz, seqlen, SB_HEADS * SB_HEAD_DIM)

def sb_decode(q, k, v, bias, k_past, v_past):
    past = k_past.shape[1]
    tq = q.shape[1]
    k_all = jnp.concatenate([k_past.astype(k.dtype), k], axis=1)
    v_all = jnp.concatenate([v_past.astype(v.dtype), v], axis=1)
    o = stick_breaking(q, k_all, v_all, bias, past + jnp.arange(tq), jnp.arange(past + tq))
    return o.reshape(q.shape[0], tq, SB_HEADS * SB_HEAD_DIM)

def gather_pages(cache, page_table):
    g = cache[page_table]
    return g.reshape(page_table.shape[0], page_table.shape[1] * PAGE_SIZE, SB_KV_HEADS, SB_HEAD_DIM)

def trunk_layer(x, conv_prev, ssm_h0, attend, w_in, conv_w, conv_b, dt_bias, a_log, d_skip,
                ssm_norm_w, w_ssm_br, w_attn_br, sb_logit_bias, w_out, ln1_g, ln1_b,
                w_up, w_down, ln2_g, ln2_b):
    bsz, seqlen, _ = x.shape
    f32 = jnp.float32
    proj = x @ w_in
    z, xbc, dt, q, k, v, gates = jnp.split(proj, IN_SPLITS, axis=-1)
    xbc, conv_state = causal_dwconv(xbc, conv_prev, conv_w, conv_b)
    xs, bm, cm = jnp.split(xbc, [D_INNER, D_INNER + SSM_GROUPS * D_STATE], axis=-1)
    dt = jax.nn.softplus(dt.astype(f32) + dt_bias.astype(f32))
    a = -jnp.exp(a_log.astype(f32))
    xs_h = xs.reshape(bsz, seqlen, SSM_HEADS, SSM_HEAD_DIM).astype(f32)
    y, h_last = ssd_scan(xs_h, dt, a,
                         bm.reshape(bsz, seqlen, SSM_GROUPS, D_STATE).astype(f32),
                         cm.reshape(bsz, seqlen, SSM_GROUPS, D_STATE).astype(f32),
                         ssm_h0.astype(f32))
    y = y + xs_h * d_skip.astype(f32)[:, None]
    y = gated_rms_norm(y.reshape(bsz, seqlen, D_INNER), z, ssm_norm_w)
    ssm_out = y @ w_ssm_br
    q = q.reshape(bsz, seqlen, SB_KV_HEADS, SB_REP, SB_HEAD_DIM)
    k = k.reshape(bsz, seqlen, SB_KV_HEADS, SB_HEAD_DIM)
    v = v.reshape(bsz, seqlen, SB_KV_HEADS, SB_HEAD_DIM)
    attn_out = attend(q, k, v, sb_logit_bias) @ w_attn_br
    g_ssm, g_attn = jnp.split(gates, 2, axis=-1)
    mixed = jax.nn.sigmoid(g_ssm) * ssm_out + jax.nn.sigmoid(g_attn) * attn_out
    x = layer_norm(DEEPNORM_ALPHA * x + mixed @ w_out, ln1_g, ln1_b)
    hid = jnp.square(jax.nn.relu(x @ w_up))
    x = layer_norm(DEEPNORM_ALPHA * x + hid @ w_down, ln2_g, ln2_b)
    return x, k, v, h_last, conv_state

def setup_inputs(seed: int = 0) -> dict:
    key = jax.random.key(seed)
    ks = jax.random.split(key, 24)
    f32 = jnp.float32
    n_pages = PAST_LEN // PAGE_SIZE
    n_used = DEC_BATCH * n_pages
    n_pool = n_used + max(1, n_used // 4)

    def nrm(k, shape, scale):
        return jax.random.normal(k, shape, f32) * scale

    x_prompt = nrm(ks[0], (BATCH, SEQ, D_MODEL), 1.0)
    x_sample = nrm(ks[1], (DEC_BATCH, DEC_SEQ, D_MODEL), 1.0)
    cache_k = nrm(ks[2], (DEPTH, n_pool, PAGE_SIZE, SB_KV_HEADS, SB_HEAD_DIM), 1.0)
    cache_v = nrm(ks[3], (DEPTH, n_pool, PAGE_SIZE, SB_KV_HEADS, SB_HEAD_DIM), 1.0)
    state_ssm = nrm(ks[4], (DEPTH, DEC_BATCH, SSM_HEADS, SSM_HEAD_DIM, D_STATE), 0.5)
    state_conv = nrm(ks[5], (DEPTH, DEC_BATCH, CONV_W - 1, CONV_DIM), 1.0)
    page_table = jax.random.permutation(ks[6], n_pool)[:n_used].reshape(
        DEC_BATCH, n_pages).astype(jnp.int32)

    w_in = nrm(ks[7], (DEPTH, D_MODEL, IN_DIM), D_MODEL ** -0.5)
    conv_w = nrm(ks[8], (DEPTH, CONV_W, CONV_DIM), CONV_W ** -0.5)
    conv_b = nrm(ks[9], (DEPTH, CONV_DIM), 0.01)
    u = jax.random.uniform(ks[10], (DEPTH, SSM_HEADS), f32)
    dt0 = jnp.exp(u * (jnp.log(0.1) - jnp.log(0.001)) + jnp.log(0.001))
    dt_bias = dt0 + jnp.log(-jnp.expm1(-dt0))
    a_log = jnp.log(jax.random.uniform(ks[11], (DEPTH, SSM_HEADS), f32, 1.0, 16.0))
    d_skip = 1.0 + nrm(ks[12], (DEPTH, SSM_HEADS), 0.1)
    ssm_norm_w = 1.0 + nrm(ks[13], (DEPTH, D_INNER), 0.02)
    w_ssm_br = nrm(ks[14], (DEPTH, D_INNER, D_MODEL), D_INNER ** -0.5)
    w_attn_br = nrm(ks[15], (DEPTH, SB_HEADS * SB_HEAD_DIM, D_MODEL), (SB_HEADS * SB_HEAD_DIM) ** -0.5)
    sb_logit_bias = SB_BIAS_INIT + nrm(ks[23], (DEPTH, SB_HEADS), 0.5)
    w_out = nrm(ks[16], (DEPTH, D_MODEL, D_MODEL), DEEPNORM_BETA * D_MODEL ** -0.5)
    ln1_g = 1.0 + nrm(ks[17], (DEPTH, D_MODEL), 0.02)
    ln1_b = nrm(ks[18], (DEPTH, D_MODEL), 0.02)
    w_up = nrm(ks[19], (DEPTH, D_MODEL, D_FF), D_MODEL ** -0.5)
    w_down = nrm(ks[20], (DEPTH, D_FF, D_MODEL), DEEPNORM_BETA * D_FF ** -0.5)
    ln2_g = 1.0 + nrm(ks[21], (DEPTH, D_MODEL), 0.02)
    ln2_b = nrm(ks[22], (DEPTH, D_MODEL), 0.02)
    return {"x_prompt": x_prompt, "x_sample": x_sample, "cache_k": cache_k, "cache_v": cache_v,
            "state_ssm": state_ssm, "state_conv": state_conv, "page_table": page_table,
            "w_in": w_in, "conv_w": conv_w, "conv_b": conv_b, "dt_bias": dt_bias, "a_log": a_log,
            "d_skip": d_skip, "ssm_norm_w": ssm_norm_w, "w_ssm_br": w_ssm_br, "w_attn_br": w_attn_br,
            "sb_logit_bias": sb_logit_bias, "w_out": w_out, "ln1_g": ln1_g, "ln1_b": ln1_b,
            "w_up": w_up, "w_down": w_down, "ln2_g": ln2_g, "ln2_b": ln2_b}

def reference(x_prompt, x_sample, cache_k, cache_v, state_ssm, state_conv, page_table,
              w_in, conv_w, conv_b, dt_bias, a_log, d_skip, ssm_norm_w, w_ssm_br, w_attn_br,
              sb_logit_bias, w_out, ln1_g, ln1_b, w_up, w_down, ln2_g, ln2_b):
    bp = x_prompt.shape[0]
    yp, ys = x_prompt, x_sample
    kp_l, vp_l, hp_l, cp_l = [], [], [], []
    ks_l, vs_l, hs_l, cs_l = [], [], [], []
    for layer in range(DEPTH):
        params = (w_in[layer], conv_w[layer], conv_b[layer], dt_bias[layer], a_log[layer],
                  d_skip[layer], ssm_norm_w[layer], w_ssm_br[layer], w_attn_br[layer],
                  sb_logit_bias[layer], w_out[layer], ln1_g[layer], ln1_b[layer],
                  w_up[layer], w_down[layer], ln2_g[layer], ln2_b[layer])
        conv0 = jnp.zeros((bp, CONV_W - 1, CONV_DIM), yp.dtype)
        h0 = jnp.zeros((bp, SSM_HEADS, SSM_HEAD_DIM, D_STATE), jnp.float32)
        yp, kp, vp, hp, cp = trunk_layer(yp, conv0, h0, sb_prompt, *params)
        attend = functools.partial(sb_decode,
                                   k_past=gather_pages(cache_k[layer], page_table),
                                   v_past=gather_pages(cache_v[layer], page_table))
        ys, ksm, vsm, hsm, csm = trunk_layer(ys, state_conv[layer], state_ssm[layer], attend, *params)
        kp_l.append(kp)
        vp_l.append(vp)
        hp_l.append(hp.astype(x_prompt.dtype))
        cp_l.append(cp)
        ks_l.append(ksm)
        vs_l.append(vsm)
        hs_l.append(hsm.astype(state_ssm.dtype))
        cs_l.append(csm.astype(state_conv.dtype))
    return (yp, ys, jnp.stack(kp_l), jnp.stack(vp_l), jnp.stack(hp_l), jnp.stack(cp_l),
            jnp.stack(ks_l), jnp.stack(vs_l), jnp.stack(hs_l), jnp.stack(cs_l))


_drawn_inputs = setup_inputs


def setup_inputs(seed=0):
    import zlib

    import numpy as np

    out = dict(_drawn_inputs(seed))
    spreads = {}
    factors = {'cache_k': 4.706,
     'cache_v': 3.773,
     'conv_b': 3.12,
     'd_skip': 3.443,
     'ssm_norm_w': 22.234,
     'w_attn_br': 29.472,
     'sb_logit_bias': 64.0,
     'ln1_g': 2.733,
     'ln1_b': 2.782,
     'ln2_g': 7.529,
     'ln2_b': 7.773}
    for name, (base, spread) in spreads.items():
        noise = np.random.default_rng([zlib.crc32(name.encode()), seed]).standard_normal(out[name].shape)
        drawn = base * np.exp(spread * noise) if base else spread * noise
        out[name] = __import__('jax').numpy.asarray(drawn.astype(out[name].dtype))
    for name, factor in factors.items():
        out[name] = (out[name] * factor).astype(out[name].dtype)
    return out
```

```python
import concourse.bass as bass
from concourse import mybir
from contextlib import ExitStack

F32 = mybir.dt.float32
I32 = mybir.dt.int32
ACT = mybir.ActivationFunctionType
ALU = mybir.AluOpType
AX_X = mybir.AxisListType.X
ds = bass.ds

D = 1024
SEQ = 1024
NDEC = 8
T = SEQ + NDEC
TN = T // 3
KT = D // 128
D_INNER = 2048
HEADS = 32
GROUPS = 4
NSTATE = 128
CONV_DIM = D_INNER + 2 * GROUPS * NSTATE
CT = CONV_DIM // 128
CHUNK = 128
NCHUNK = SEQ // CHUNK
SB_HEADS = 16
HD = 64
KV = 4
PAGES = 16
PAST = 2048
N_POOL = 160
D_FF = 4096
COL_Z, COL_X = 0, D_INNER
COL_B = COL_X + D_INNER
COL_C = COL_B + GROUPS * NSTATE
COL_DT = COL_C + GROUPS * NSTATE
COL_Q = COL_DT + HEADS
COL_K = COL_Q + SB_HEADS * HD
COL_V = COL_K + KV * HD
COL_GS = COL_V + KV * HD
COL_GA = COL_GS + D
SCALE = HD ** -0.5
ALPHA = 2.0 ** 0.25
EPS = 1e-5
DT_CUM = 13
FAR = 1e30
RAWLEN = 3 + SEQ + 4 * NDEC
ACCLEN = RAWLEN - 3
DEC0 = SEQ + 3
NPAR = 5 + 3 * NDEC

J_X = 0
J_PAR = J_X + NCHUNK + 1
J_QKV = J_PAR + 2
J_KVT = J_QKV + 12
J_GA = J_KVT + 9
J_ABR = J_GA + 8
J_DT = J_ABR + 8
J_SSD = J_DT + 2
J_GS = J_SSD + 10 * GROUPS
J_RMS = J_GS + 8
J_SBR = J_RMS + 1
J_OUT = J_SBR + 8
J_LN1 = J_OUT + 8
J_UP = J_LN1 + 2
J_DOWN = J_UP + 32
J_LN2 = J_DOWN + 8
J_TAIL = J_LN2 + 2
J_Y = J_TAIL + 2
J_END = J_Y + 9
U_SBR = J_SBR
U_OUT = U_SBR + 16
U_LN1 = U_OUT + 8
U_UP = U_LN1 + 2
U_DOWN = U_UP + 32
U_LN2 = U_DOWN + 32
U_TAIL = U_LN2 + 2
U_Y = U_TAIL + 2
P_QKV = 0
P_GA = P_QKV + 12
P_ABR = P_GA + 8
P_DT = P_ABR
P_SSD = P_DT + 1
P_GS = P_SSD + 10 * GROUPS
P_SBR = P_GS + 8
P_OUT = P_SBR + 16
P_UP = P_OUT + 8
P_DOWN = P_UP + 32


def build(nc, ins, outs):
    y_prompt, y_sample, k_prompt, v_prompt, ssm_prompt, conv_prompt, k_sample, v_sample, ssm_sample, conv_sample = outs
    w_in = ins["w_in"][0].rearrange("(t p) n -> p t n", p=128)
    w_ssm = ins["w_ssm_br"][0].rearrange("(t p) n -> p t n", p=128)
    w_out = ins["w_out"][0].rearrange("(t p) n -> p t n", p=128)
    w_up = ins["w_up"][0].rearrange("(t p) n -> p t n", p=128)
    w_down = ins["w_down"][0].rearrange("(t p) n -> p t n", p=128)
    w_att = ins["w_attn_br"][0].rearrange("(c k i d) n -> k d c i n", c=2, k=2, i=4)
    scr_cum = nc.dram_tensor("scr_cum", [HEADS, SEQ], F32, kind="Internal").ap()
    scr_dec = nc.dram_tensor("scr_dec", [2, HEADS, NDEC], F32, kind="Internal").ap()
    scr_bc = nc.dram_tensor("scr_bc", [GROUPS, 2, NDEC, NSTATE], F32, kind="Internal").ap()

    with ExitStack() as ctx:
        def sb(name, shape, dt=F32):
            return ctx.enter_context(nc.sbuf_tensor(name, shape, dt))

        def sem(name):
            return ctx.enter_context(nc.semaphore(name))

        res = sb("res", [128, KT, T])
        big = sb("big", [128, 32, T])
        wbuf = sb("wbuf", [128, 2, 8, 128])
        work = sb("work", [128, 7168])
        ident = sb("ident", [128, 128])
        ones = sb("ones", [128, 128])
        keep = sb("keep", [128, 128])
        far = sb("far", [128, 128])
        tri = sb("tri", [128, 128])
        par = sb("par", [128, CT, NPAR])
        vec = sb("vec", [128, KT, 6])
        tail = sb("tail", [128, CT, 3 + NDEC])
        cumtok = sb("cumtok", [128, NCHUNK, HEADS])
        dttok = sb("dttok", [128, NCHUNK, HEADS])
        dtx = sb("dtx", [128, 2, 16, NDEC])
        dskip = sb("dskip", [128, 16])
        sbb = sb("sbb", [128, SB_HEADS])
        sbd = sb("sbd", [128, 1])
        dtb = sb("dtb", [HEADS, 1])
        alog = sb("alog", [HEADS, 1])
        pages = sb("pages", [1, NDEC * PAGES], I32)
        eps = sb("eps", [128, 1])
        small = sb("small", [128, 64])
        PS = ctx.enter_context(nc.psum_tensor("PS", [128, 8, 512], F32))

        flat = big[:, :, :].rearrange("p t n -> p (t n)")

        def carve(base, *shape):
            n = 1
            for s in shape:
                n *= s
            return base[:, 0:n] if len(shape) == 1 else base[:, 0:n].rearrange(
                {2: "p (a b) -> p a b", 3: "p (a b c) -> p a b c"}[len(shape)],
                **dict(zip("abc", shape)))

        def area(off, *shape):
            return carve(flat[:, off:], *shape)

        def wk(off, *shape):
            return carve(work[:, off:], *shape)

        qT = big[:, 0:8, :]
        kvT = big[:, 24:28, :]
        mixT = big[:, 16:24, :]
        hT = big[:, 0:16, :]
        xsT = big[:, 24:28, :]
        bT = big[:, 28, :]
        cT = big[:, 29, :]
        gsT = big[:, 24:32, :]
        hidT = big
        xbuf = area(24 * T, 2, 1024)
        xsam = area(26 * T + 512, 1024)
        prow = area(8 * T, CONV_DIM)
        vrow = area(11 * T + 64, 1024)
        kvtok = area(8 * T, 9, 512)
        o = 8 * T + 9 * 512
        qst = area(o, 1024)
        kst = area(o + 1024, 1024)
        vst = area(o + 2048, 8, 128)
        zb = area(o + 3072, 2, 1024)
        lb = area(o + 5120, 2, 1024)
        sbuf_s = area(o + 7168, 2, 1024)
        wTb = area(o + 9216, 2, 8, 128)
        kvst = area(28 * T, 2, 4, 128)
        pbuf = area(8 * T, 2, PAGES, 256)
        o = 8 * T + 2 * PAGES * 256
        zd = area(o, PAST)
        ld = area(o + PAST, PAST)
        sd = area(o + 2 * PAST, PAST)
        wTd = area(o + 3 * PAST, PAGES, 128)
        kTst = area(28 * T, 2, 512)
        qbd = area(28 * T + 1024, NDEC, 2, 128)
        qstd = area(28 * T + 3072, 2, 2, 128)
        raw = wk(0, RAWLEN)
        acc = wk(RAWLEN + 1, ACCLEN)
        sig = wk(RAWLEN + 1 + ACCLEN, ACCLEN)
        cumb = wk(0, 2, 8, 128)
        seg = wk(2048, 8, 128)
        ecm = wk(3072, 8, 128)
        xdt = wk(4096, 8, 64)
        xdte = wk(4608, 8, 64)
        hst = wk(5120, 8, 64)
        btok = wk(5632, 128)
        cbm = wk(5760, 128)
        y1 = wk(5888, 4, 128)
        hout = wk(6400, 4, 128)
        xst = area(30 * T, 2, 4, 128)
        bst = area(30 * T + 1024, 2, 128)
        t8 = small[:, 0:8]
        dte = small[:, 8:16]
        cd = small[:, 16:24]
        xdd = small[:, 24:32]
        yd = small[:, 32:40]
        h0b = wk(0, 2, NDEC, 128)
        t2 = wk(2048, NDEC, 128)
        bcb = wk(3072, 2, NDEC, 128)
        dtr, dte1, dtu, dtl, dtv = [work[0:HEADS, 1040 * n:1040 * n + T] for n in range(5)]
        chm = work[0:HEADS, 5200:5200 + SEQ]
        nacc = wk(0, T)
        nsq = wk(1032, 2, T)
        nbc = wk(3096, T)
        nbc2 = wk(4128, T)
        ytok = area(0, 2, 1024)
        yst = area(3 * T, 2, 8, 128)
        tailrow = area(8 * T, CONV_DIM)

        s_pass = sem("s_pass")
        s_const = sem("s_const")
        s_par = sem("s_par")
        s_small = sem("s_small")
        s_xin = [sem("s_xin0"), sem("s_xin1")]
        s_w = [sem("s_w0"), sem("s_w1")]
        s_unit = sem("s_unit")
        s_psfree = sem("s_psfree")

        block = ctx.enter_context(nc.Block())

        def banks(j, n=3, w=TN):
            return PS[:, 3 * (j % 2):3 * (j % 2) + n, 0:w]

        def tile(t, m):
            return t[:, ds(m, 1), :].rearrange("p o (a b) -> p (o a) b", b=TN)

        s_kst = sem("s_kst")
        s_kvo = sem("s_kvo")
        s_qk = sem("s_qk")
        s_z = sem("s_z")
        s_zs = sem("s_zs")
        s_ab = sem("s_ab")
        s_ex = sem("s_ex")
        s_ln = sem("s_ln")
        s_sp = sem("s_sp")
        s_spm = sem("s_spm")
        s_scan = sem("s_scan")
        s_far = sem("s_far")
        s_d = sem("s_d")
        s_wt = sem("s_wt")
        s_tr = sem("s_tr")
        s_tr1 = sem("s_tr1")
        s_cp = sem("s_cp")
        s_cp1 = sem("s_cp1")
        s_o = sem("s_o")
        s_oc = sem("s_oc")
        s_pt = sem("s_pt")
        s_kp = [sem("s_kp0"), sem("s_kp1")]
        s_wa = [sem("s_wa0"), sem("s_wa1")]
        s_dact = sem("s_dact")
        s_dd = sem("s_dd")
        s_dexp = sem("s_dexp")
        s_tok = sem("s_tok")
        s_nz = sem("s_nz")
        s_nz2 = sem("s_nz2")
        s_cst0 = sem("s_cst0")
        s_yn0 = sem("s_yn0")
        s_rz = sem("s_rz")
        s_yout = [sem("s_yout0"), sem("s_yout1")]
        s_nsum = sem("s_nsum")
        s_dm = sem("s_dm")
        s_rs = sem("s_rs")
        s_yn = sem("s_yn")
        s_qz = sem("s_qz")
        s_qb = sem("s_qb")
        s_qs = sem("s_qs")
        s_dtr = sem("s_dtr")
        s_dcp = sem("s_dcp")
        s_dz = sem("s_dz")
        s_dtw = sem("s_dtw")
        s_dcw = sem("s_dcw")
        s_do = sem("s_do")
        s_doc = sem("s_doc")
        s_dt = sem("s_dt")
        s_dta = sem("s_dta")
        s_scr = sem("s_scr")
        s_dtx = sem("s_dtx")
        s_dtxe = sem("s_dtxe")
        s_zsg = sem("s_zsg")
        s_raw = sem("s_raw")
        s_cv = sem("s_cv")
        s_csg = sem("s_csg")
        s_cout = sem("s_cout")
        s_cb = [sem("s_cb0"), sem("s_cb1")]
        s_stg = sem("s_stg")
        s_tp = sem("s_tp")
        s_bc = sem("s_bc")
        s_t8 = sem("s_t8")
        s_t8e = sem("s_t8e")
        s_dte = sem("s_dte")
        s_cd = sem("s_cd")
        s_xdt = sem("s_xdt")
        s_sg = sem("s_sg")
        s_sg2 = sem("s_sg2")
        s_M = sem("s_M")
        s_Mm = sem("s_Mm")
        s_ec = sem("s_ec")
        s_CE = sem("s_CE")
        s_y = sem("s_y")
        s_st = sem("s_st")
        s_y1 = sem("s_y1")
        s_y2 = sem("s_y2")
        s_hm = sem("s_hm")
        s_hupd = sem("s_hupd")
        s_h0 = sem("s_h0")
        s_ht = sem("s_ht")
        s_hc = sem("s_hc")
        s_ho = sem("s_ho")
        s_bcw = sem("s_bcw")
        s_bcr = sem("s_bcr")
        s_dh = [sem("s_dh0"), sem("s_dh1")]
        s_d1 = sem("s_d1")
        s_d2 = sem("s_d2")
        s_d3 = sem("s_d3")
        s_d4 = sem("s_d4")
        s_d5 = sem("s_d5")
        s_d6 = sem("s_d6")
        s_d7 = sem("s_d7")
        s_d8 = sem("s_d8")
        s_dso = [sem("s_dso0"), sem("s_dso1")]
        s_sq = sem("s_sq")
        s_nac = sem("s_nac")
        s_hn = sem("s_hn")
        s_gr = sem("s_gr")
        s_mix = sem("s_mix")
        s_hid = sem("s_hid")
        s_ys = sem("s_ys")
        s_yo = sem("s_yo")
        s_out = sem("s_out")

        @block.sync
        def _(sp):
            def load(slot, lo, src_lo, hi, src_hi, unit):
                sp.wait_ge(s_unit, unit - 1)
                sp.dma_start(lo, src_lo).then_inc(s_w[slot], 16)
                sp.dma_start(hi, src_hi).then_inc(s_w[slot], 16)

            def load_cols(P, unit, w, k0, col, n=128):
                b = wbuf[:, P % 2]
                load(P % 2, b[:, 0:4, 0:n], w[:, k0:k0 + 4, ds(col, n)], b[:, 4:8, 0:n], w[:, k0 + 4:k0 + 8, ds(col, n)],
                     unit)

            sp.dma_start(prow[0:4, :], ins["conv_w"][0]).then_inc(s_par, 16)
            sp.dma_start(prow[4:5, :], ins["conv_b"]).then_inc(s_par, 16)
            sp.dma_start(prow[5:NPAR, :], ins["state_conv"][0].rearrange("b k c -> (b k) c")).then_inc(s_par, 16)
            for n, name in enumerate(("ln1_g", "ln1_b", "ln2_g", "ln2_b")):
                sp.dma_start(vrow[n:n + 1, :], ins[name]).then_inc(s_par, 16)
            sp.dma_start(vrow[4:6, :], ins["ssm_norm_w"].rearrange("o (a d) -> (o a) d", a=2)).then_inc(s_par, 16)
            for n in range(2):
                sp.dma_start(xbuf[:, n, :], ins["x_prompt"][0, n * 128:(n + 1) * 128, :]).then_inc(s_xin[n], 16)
            sp.dma_start(xsam[0:NDEC, :], ins["x_sample"].rearrange("b o d -> (b o) d")).then_inc(s_small, 16)
            with nc.allow_non_contiguous_dma("small parameters"):
                for k in range(2):
                    src = ins["d_skip"].rearrange("o (j k) -> o k j", k=2)[:, k, :]
                    sp.dma_start(dskip[64 * k:64 * k + 64, :], src.to_broadcast([64, 16])).then_inc(s_small, 16)
                sp.dma_start(sbb[:], ins["sb_logit_bias"].to_broadcast([128, SB_HEADS])).then_inc(s_small, 16)
                for b in range(NDEC):
                    sp.dma_start(sbd[16 * b:16 * b + 16, :], ins["sb_logit_bias"].rearrange("o h -> h o")).then_inc(s_small, 16)
                sp.dma_start(dtb[:], ins["dt_bias"].rearrange("o h -> h o")).then_inc(s_small, 16)
                sp.dma_start(alog[:], ins["a_log"].rearrange("o h -> h o")).then_inc(s_small, 16)
            sp.dma_start(pages[:], ins["page_table"].rearrange("b n -> (b n)").rearrange("(o n) -> o n", o=1)).then_inc(s_pt, 16)
            with sp.Fori(1, NCHUNK // 2) as r:
                for j in range(2):
                    sp.wait_ge(s_unit, 2 * r + j - 1)
                    sp.dma_start(xbuf[:, j, :], ins["x_prompt"][0, ds(r * 256 + j * 128, 128), :]).then_inc(s_xin[j], 16)

            for c in range(2):
                with sp.Fori(0, 2) as r:
                    for j in range(2):
                        n = 4 * c + j
                        cols = [COL_Q + 512 * c + 256 * k + 64 * j for k in range(2)]
                        b = wbuf[:, n % 2]
                        load(n % 2, b[:, :, 0:64], w_in[:, :, ds(r * 128 + cols[0], 64)],
                             b[:, :, 64:128], w_in[:, :, ds(r * 128 + cols[1], 64)], J_QKV + n + 2 * r)
            with sp.Fori(0, 2) as r:
                for j in range(2):
                    load_cols(P_QKV + 8 + j, J_QKV + 8 + j + 2 * r, w_in, 0, r * 256 + (COL_K + 128 * j))

            sp.wait_ge(s_psfree, J_GA + 2)
            for t, po, so in ((0, k_prompt, k_sample), (256, v_prompt, v_sample)):
                sp.dma_start(po[0, 0].rearrange("(t p) g d -> p t (g d)", p=128), kvtok[:, 0:8, t:t + 256]).then_inc(s_kvo, 16)
                sp.dma_start(so[0].rearrange("b o g d -> (b o) (g d)"), kvtok[0:NDEC, 8, t:t + 256]).then_inc(s_kvo, 16)

            sp.wait_ge(s_pt, 16)
            sp.wait_ge(s_kvo, 64)
            sp.wait_ge(s_oc, 130)
            def load_pages(cache, r, j):
                with sp.Fori(0, PAGES) as i:
                    page = sp.value_load(pages[0:1, ds(r * 2 * PAGES + (i + j * PAGES), 1)], min_val=0, max_val=N_POOL - 1)
                    sp.dma_start(pbuf[:, j, ds(i, 1), :],
                                 ins[cache][0, ds(page, 1)].rearrange("o t g d -> t o (g d)")).then_inc(s_kp[j], 16)

            for j in range(2):
                load_pages("cache_k", 0, j)
            with sp.Fori(1, NDEC // 2) as r:
                for j in range(2):
                    sp.wait_ge(s_dtr, 16 * r + 8 * (j - 1))
                    sp.sem_inc(s_pass, 1)
                    load_pages("cache_k", r, j)
            sp.wait_ge(s_dtr, 64)
            for j in range(2):
                load_pages("cache_v", 0, j)
            with sp.Fori(1, NDEC // 2) as r:
                for j in range(2):
                    sp.wait_ge(s_do, 2 * r + j - 1)
                    sp.sem_inc(s_pass, 1)
                    load_pages("cache_v", r, j)

            with sp.Fori(0, 4) as r:
                for j in range(2):
                    load_cols(P_GA + j, J_GA + j + 2 * r, w_in, 0, r * 256 + (COL_GA + 128 * j))
            with sp.Fori(0, 4) as r:
                for j in range(2):
                    b = wbuf[:, (P_ABR + j) % 2]
                    sp.wait_ge(s_unit, J_ABR + j - 1 + 2 * r)
                    for k in range(2):
                        for c in range(2):
                            sp.dma_start(b[64 * k:64 * k + 64, 4 * c:4 * c + 4, :],
                                         w_att[k, :, c, :, ds(r * 256 + 128 * j, 128)]).then_inc(s_wa[(P_ABR + j) % 2], 16)

            load_cols(P_DT, J_DT, w_in, 0, COL_DT, HEADS)

            sp.wait_ge(s_dt, DT_CUM)
            sp.dma_start(scr_cum, dtv[:, 0:SEQ]).then_inc(s_scr, 16)
            sp.dma_start(scr_dec[0], dtl[:, SEQ:T]).then_inc(s_scr, 16)
            sp.dma_start(scr_dec[1], dtr[:, SEQ:T]).then_inc(s_scr, 16)
            sp.wait_ge(s_scr, 48)
            for n in range(2):
                for k in range(2):
                    src = scr_dec[n].rearrange("(j k) b -> k j b", k=2)[k:k + 1]
                    sp.dma_start(dtx[64 * k:64 * k + 64, n], src.to_broadcast([64, 16, NDEC])).then_inc(s_dtx, 16)

            with sp.Fori(0, GROUPS) as g:
                for n in range(4):
                    load_cols(P_SSD + n, J_SSD + n + 10 * g, w_in, 0, g * 512 + (COL_Z + 128 * n))
                for n in range(4):
                    load_cols(P_SSD + 4 + n, J_SSD + 4 + n + 10 * g, w_in, 0, g * 512 + (COL_X + 128 * n))
                load_cols(P_SSD + 8, J_SSD + 8 + 10 * g, w_in, 0, g * 128 + COL_B)
                load_cols(P_SSD + 9, J_SSD + 9 + 10 * g, w_in, 0, g * 128 + COL_C)
                sp.wait_ge(s_cout, 6 * g + 8)
                sp.sem_inc(s_pass, 1)
                with sp.Fori(0, NCHUNK // 2) as r:
                    for j in range(2):
                        sp.wait_ge(s_hupd, g * 8 + 2 * r + (j + 1))
                        src = scr_cum[ds(g * 8, 8), ds(r * 256 + j * 128, 128)]
                        sp.dma_start(cumb[:, j], src.rearrange("(o h) l -> o h l", o=1).to_broadcast([128, 8, 128])).then_inc(s_cb[j], 16)
                sp.wait_ge(s_hc, g + 3)
                sp.dma_start(ssm_prompt[0, 0].rearrange("h p n -> (h p) n")[ds(g * 512, 512), :].rearrange("(j q) n -> q j n", q=128),
                             hout[:]).then_inc(s_ho, 16)
                with nc.allow_non_contiguous_dma("B, C of the decode tokens, token-major"):
                    for n, t in enumerate((bT, cT)):
                        sp.dma_start(scr_bc[ds(g, 1), n].rearrange("o b s -> s (o b)"), t[:, SEQ:T]).then_inc(s_bcw, 16)
                sp.wait_ge(s_bcw, 32 * g + 32)
                sp.wait_ge(s_hupd, 8 * g + 10)
                sp.wait_ge(s_ho, 16 * g + 32)
                sp.dma_start(bcb[:], scr_bc[ds(g, 1)].to_broadcast([128, 2, NDEC, NSTATE])).then_inc(s_bcr, 16)
                with sp.Fori(0, 2) as r:
                    for j in range(2):
                        sp.wait_ge(s_d8, g * 4 + 2 * r + (j + 1))
                        sp.wait_ge(s_dso[j], g * 32 + 16 * r + 16)
                        src = ins["state_ssm"][0].rearrange("b h p n -> (h p) b n")[ds(g * 512 + r * 256 + j * 128, 128)]
                        sp.dma_start(h0b[:, j], src).then_inc(s_dh[j], 16)

            with sp.Fori(0, 4) as r:
                for j in range(2):
                    load_cols(P_GS + j, J_GS + j + 2 * r, w_in, 0, r * 256 + (COL_GS + 128 * j))
            with sp.Fori(0, 4) as r:
                for j in range(2):
                    for kp in range(2):
                        n = 2 * j + kp
                        load_cols(P_SBR + n, U_SBR + n + 4 * r, w_ssm, 8 * kp, r * 256 + 128 * j)
            with sp.Fori(0, 4) as r:
                for j in range(2):
                    load_cols(P_OUT + j, U_OUT + j + 2 * r, w_out, 0, r * 256 + 128 * j)
            with sp.Fori(0, 16) as r:
                for j in range(2):
                    load_cols(P_UP + j, U_UP + j + 2 * r, w_up, 0, r * 256 + 128 * j)
            with sp.Fori(0, 4) as r:
                for j in range(2):
                    for kp in range(4):
                        n = 4 * j + kp
                        load_cols(P_DOWN + n, U_DOWN + n + 8 * r, w_down, 8 * kp, r * 256 + 128 * j)

            sp.wait_ge(s_psfree, J_Y + 2)
            sp.dma_start(conv_prompt[0, 0], tailrow[0:3, :]).then_inc(s_out, 16)
            sp.dma_start(conv_sample[0, :, 2, :], tailrow[3:3 + NDEC, :]).then_inc(s_out, 16)
            sp.dma_start(conv_sample[0, :, 0:2, :], ins["state_conv"][0, :, 1:3, :]).then_inc(s_out, 16)
            with sp.Fori(0, NCHUNK // 2) as r:
                for j in range(2):
                    sp.wait_ge(s_psfree, J_Y + j + 3 + 2 * r)
                    sp.dma_start(y_prompt[0, ds(r * 256 + 128 * j, 128), :], ytok[:, j, :]).then_inc(s_yout[j], 16)
            sp.wait_ge(s_psfree, J_END + 2)
            sp.dma_start(y_sample.rearrange("b o d -> (b o) d"), ytok[0:NDEC, 0, :]).then_inc(s_yo, 16)
            sp.wait_ge(s_yout[0], 80)
            sp.wait_ge(s_yout[1], 80)
            sp.wait_ge(s_yo, 16)
            sp.wait_ge(s_out, 48)
            sp.wait_ge(s_kvo, 64)
            sp.wait_ge(s_ho, 80)
            sp.wait_ge(s_dso[0], 144)
            sp.wait_ge(s_dso[1], 144)

        @block.tensor
        def _(pe):
            def product(j, joff, unit, p, off, kpieces, x, m=128, wa=False):
                pe.wait_ge(s_psfree, j + 1 + joff)
                for kp in range(kpieces):
                    slot = (p + kp) % 2
                    if wa:
                        pe.wait_ge(s_wa[slot], 64 * ((p + kp - P_ABR) // 2 + 1) + 32 * off)
                    else:
                        pe.wait_ge(s_w[slot], 32 * ((p + kp) // 2 + 1) + 16 * off)
                    for n in range(3):
                        for k in range(8):
                            mm = nc.tensor.matmul(PS[0:m, 3 * (j % 2) + n, 0:TN], wbuf[:, slot, k, 0:m],
                                                  x[:, 8 * kp + k, n * TN:(n + 1) * TN],
                                                  start=(kp == 0 and k == 0), stop=(kp == kpieces - 1 and k == 7))
                    mm.then_inc(s_unit, 1)

            def turn(bank, col, src, part=128):
                n = src.shape[1]
                return nc.tensor.transpose(PS[0:n, bank, col:col + part], src, ident[0:part, 0:part])

            pe.wait_ge(s_const, 5)
            with pe.Fori(0, NCHUNK // 2) as r:
                for j in range(2):
                    pe.wait_ge(s_xin[j], 16 * r + 16)
                    pe.wait_ge(s_psfree, J_X + j + 1 + 2 * r)
                    for f in range(KT):
                        mm = turn(3 * ((J_X + j) % 2) + f // 4, 128 * (f % 4), xbuf[:, j, 128 * f:128 * f + 128])
                    mm.then_inc(s_unit, 1)
            pe.wait_ge(s_small, 16 * 14)
            pe.wait_ge(s_psfree, J_PAR)
            for f in range(KT):
                mm = turn(3 * ((J_X + 8) % 2), NDEC * f, xsam[0:NDEC, 128 * f:128 * f + 128], NDEC)
            mm.then_inc(s_unit, 1)
            pe.wait_ge(s_par, 16 * 8)
            pe.wait_ge(s_psfree, J_PAR + 1)
            for t in range(CT):
                mm = turn(3 * (J_PAR % 2) + t // 12, NPAR * (t % 12), prow[0:NPAR, 128 * t:128 * t + 128], NPAR)
            mm.then_inc(s_unit, 1)
            pe.wait_ge(s_psfree, J_PAR + 2)
            for f in range(KT):
                mm = turn(3 * ((J_PAR + 1) % 2), 6 * f, vrow[0:6, 128 * f:128 * f + 128], 6)
            mm.then_inc(s_unit, 1)

            pe.wait_ge(s_psfree, J_PAR + 2)
            with pe.Fori(0, 6) as r:
                for j in range(2):
                    product(J_QKV + j, 2 * r, J_QKV + j, P_QKV + j, 2 * r, 1, res)

            with pe.Fori(0, NCHUNK // 2) as r:
                for j in range(2):
                    pe.wait_ge(s_kst, j + 1 + 2 * r)
                    pe.wait_ge(s_psfree, J_KVT + j + 1 + 2 * r)
                    for f in range(4):
                        mm = turn(3 * ((J_KVT + j) % 2), 128 * f, kvst[:, j, f, :])
                    mm.then_inc(s_unit, 1)
            pe.wait_ge(s_kst, 9)
            pe.wait_ge(s_psfree, J_GA)
            for f in range(4):
                mm = turn(3 * ((J_KVT + 8) % 2), 128 * f, kvst[:, 0, f, 0:NDEC])
            mm.then_inc(s_unit, 1)

            pe.wait_ge(s_psfree, J_GA + 2)
            with pe.Fori(0, 2) as c:
                with pe.Fori(0, 4) as i:
                    pair = c * 4 + i
                    pe.wait_ge(s_qk, pair * 3 + 3)
                    for m in range(18):
                        if m < 16:
                            k, qb = m // 8, m % 8
                            pe.wait_ge(s_ab, pair * 16 + (m + 1))
                            for s0 in range(0, 128 * (qb + 1), 512):
                                w = min(512, 128 * (qb + 1) - s0)
                                mm = nc.tensor.matmul(PS[:, 2 * (m % 2) + s0 // 512, 0:w],
                                                      qst[64 * k:64 * k + 64, 128 * qb:128 * qb + 128],
                                                      kst[64 * k:64 * k + 64, s0:s0 + w], start=True, stop=True)
                            mm.then_inc(s_z, 1)
                        if m >= 2:
                            k, qb = (m - 2) // 8, (m - 2) % 8
                            pe.wait_ge(s_cp, pair * 16 + (m - 1))
                            if qb >= 4:
                                pe.wait_ge(s_cp1, pair * 8 + (4 * k + qb - 3))
                            pe.wait_ge(s_oc, pair * 16 + (m - 1))
                            for kb in range(qb + 1):
                                mm = nc.tensor.matmul(PS[64 * k:64 * k + 64, 6 + m % 2, 0:128],
                                                      vst[:, kb, 64 * k:64 * k + 64], wTb[:, m % 2, kb, :],
                                                      start=(kb == 0), stop=(kb == qb))
                            mm.then_inc(s_o, 1)
                        if 1 <= m < 17:
                            k, qb = (m - 1) // 8, (m - 1) % 8
                            pe.wait_ge(s_wt, pair * 16 + m)
                            if m > 1:
                                pe.wait_ge(s_cp, pair * 16 + (m - 1))
                            for kb in range(qb + 1):
                                if kb == 4:
                                    mm.then_inc(s_tr, 1)
                                    if 4 * k + qb > 4:
                                        pe.wait_ge(s_cp1, pair * 8 + (4 * k + qb - 4))
                                mm = turn(4 + kb // 4, 128 * (kb % 4), zb[:, (m - 1) % 2, 128 * kb:128 * kb + 128])
                            mm.then_inc(s_tr if qb < 4 else s_tr1, 1)

            def decode_keys(b, j, first, last):
                pe.wait_ge(s_kp[j], 16 * PAGES + 8 * PAGES * (b - j))
                pe.wait_ge(s_qs, b + 1)
                for q in range(9):
                    if q < 8:
                        c, jb = q // 4, q % 4
                        pe.wait_ge(s_dcp, b * 8 + (q + 1))
                        for n in range(4):
                            mm = turn(4 + q % 2, 128 * n, pbuf[:, j, 4 * jb + n, 128 * c:128 * c + 128])
                        mm.then_inc(s_dtr, 1)
                    if q >= 1:
                        c, jb = (q - 1) // 4, (q - 1) % 4
                        pe.wait_ge(s_dcp, b * 8 + (q + 2))
                        nc.tensor.matmul(PS[:, jb, :], qstd[:, j, c, :], kTst[:, (q - 1) % 2, :],
                                         start=(first and c == 0), stop=(last and c == 1)).then_inc(s_dz, 1)

            pe.wait_ge(s_oc, 130)
            decode_keys(0, 0, True, False)
            decode_keys(1, 1, False, False)
            with pe.Fori(1, 3) as r:
                for j in range(2):
                    decode_keys(r * 2 + j, j, False, False)
            decode_keys(6, 0, False, False)
            decode_keys(7, 1, False, True)
            pe.wait_ge(s_dexp, 1)
            for n in range(PAGES):
                mm = turn(n // 4, 128 * (n % 4), zd[:, 128 * n:128 * n + 128])
            mm.then_inc(s_dtw, 1)
            pe.wait_ge(s_dcw, 1)
            with pe.Fori(0, NDEC // 2) as r:
                for j in range(2):
                    pe.wait_ge(s_kp[j], 16 * PAGES * 5 + 16 * PAGES * r)
                    pe.wait_ge(s_doc, j + 1 + 2 * r)
                    for c in range(2):
                        for n in range(PAGES):
                            mm = nc.tensor.matmul(PS[:, 4 + j, 8 * c:8 * c + 8], pbuf[:, j, n, 128 * c:128 * c + 128],
                                                  wTd[:, n, ds(r * 32 + (16 * j + 8 * c), 8)],
                                                  start=(n == 0), stop=(n == PAGES - 1))
                    mm.then_inc(s_do, 1)

            pe.wait_ge(s_doc, NDEC + 2)
            with pe.Fori(0, 4) as r:
                for j in range(2):
                    product(J_GA + j, 2 * r, J_GA + j, P_GA + j, 2 * r, 1, res)
            with pe.Fori(0, 4) as r:
                for j in range(2):
                    product(J_ABR + j, 2 * r, J_ABR + j, P_ABR + j, 2 * r, 1, qT, wa=True)

            product(J_DT, 0, J_DT, P_DT, 0, 1, res, m=HEADS)
            pe.wait_ge(s_dt, DT_CUM)
            pe.wait_ge(s_psfree, J_DT + 2)
            for n in range(NCHUNK):
                turn(3 * ((J_DT + 1) % 2), 32 * n, dtv[:, 128 * n:128 * n + 128], HEADS)
                mm = turn(3 * ((J_DT + 1) % 2), 256 + 32 * n, dtr[:, 128 * n:128 * n + 128], HEADS)
            mm.then_inc(s_unit, 1)

            with pe.Fori(0, GROUPS) as g:
                pe.wait_ge(s_hupd, g * 8 + 2)
                pe.wait_ge(s_hc, g + 2)
                for n in range(10):
                    product(J_SSD + n, 10 * g, J_SSD + n, P_SSD + n, 10 * g, 1, res)
                pe.wait_ge(s_psfree, g * 10 + (J_SSD + 12))
                pe.sem_inc(s_pass, 1)
                with pe.Fori(0, NCHUNK // 2) as r:
                    for j in range(2):
                        n = g * 8 + 2 * r + j
                        pe.wait_ge(s_stg, 2 * n + 2)
                        pe.wait_ge(s_hupd, n + 1)
                        for f in range(4):
                            turn(3 * j, 128 * f, xst[:, j, f, :])
                        turn(3 * j + 1, 0, bst[:, j, :])
                        nc.tensor.matmul(PS[:, 3 * j + 1, 128:256], bst[:, j, :], cT[:, ds(r * 256 + 128 * j, 128)],
                                         start=True, stop=True).then_inc(s_tp, 1)
                        pe.wait_ge(s_bc, 2 * n + 2)
                        pe.wait_ge(s_xdt, 2 * n + 2)
                        nc.tensor.matmul(PS[:, 6 + j, :], btok, xdte.rearrange("p h d -> p (h d)"),
                                         start=True, stop=True).then_inc(s_st, 1)
                        pe.wait_ge(s_Mm, n + 1)
                        pe.wait_ge(s_CE, n + 1)
                        pe.wait_ge(s_hupd, n + 2)
                        pe.wait_ge(s_h0, g + 1)
                        for h in range(8):
                            y = PS[64 * (h % 2):64 * (h % 2) + 64, 3 * j + 2, 128 * (h // 2):128 * (h // 2) + 128]
                            nc.tensor.matmul(y, xdt[:, h, :], seg[:, h, :], start=True, stop=False)
                            mm = nc.tensor.matmul(y, hst[:, h, :], ecm[:, h, :], start=False, stop=True)
                        mm.then_inc(s_y, 1)
                pe.wait_ge(s_hupd, g * 8 + 10)
                for f in range(4):
                    mm = turn(0, 128 * f, hst[:, 2 * f:2 * f + 2, :].rearrange("p h d -> p (h d)"))
                mm.then_inc(s_ht, 1)

            pe.wait_ge(s_hc, GROUPS + 2)
            pe.wait_ge(s_d8, 18)
            with pe.Fori(0, 4) as r:
                for j in range(2):
                    product(J_GS + j, 2 * r, J_GS + j, P_GS + j, 2 * r, 1, res)

            def column_sums(j, ready, value):
                pe.wait_ge(ready, value)
                pe.wait_ge(s_psfree, j + 1)
                for n in range(3):
                    mm = nc.tensor.matmul(PS[:, 3 * (j % 2) + n, 0:TN], ones[:], nacc[:, n * TN:(n + 1) * TN],
                                          start=True, stop=True)
                mm.then_inc(s_unit, 1)

            column_sums(J_RMS, s_nac, 18)
            pe.wait_ge(s_hn, 16)
            with pe.Fori(0, 4) as r:
                for j in range(2):
                    product(J_SBR + j, 2 * r, U_SBR + 2 * j, P_SBR + 2 * j, 4 * r, 2, hT)
            pe.wait_ge(s_mix, 8)
            with pe.Fori(0, 4) as r:
                for j in range(2):
                    product(J_OUT + j, 2 * r, U_OUT + j, P_OUT + j, 2 * r, 1, mixT)
            column_sums(J_LN1, s_nsum, 10)
            column_sums(J_LN1 + 1, s_nac, 26)
            pe.wait_ge(s_yn, 8)
            with pe.Fori(0, 16) as r:
                for j in range(2):
                    product(J_UP + j, 2 * r, U_UP + j, P_UP + j, 2 * r, 1, res)
            pe.wait_ge(s_hid, 32)
            with pe.Fori(0, 4) as r:
                for j in range(2):
                    product(J_DOWN + j, 2 * r, U_DOWN + 4 * j, P_DOWN + 4 * j, 8 * r, 4, hidT)
            column_sums(J_LN2, s_nsum, 18)
            column_sums(J_LN2 + 1, s_nac, 34)
            for n in range(2):
                pe.wait_ge(s_psfree, J_TAIL + n + 1)
                for t in range(12):
                    mm = turn(3 * ((J_TAIL + n) % 2) + t // 4, 128 * (t % 4), tail[:, 12 * n + t, :])
                mm.then_inc(s_unit, 1)
            with pe.Fori(0, NCHUNK // 2) as r:
                for j in range(2):
                    pe.wait_ge(s_ys, j + 1 + 2 * r)
                    pe.wait_ge(s_psfree, J_Y + j + 1 + 2 * r)
                    for f in range(KT):
                        mm = turn(3 * ((J_Y + j) % 2) + f // 4, 128 * (f % 4), yst[:, j, f, :])
                    mm.then_inc(s_unit, 1)
            pe.wait_ge(s_ys, 9)
            pe.wait_ge(s_psfree, J_Y + 9)
            for f in range(KT):
                mm = turn(3 * ((J_Y + 8) % 2) + f // 4, 128 * (f % 4), yst[:, 0, f, 0:NDEC])
            mm.then_inc(s_unit, 1)

        @block.scalar
        def _(act):
            def fn(out, in_, f, **kw):
                return nc.scalar.activation(out, in_, f, **kw)

            with act.Fori(0, NCHUNK // 2) as r:
                for j in range(2):
                    act.wait_ge(s_unit, J_X + j + 1 + 2 * r)
                    act.sem_inc(s_pass, 1)
                    nc.scalar.copy(res[:, :, ds(r * 256 + 128 * j, 128)].rearrange("p (a f) b -> p a f b", a=2),
                                   banks(J_X + j, 2, 512).rearrange("p a (f b) -> p a f b", b=128)).then_inc(s_psfree, 1)
            act.wait_ge(s_unit, J_PAR)
            nc.scalar.copy(res[:, :, SEQ:T], PS[:, 3 * ((J_X + 8) % 2), 0:KT * NDEC].rearrange("p (f b) -> p f b", b=NDEC)).then_inc(s_psfree, 1)
            act.wait_ge(s_unit, J_PAR + 1)
            nc.scalar.copy(par[:, :, :].rearrange("p (a t) n -> p a (t n)", a=2), banks(J_PAR, 2, 12 * NPAR)).then_inc(s_psfree, 1)
            act.wait_ge(s_unit, J_PAR + 2)
            nc.scalar.copy(vec[:, :, :], PS[:, 3 * ((J_PAR + 1) % 2), 0:6 * KT].rearrange("p (f n) -> p f n", n=6)).then_inc(s_psfree, 1)
            for c0, n, t in ((0, 4, qT), (8, 2, kvT)):
                with act.Fori(0, n) as r:
                    for j in range(2):
                        act.wait_ge(s_unit, J_QKV + c0 + j + 1 + 2 * r)
                        act.sem_inc(s_pass, 1)
                        nc.scalar.copy(tile(t, r * 2 + j), banks(J_QKV + c0 + j)).then_inc(s_psfree, 1)
            with act.Fori(0, NCHUNK // 2) as r:
                for j in range(2):
                    act.wait_ge(s_unit, J_KVT + j + 1 + 2 * r)
                    act.sem_inc(s_pass, 1)
                    nc.scalar.copy(kvtok[:, ds(r * 2 + j, 1), :], banks(J_KVT + j, 1, 512)).then_inc(s_psfree, 1)
            act.wait_ge(s_unit, J_GA)
            nc.scalar.copy(kvtok[0:NDEC, 8:9, :], PS[0:NDEC, 3 * ((J_KVT + 8) % 2):3 * ((J_KVT + 8) % 2) + 1, :]).then_inc(s_psfree, 1)

            act.wait_ge(s_small, 16 * 14)
            act.preload_act_table_set("natural_log_exp_and_others")
            with act.Fori(0, 2) as c:
                with act.Fori(0, 4) as i:
                    pair = c * 4 + i
                    for m in range(18):
                        if m < 16:
                            k, qb = m // 8, m % 8
                            S = 128 * (qb + 1)
                            N = pair * 16 + m
                            bias = sbb[:, ds(c * 8 + i + 4 * k, 1)]
                            z = PS[:, 2 * (m % 2):2 * (m % 2) + 2, :].rearrange("p a b -> p (a b)")[:, 0:S]
                            l = lb[:, m % 2, 0:S]
                            act.wait_ge(s_z, N + 1)
                            act.sem_inc(s_pass, 1)
                            fn(zb[:, m % 2, 0:S], z, ACT.Identity, bias=bias, scale=SCALE).then_inc(s_zs, 1)
                            act.wait_ge(s_scan, N + 1)
                            act.sem_inc(s_pass, 1)
                            fn(l, z, ACT.Abs, bias=bias, scale=SCALE).then_inc(s_ab, 1)
                            act.wait_ge(s_ab, N + 3)
                            fn(l, l, ACT.Exp, scale=-1.0).then_inc(s_ex, 1)
                            act.wait_ge(s_ex, N + 1)
                            fn(l, l, ACT.Ln, bias=1.0).then_inc(s_ln, 1)
                        if 1 <= m < 17:
                            S = 128 * ((m - 1) % 8 + 1)
                            act.wait_ge(s_d, pair * 16 + (m + 2))
                            fn(zb[:, (m - 1) % 2, 0:S], zb[:, (m - 1) % 2, 0:S], ACT.Exp).then_inc(s_wt, 1)
                        if m >= 2:
                            k, qb = (m - 2) // 8, (m - 2) % 8
                            act.wait_ge(s_o, pair * 16 + (m + 1))
                            act.sem_inc(s_pass, 1)
                            nc.scalar.copy(big[64 * k:64 * k + 64, ds(pair, 1), 128 * qb:128 * qb + 128],
                                           PS[64 * k:64 * k + 64, 6 + m % 2:7 + m % 2, 0:128]).then_inc(s_oc, 1)

            with act.Fori(0, NDEC) as b:
                for q in range(8):
                    act.wait_ge(s_dtr, b * 8 + (q + 1))
                    act.wait_ge(s_dz, b * 8 + (q + 1))
                    nc.scalar.copy(kTst[:, q % 2, :], PS[:, 4 + q % 2, :]).then_inc(s_dcp, 1)
            zall = PS[:, 0:4, :].rearrange("p a b -> p (a b)")
            act.wait_ge(s_dz, 66)
            fn(zd, zall, ACT.Identity, bias=sbd[:], scale=SCALE).then_inc(s_dact, 1)
            fn(ld, zall, ACT.Abs, bias=sbd[:], scale=SCALE).then_inc(s_dact, 1)
            act.wait_ge(s_dact, 2)
            fn(ld, ld, ACT.Exp, scale=-1.0).then_inc(s_dact, 1)
            act.wait_ge(s_dact, 3)
            fn(ld, ld, ACT.Ln, bias=1.0).then_inc(s_dact, 1)
            act.wait_ge(s_dd, 3)
            fn(zd, zd, ACT.Exp).then_inc(s_dexp, 1)

            with act.Fori(0, 4) as r:
                for j in range(2):
                    act.wait_ge(s_unit, J_GA + j + 1 + 2 * r)
                    act.sem_inc(s_pass, 1)
                    fn(tile(mixT, r * 2 + j), banks(J_GA + j), ACT.Sigmoid).then_inc(s_psfree, 1)

            act.wait_ge(s_small, 16 * 14)
            fn(alog[:], alog[:], ACT.Exp).then_inc(s_dta, 1)
            act.wait_ge(s_dt, 2)
            fn(dte1, dtr, ACT.Abs).then_inc(s_dta, 1)
            act.wait_ge(s_dta, 2)
            fn(dte1, dte1, ACT.Exp, scale=-1.0).then_inc(s_dta, 1)
            act.wait_ge(s_dt, 3)
            fn(dtl, dtu, ACT.Ln).then_inc(s_dta, 1)
            act.wait_ge(s_dtx, 64)
            fn(dtx[:, 0], dtx[:, 0], ACT.Exp).then_inc(s_dtxe, 1)

            with act.Fori(0, GROUPS) as g:
                for n in range(4):
                    act.wait_ge(s_unit, g * 10 + (J_SSD + n + 1))
                    act.wait_ge(s_psfree, g * 10 + (J_SSD + n + 2))
                    if n == 0:
                        act.wait_ge(s_rz, g + 1)
                    fn(wk(3176, 3, TN), banks(J_SSD + n), ACT.Sigmoid).then_inc(s_zsg, 1)
                for n in range(6):
                    ct = g * 4 + n if n < 4 else g + (16 + 4 * (n - 4))
                    J = J_SSD + 4 + n
                    act.wait_ge(s_unit, g * 10 + (J + 1))
                    if n == 0:
                        act.wait_ge(s_psfree, g * 10 + (J + 2))
                    act.wait_ge(s_cv, g * 24 + (4 * n + 2))
                    b0 = 3 * (J % 2)
                    nc.scalar.copy(raw[:, 3:3 + 2 * TN].rearrange("p (a b) -> p a b", a=2), PS[:, b0:b0 + 2, 0:TN])
                    nc.scalar.copy(raw[:, 3 + 2 * TN:3 + SEQ], PS[:, b0 + 2, 0:TN - NDEC])
                    nc.scalar.copy(raw[:, 3 + SEQ:RAWLEN].rearrange("p (b k) -> p b k", k=4)[:, :, 0:3],
                                   par[:, ds(ct, 1), 5:NPAR].rearrange("p o (b k) -> p (o b) k", k=3))
                    nc.scalar.copy(raw[:, 3 + SEQ:RAWLEN].rearrange("p (b k) -> p b k", k=4)[:, :, 3:4],
                                   PS[:, b0 + 2, TN - NDEC:TN].rearrange("p (b o) -> p b o", o=1)).then_inc(s_raw, 1)
                    nc.scalar.copy(tail[:, ds(ct, 1), :], PS[:, b0 + 2:b0 + 3, TN - NDEC - 3:TN]).then_inc(s_psfree, 1)
                    act.wait_ge(s_cv, g * 24 + (4 * n + 6))
                    act.wait_ge(s_cout, g * 6 + (n + 2))
                    fn(sig, acc, ACT.Sigmoid).then_inc(s_csg, 1)
                with act.Fori(0, NCHUNK // 2) as r:
                    for j in range(2):
                        n = g * 8 + 2 * r + j
                        act.wait_ge(s_cb[j], g * 64 + 16 * r + 16)
                        act.wait_ge(s_y, n + 2)
                        fn(ecm, cumb[:, j], ACT.Exp).then_inc(s_ec, 1)
                        act.wait_ge(s_hupd, n + 2)
                        fn(cd, cumb[:, j, :, 127], ACT.Exp).then_inc(s_cd, 1)
                        act.wait_ge(s_t8, n + 1)
                        fn(t8, t8, ACT.Exp).then_inc(s_t8e, 1)
                        act.wait_ge(s_sg2, n + 1)
                        fn(seg, seg, ACT.Exp).then_inc(s_M, 1)
                act.wait_ge(s_ht, g + 1)
                act.wait_ge(s_ho, g * 16 + 16)
                nc.scalar.copy(hout.rearrange("p j n -> p (j n)"), PS[:, 0, :]).then_inc(s_hc, 1)
                with act.Fori(0, 2) as r:
                    for j in range(2):
                        act.wait_ge(s_d4, g * 4 + 2 * r + (j + 1))
                        dst = ssm_sample[0].rearrange("b h p n -> (h p) b n")[ds(g * 512 + r * 256 + j * 128, 128)]
                        act.dma_start(dst, h0b[:, j]).then_inc(s_dso[j], 16)

            with act.Fori(0, 4) as r:
                for j in range(2):
                    act.wait_ge(s_unit, J_GS + j + 1 + 2 * r)
                    act.sem_inc(s_pass, 1)
                    fn(tile(gsT, r * 2 + j), banks(J_GS + j), ACT.Sigmoid).then_inc(s_psfree, 1)

            def squares(t, n, base, nbase):
                with act.Fori(0, n // 2) as r:
                    for j in range(2):
                        if t is res:
                            act.wait_ge(s_dm, nbase + j + 1 + 2 * r)
                        act.wait_ge(s_nac, base + j + 1 + 2 * r)
                        act.sem_inc(s_pass, 1)
                        fn(nsq[:, j], t[:, ds(r * 2 + j, 1), :].rearrange("p o t -> p (o t)"), ACT.Square).then_inc(s_sq, 1)

            for j in range(2):
                act.wait_ge(s_dso[j], 144)
            act.wait_ge(s_d8, 18)
            squares(hT, 16, 0, 0)
            act.wait_ge(s_unit, J_RMS + 1)
            fn(nbc.rearrange("p (a b) -> p a b", a=3), banks(J_RMS), ACT.Sqrt, bias=eps[:], scale=1.0 / D_INNER).then_inc(s_psfree, 1)

            def norm(n, unit, j):
                squares(res, 8, 16 + 8 * n, 8 * n)
                act.wait_ge(s_unit, unit + 2)
                fn(nbc2.rearrange("p (a b) -> p a b", a=3), banks(j + 1), ACT.Sqrt, bias=eps[:], scale=1.0 / D).then_inc(s_psfree, 1)
                with act.Fori(0, KT) as m:
                    act.wait_ge(s_yn0, m + (8 * n + 1))
                    act.sem_inc(s_pass, 1)
                    fn(res[:, ds(m, 1), :], res[:, ds(m, 1), :], ACT.Identity, bias=vec[:, ds(m, 1), 2 * n + 1],
                       scale=vec[:, ds(m, 1), 2 * n]).then_inc(s_yn, 1)

            norm(0, U_LN1, J_LN1)
            with act.Fori(0, 16) as r:
                for j in range(2):
                    act.wait_ge(s_unit, U_UP + j + 1 + 2 * r)
                    act.sem_inc(s_pass, 1)
                    fn(tile(hidT, r * 2 + j), banks(J_UP + j), ACT.Relu).then_inc(s_psfree, 1)
            norm(1, U_LN2, J_LN2)
            for n in range(2):
                act.wait_ge(s_unit, U_TAIL + n + 1)
                b0 = 3 * ((J_TAIL + n) % 2)
                nc.scalar.copy(tailrow[0:3 + NDEC, 1536 * n:1536 * n + 1536].rearrange("p (a b) -> p a b", a=3),
                               PS[0:3 + NDEC, b0:b0 + 3, :]).then_inc(s_psfree, 1)
            with act.Fori(0, NCHUNK // 2) as r:
                for j in range(2):
                    act.wait_ge(s_unit, U_Y + j + 1 + 2 * r)
                    act.wait_ge(s_yout[j], 16 * r + 16)
                    nc.scalar.copy(ytok[:, j, :].rearrange("p (a b) -> p a b", a=2), banks(J_Y + j, 2, 512)).then_inc(s_psfree, 1)
            act.wait_ge(s_unit, U_Y + 9)
            act.wait_ge(s_yout[0], 80)
            b0 = 3 * ((J_Y + 8) % 2)
            nc.scalar.copy(ytok[0:NDEC, 0, :].rearrange("p (a b) -> p a b", a=2), PS[0:NDEC, b0:b0 + 2, :]).then_inc(s_psfree, 1)

        @block.vector
        def _(dve):
            tt, ts, stt, copy = nc.vector.tensor_tensor, nc.vector.tensor_scalar, nc.vector.scalar_tensor_tensor, nc.vector.tensor_copy
            for s in (s_psfree, s_ab, s_scan, s_d, s_o, s_oc, s_dcp, s_dz, s_doc, s_hupd, s_nac, s_hc, s_y, s_cv, s_cout, s_nsum, s_d8):
                dve.sem_inc(s, 2)
            for s in (*s_dso, *s_yout, s_ho):
                dve.sem_inc(s, 16)
            nc.vector.memset(eps[:], EPS)
            nc.vector.memset(ones[:], 1.0).then_inc(s_const, 1)

            dve.wait_ge(s_qz, 1)
            dve.wait_ge(s_psfree, J_KVT + 2)
            for b in range(NDEC):
                for c in range(2):
                    for k in range(2):
                        dst = qbd[64 * k:64 * k + 64, b, c, 16 * b + 8 * c + 4 * k:16 * b + 8 * c + 4 * k + 4]
                        copy(dst, big[64 * k:64 * k + 64, 4 * c:4 * c + 4, SEQ + b]).then_inc(s_qb, 1)
            dve.wait_ge(s_const, 5)
            with dve.Fori(0, 8) as pair:
                for m in range(17):
                    if m < 16:
                        qb = m % 8
                        S = 128 * (qb + 1)
                        N = pair * 16 + m
                        l, sm = lb[:, m % 2, :], sbuf_s[:, m % 2, :]
                        dve.wait_ge(s_ln, N + 1)
                        stt(l[:, 0:S], zb[:, m % 2, 0:S], 0.0, l[:, 0:S], ALU.max, ALU.add).then_inc(s_sp, 1)
                        dve.wait_ge(s_sp, N + 1)
                        tt(l[:, S - 128:S], l[:, S - 128:S], keep[:], ALU.mult).then_inc(s_spm, 1)
                        dve.wait_ge(s_spm, N + 1)
                        dve.wait_ge(s_d, N + 1)
                        back = slice(S - 1, None, -1)
                        nc.vector.tensor_tensor_scan(sm[:, back], ones[:, 0:1].to_broadcast([128, S]), l[:, back], 0.0,
                                                     ALU.mult, ALU.add).then_inc(s_scan, 1)
                        dve.wait_ge(s_scan, N + 3)
                        tt(sm[:, S - 128:S], sm[:, S - 128:S], far[:], ALU.add).then_inc(s_far, 1)
                    if m >= 1:
                        k, qb = (m - 1) // 8, (m - 1) % 8
                        nb = min(4, qb + 1)
                        dve.wait_ge(s_tr, pair * 16 + m)
                        dve.wait_ge(s_o, pair * 16 + m)
                        copy(wTb[:, (m - 1) % 2, 0:nb, :].rearrange("p a b -> p (a b)"), PS[:, 4, 0:128 * nb]).then_inc(s_cp, 1)
                        if qb >= 4:
                            nb = qb - 3
                            dve.wait_ge(s_tr1, pair * 8 + (4 * k + qb - 3))
                            copy(wTb[:, (m - 1) % 2, 4:4 + nb, :].rearrange("p a b -> p (a b)"), PS[:, 5, 0:128 * nb]).then_inc(s_cp1, 1)

            dve.wait_ge(s_dact, 4)
            stt(ld, zd, 0.0, ld, ALU.max, ALU.add).then_inc(s_dd, 1)
            dve.wait_ge(s_dd, 1)
            nc.vector.tensor_tensor_scan(sd[:, ::-1], ones[:, 0:1].to_broadcast([128, PAST]), ld[:, ::-1], 0.0, ALU.mult, ALU.add).then_inc(s_dd, 1)
            dve.wait_ge(s_dd, 2)
            tt(zd, zd, sd, ALU.subtract).then_inc(s_dd, 1)
            dve.wait_ge(s_dtw, 1)
            copy(wTd.rearrange("p a b -> p (a b)"), PS[:, 0:4, :].rearrange("p a b -> p (a b)")).then_inc(s_dcw, 1)
            with dve.Fori(0, NDEC // 2) as r:
                for j in range(2):
                    dve.wait_ge(s_do, 2 * r + j + 1)
                    o = PS[:, 4 + j, 0:16].rearrange("p (c k i) -> p c k i", c=2, k=2)
                    for k in range(2):
                        dst = big[64 * k:64 * k + 64, 0:8, ds(r * 2 + (SEQ + j), 1)].rearrange("p (c i) o -> p c (i o)", c=2)
                        op = copy(dst, o[64 * k:64 * k + 64, :, k, :])
                    op.then_inc(s_doc, 1)

            dve.wait_ge(s_psfree, J_ABR + 2)
            with dve.Fori(0, 4) as r:
                for j in range(2):
                    dve.wait_ge(s_unit, J_ABR + j + 1 + 2 * r)
                    t = tile(mixT, r * 2 + j)
                    tt(t, banks(J_ABR + j), t, ALU.mult).then_inc(s_psfree, 1)

            dve.wait_ge(s_dta, 1)
            ts(alog[:], alog[:], -1.0, None, ALU.mult).then_inc(s_dt, 1)
            dve.wait_ge(s_unit, J_DT + 1)
            dve.wait_ge(s_psfree, J_DT + 2)
            ts(dtr.rearrange("p (a b) -> p a b", a=3), PS[0:HEADS, 3 * (J_DT % 2):3 * (J_DT % 2) + 3, 0:TN], dtb[:], None,
               ALU.add).then_inc(s_dt, 1)
            dve.wait_ge(s_dta, 3)
            ts(dtu, dte1, 1.0, None, ALU.add).then_inc(s_dt, 1)
            dve.wait_ge(s_dt, 3)
            ts(dtv, dtu, 1.0, None, ALU.subtract).then_inc(s_dt, 1)
            dve.wait_ge(s_dt, 4)
            tt(dtv, dte1, dtv, ALU.subtract).then_inc(s_dt, 1)
            dve.wait_ge(s_dta, 4)
            nc.vector.reciprocal(dtu, dtu).then_inc(s_dt, 1)
            dve.wait_ge(s_dt, 6)
            tt(dtv, dtv, dtu, ALU.mult).then_inc(s_dt, 1)
            dve.wait_ge(s_dt, 7)
            tt(dtl, dtl, dtv, ALU.add).then_inc(s_dt, 1)
            dve.wait_ge(s_dt, 8)
            stt(dtr, dtr, 0.0, dtl, ALU.max, ALU.add).then_inc(s_dt, 1)
            nc.vector.memset(chm, 1.0).then_inc(s_dt, 1)
            dve.wait_ge(s_dt, 10)
            nc.vector.memset(chm.rearrange("p (c l) -> p c l", l=CHUNK)[:, :, 0:1], 0.0).then_inc(s_dt, 1)
            ts(dtl, dtr, alog[:], None, ALU.mult).then_inc(s_dt, 1)
            dve.wait_ge(s_dt, 12)
            nc.vector.tensor_tensor_scan(dtv[:, 0:SEQ], chm, dtl[:, 0:SEQ], 0.0, ALU.mult, ALU.add).then_inc(s_dt, 1)
            dve.wait_ge(s_dt, DT_CUM)
            dve.sem_inc(s_psfree, 1)
            dve.wait_ge(s_unit, J_DT + 2)
            b0 = 3 * ((J_DT + 1) % 2)
            copy(cumtok[:, :, :].rearrange("p c h -> p (c h)"), PS[:, b0, 0:256]).then_inc(s_tok, 1)
            copy(dttok[:, :, :].rearrange("p c h -> p (c h)"), PS[:, b0, 256:512]).then_inc(s_psfree, 1)
            dve.wait_ge(s_tok, 1)
            dve.wait_ge(s_psfree, J_SSD + 2)

            with dve.Fori(0, GROUPS) as g:
                dve.wait_ge(s_dso[0], g * 32 + 16)
                dve.wait_ge(s_dso[1], g * 32 + 16)
                dve.wait_ge(s_hc, g + 2)
                dve.wait_ge(s_scr, 48)
                nc.vector.memset(hst, 0.0).then_inc(s_h0, 1)
                nc.vector.memset(raw[:, 0:3], 0.0).then_inc(s_rz, 1)
                dve.wait_ge(s_psfree, g * 10 + (J_SSD + 2))
                for n in range(4):
                    dve.wait_ge(s_zsg, g * 4 + (n + 1))
                    tt(tile(hT, g * 4 + n), banks(J_SSD + n), wk(3176, 3, TN), ALU.mult).then_inc(s_psfree, 1)
                for n in range(6):
                    ct = g * 4 + n if n < 4 else g + (16 + 4 * (n - 4))
                    w = [par[:, ds(ct, 1), k] for k in range(5)]
                    dve.wait_ge(s_raw, g * 6 + (n + 1))
                    dve.wait_ge(s_cout, g * 6 + (n + 2))
                    ts(acc, raw[:, 0:ACCLEN], w[0], w[4], ALU.mult, ALU.add).then_inc(s_cv, 1)
                    for k in range(1, 4):
                        dve.wait_ge(s_cv, g * 24 + (4 * n + k + 2))
                        stt(acc, raw[:, k:k + ACCLEN], w[k], acc, ALU.mult, ALU.add).then_inc(s_cv, 1)
                    dve.wait_ge(s_csg, g * 6 + (n + 1))
                    t = big[:, 24 + n, :]
                    tt(t[:, 0:SEQ], acc[:, 0:SEQ], sig[:, 0:SEQ], ALU.mult)
                    tt(t[:, SEQ:T], acc[:, DEC0:ACCLEN:4], sig[:, DEC0:ACCLEN:4], ALU.mult).then_inc(s_cout, 1)
                with dve.Fori(0, NCHUNK // 2) as r:
                    for j in range(2):
                        n = g * 8 + 2 * r + j
                        c = r * 2 + j
                        cum8 = cumtok[:, ds(c, 1), ds(g * 8, 8)].rearrange("p o h -> p (o h)")
                        dt8 = dttok[:, ds(c, 1), ds(g * 8, 8)].rearrange("p o h -> p (o h)")
                        wide = lambda v, w: v.rearrange("p (h o) -> p h o", o=1).to_broadcast([128, 8, w])
                        dve.wait_ge(s_cb[j], g * 64 + 16 * r + 16)
                        dve.wait_ge(s_hupd, n + 2)
                        tt(t8, cumb[:, j, :, 127], cum8, ALU.subtract).then_inc(s_t8, 1)
                        tt(seg, cumb[:, j], wide(cum8, 128), ALU.subtract).then_inc(s_sg, 1)
                        dve.wait_ge(s_sg, n + 1)
                        ts(seg, seg, 0.0, None, ALU.min).then_inc(s_sg2, 1)
                        dve.wait_ge(s_tp, n + 1)
                        copy(btok, PS[:, 3 * j + 1, 0:128]).then_inc(s_bc, 1)
                        tt(cbm, PS[:, 3 * j + 1, 128:256], tri[:], ALU.mult).then_inc(s_bc, 1)
                        dve.wait_ge(s_t8e, n + 1)
                        tt(dte, t8, dt8, ALU.mult).then_inc(s_dte, 1)
                        x = PS[:, 3 * j, :].rearrange("p (h d) -> p h d", d=64)
                        tt(xdt, x, wide(dt8, 64), ALU.mult).then_inc(s_xdt, 1)
                        dve.wait_ge(s_dte, n + 1)
                        tt(xdte, x, wide(dte, 64), ALU.mult).then_inc(s_xdt, 1)
                        dve.wait_ge(s_ec, n + 1)
                        tt(ecm, ecm, cT[:, ds(r * 256 + 128 * j, 128)].rearrange("p (o l) -> p o l", o=1).to_broadcast([128, 8, 128]),
                           ALU.mult).then_inc(s_CE, 1)
                        dve.wait_ge(s_y, n + 3)
                        for f in range(4):
                            stt(y1[:, f, :], xst[:, j, f, :], dskip[:, ds(g * 4 + f, 1)],
                                PS[:, 3 * j + 2, 128 * f:128 * f + 128], ALU.mult, ALU.add).then_inc(s_y1, 1)
                        dve.wait_ge(s_cd, n + 1)
                        tt(hst, hst, wide(cd, 64), ALU.mult).then_inc(s_hm, 1)
                        dve.wait_ge(s_y1, 4 * n + 4)
                        t = hT[:, ds(g * 4, 4), ds(r * 256 + 128 * j, 128)]
                        tt(t, t, y1, ALU.mult).then_inc(s_y2, 1)
                        dve.wait_ge(s_hm, n + 1)
                        dve.wait_ge(s_st, n + 1)
                        tt(hst, hst, PS[:, 6 + j, :].rearrange("p (h d) -> p h d", d=64), ALU.add).then_inc(s_hupd, 1)
                dve.wait_ge(s_bcr, g * 16 + 16)
                dve.sem_inc(s_pass, 1)
                dve.wait_ge(s_dtxe, 1)
                wide8 = lambda v: v.rearrange("p (b o) -> p b o", o=1).to_broadcast([128, NDEC, 128])
                with dve.Fori(0, 2) as r:
                    for j in range(2):
                        n = g * 4 + 2 * r + j
                        q = r * 2 + j
                        xcol = xsT[:, ds(q, 1), SEQ:T].rearrange("p o b -> p (o b)")
                        tt(xdd, xcol, dtx[:, 1, ds(n, 1), :].rearrange("p o b -> p (o b)"), ALU.mult).then_inc(s_d1, 1)
                        dve.wait_ge(s_dh[j], g * 32 + 16 * r + 16)
                        tt(h0b[:, j], h0b[:, j], wide8(dtx[:, 0, ds(n, 1), :].rearrange("p o b -> p (o b)")), ALU.mult).then_inc(s_d3, 1)
                        dve.wait_ge(s_d2, n + 1)
                        dve.wait_ge(s_d3, n + 1)
                        tt(h0b[:, j], h0b[:, j], t2, ALU.add).then_inc(s_d4, 1)
                        dve.wait_ge(s_d5, n + 1)
                        nc.vector.tensor_reduce(yd, t2, AX_X, ALU.add).then_inc(s_d6, 1)
                        dve.wait_ge(s_d6, n + 1)
                        stt(yd, xcol, dskip[:, ds(n, 1)], yd, ALU.mult, ALU.add).then_inc(s_d7, 1)
                        dve.wait_ge(s_d7, n + 1)
                        t = hT[:, ds(n, 1), SEQ:T].rearrange("p o b -> p (o b)")
                        tt(t, t, yd, ALU.mult).then_inc(s_d8, 1)

            def add_squares(n, k):
                with dve.Fori(0, n // 2) as r:
                    for j in range(2):
                        dve.wait_ge(s_sq, k + j + 1 + 2 * r)
                        dve.wait_ge(s_nac, k + j + 2 + 2 * r)
                        tt(nacc, nacc, nsq[:, j], ALU.add).then_inc(s_nac, 1)

            for j in range(2):
                dve.wait_ge(s_dso[j], 144)
            dve.wait_ge(s_d8, 18)
            nc.vector.memset(nacc, 0.0).then_inc(s_nz, 1)
            dve.wait_ge(s_nz, 1)
            add_squares(16, 0)
            for half in range(2):
                with dve.Fori(0, 8) as m:
                    t = hT[:, ds(m + 8 * half, 1), :]
                    ts(t, t, vec[:, ds(m, 1), 4 + half], None, ALU.mult).then_inc(s_hn, 1)
            dve.wait_ge(s_psfree, J_RMS + 3)
            nc.vector.reciprocal(nbc, nbc).then_inc(s_rs, 1)
            dve.wait_ge(s_rs, 1)
            with dve.Fori(0, 8) as m:
                t = gsT[:, ds(m, 1), :]
                tt(t, t, nbc.rearrange("p (o t) -> p o t", o=1), ALU.mult).then_inc(s_gr, 1)
            dve.wait_ge(s_gr, 8)
            with dve.Fori(0, 4) as r:
                for j in range(2):
                    dve.wait_ge(s_unit, U_SBR + 2 * j + 2 + 4 * r)
                    u = nsq[:, j].rearrange("p (a b) -> p a b", a=3)
                    tt(u, banks(J_SBR + j), tile(gsT, r * 2 + j), ALU.mult).then_inc(s_psfree, 1)
                    dve.wait_ge(s_psfree, J_SBR + j + 3 + 2 * r)
                    t = tile(mixT, r * 2 + j)
                    tt(t, t, u, ALU.add).then_inc(s_mix, 1)

            def residual(j0, unit, per):
                with dve.Fori(0, 4) as r:
                    for j in range(2):
                        dve.wait_ge(s_unit, unit + per * (j + 1) + 2 * per * r)
                        t = tile(res, r * 2 + j)
                        stt(t, t, ALPHA, banks(j0 + j), ALU.mult, ALU.add).then_inc(s_psfree, 1)

            def norm(n, unit, j):
                dve.wait_ge(s_unit, unit + 1)
                ts(nbc.rearrange("p (a b) -> p a b", a=3), banks(j), 1.0 / D, None, ALU.mult).then_inc(s_psfree, 1)
                nc.vector.memset(nacc, 0.0).then_inc(s_nz, 1)
                dve.wait_ge(s_psfree, j + 3)
                with dve.Fori(0, KT) as m:
                    t = res[:, ds(m, 1), :]
                    tt(t, t, nbc.rearrange("p (o t) -> p o t", o=1), ALU.subtract).then_inc(s_dm, 1)
                dve.wait_ge(s_nz, 2 + n)
                add_squares(8, 16 + 8 * n)
                dve.wait_ge(s_psfree, j + 4)
                nc.vector.reciprocal(nbc2, nbc2).then_inc(s_rs, 1)
                dve.wait_ge(s_rs, 2 + n)
                dve.sem_inc(s_pass, 1)
                with dve.Fori(0, KT) as m:
                    t = res[:, ds(m, 1), :]
                    tt(t, t, nbc2.rearrange("p (o t) -> p o t", o=1), ALU.mult).then_inc(s_yn0, 1)

            residual(J_OUT, U_OUT, 1)
            norm(0, U_LN1, J_LN1)
            dve.wait_ge(s_yn, 8)
            dve.wait_ge(s_psfree, J_DOWN + 2)
            residual(J_DOWN, U_DOWN, 4)
            norm(1, U_LN2, J_LN2)

        @block.gpsimd
        def _(pool):
            tt, ts, copy = nc.gpsimd.tensor_tensor, nc.gpsimd.tensor_scalar, nc.gpsimd.tensor_copy
            nc.gpsimd.memset(ident[:], 0.0).then_inc(s_cst0, 1)
            nc.gpsimd.memset(keep[:], 1.0).then_inc(s_cst0, 1)
            nc.gpsimd.memset(far[:], 0.0).then_inc(s_cst0, 1)
            nc.gpsimd.memset(tri[:], 1.0).then_inc(s_cst0, 1)
            pool.wait_ge(s_cst0, 4)
            for t, op, fill, step, ch in ((ident, ALU.not_equal, 1.0, -1, 1), (keep, ALU.is_gt, 0.0, -1, 1),
                                          (far, ALU.is_gt, FAR, -1, 1), (tri, ALU.is_ge, 0.0, 1, -1)):
                nc.gpsimd.affine_select(out=t[:], in_=t[:], compare_op=op, fill=fill, base=0, pattern=[[step, 128]],
                                        channel_multiplier=ch).then_inc(s_const, 1)
            pool.wait_ge(s_psfree, J_KVT + 2)
            with pool.Fori(0, NCHUNK // 2) as r:
                for j in range(2):
                    pool.wait_ge(s_psfree, J_KVT + j + 1 + 2 * r)
                    copy(kvst[:, j], kvT[:, :, ds(r * 256 + 128 * j, 128)]).then_inc(s_kst, 1)
            pool.wait_ge(s_psfree, J_GA)
            copy(kvst[:, 0, :, 0:NDEC], kvT[:, :, SEQ:T]).then_inc(s_kst, 1)
            nc.gpsimd.memset(qbd, 0.0).then_inc(s_qz, 1)
            pool.wait_ge(s_psfree, J_GA + 2)
            with pool.Fori(0, 2) as c:
                with pool.Fori(0, 4) as i:
                    pair = c * 4 + i
                    pool.wait_ge(s_o, pair * 16 + 2)
                    copy(qst, big[:, ds(pair, 1), 0:SEQ].rearrange("p o t -> p (o t)")).then_inc(s_qk, 1)
                    copy(kst, kvT[:, ds(c, 1), 0:SEQ].rearrange("p o t -> p (o t)")).then_inc(s_qk, 1)
                    copy(vst, kvtok[:, 0:8, ds(c * 128 + 256, 128)]).then_inc(s_qk, 1)
                    for m in range(16):
                        S = 128 * (m % 8 + 1)
                        pool.wait_ge(s_far, pair * 16 + (m + 1))
                        tt(zb[:, m % 2, 0:S], zb[:, m % 2, 0:S], sbuf_s[:, m % 2, 0:S], ALU.subtract).then_inc(s_d, 1)
            pool.wait_ge(s_qb, 32)
            for j in range(2):
                copy(qstd[:, j], qbd[:, j]).then_inc(s_qs, 1)
            with pool.Fori(1, NDEC // 2) as r:
                for j in range(2):
                    pool.wait_ge(s_dz, r * 16 + (8 * j - 6))
                    copy(qstd[:, j], qbd[:, ds(r * 2 + j, 1)].rearrange("p o c n -> p (o c) n")).then_inc(s_qs, 1)

            with pool.Fori(0, GROUPS) as g:
                pool.wait_ge(s_cout, g * 6 + 8)
                pool.sem_inc(s_pass, 1)
                with pool.Fori(0, NCHUNK // 2) as r:
                    for j in range(2):
                        n = g * 8 + 2 * r + j
                        pool.wait_ge(s_hupd, n + 1)
                        copy(xst[:, j], xsT[:, :, ds(r * 256 + 128 * j, 128)]).then_inc(s_stg, 1)
                        copy(bst[:, j], bT[:, ds(r * 256 + 128 * j, 128)]).then_inc(s_stg, 1)
                        pool.wait_ge(s_M, n + 1)
                        pool.wait_ge(s_bc, 2 * n + 2)
                        tt(seg, seg, cbm.rearrange("p (o l) -> p o l", o=1).to_broadcast([128, 8, 128]), ALU.mult).then_inc(s_Mm, 1)
                wide8 = lambda v: v.rearrange("p (b o) -> p b o", o=1).to_broadcast([128, NDEC, 128])
                pool.wait_ge(s_bcr, g * 16 + 16)
                pool.sem_inc(s_pass, 1)
                with pool.Fori(0, 2) as r:
                    for j in range(2):
                        n = g * 4 + 2 * r + j
                        pool.wait_ge(s_d1, n + 1)
                        tt(t2, bcb[:, 0], wide8(xdd), ALU.mult).then_inc(s_d2, 1)
                        pool.wait_ge(s_d4, n + 1)
                        tt(t2, h0b[:, j], bcb[:, 1], ALU.mult).then_inc(s_d5, 1)

            def sums(n, j0):
                nc.gpsimd.memset(nacc, 0.0).then_inc(s_nz2, 1)
                pool.wait_ge(s_nz2, 1 + n)
                pool.sem_inc(s_pass, 1)
                with pool.Fori(0, KT) as m:
                    pool.wait_ge(s_psfree, m + (j0 + 3))
                    pool.wait_ge(s_nsum, m + (8 * n + 2))
                    tt(nacc, nacc, res[:, ds(m, 1), :].rearrange("p o t -> p (o t)"), ALU.add).then_inc(s_nsum, 1)

            pool.wait_ge(s_mix, 8)
            sums(0, J_OUT)
            with pool.Fori(0, 32) as m:
                pool.wait_ge(s_psfree, m + (J_UP + 3))
                t = hidT[:, ds(m, 1), :]
                tt(t, t, t, ALU.mult).then_inc(s_hid, 1)
            sums(1, J_DOWN)
            pool.wait_ge(s_yn, 16)
            with pool.Fori(0, NCHUNK // 2) as r:
                for j in range(2):
                    pool.wait_ge(s_psfree, J_Y + j + 1 + 2 * r)
                    copy(yst[:, j], res[:, :, ds(r * 256 + 128 * j, 128)]).then_inc(s_ys, 1)
            pool.wait_ge(s_psfree, J_Y + 9)
            copy(yst[:, 0, :, 0:NDEC], res[:, :, SEQ:T]).then_inc(s_ys, 1)


_INS = ['x_prompt', 'x_sample', 'cache_k', 'cache_v', 'state_ssm', 'state_conv', 'page_table',
        'w_in', 'conv_w', 'conv_b', 'dt_bias', 'a_log', 'd_skip', 'ssm_norm_w', 'w_ssm_br', 'w_attn_br',
        'sb_logit_bias', 'w_out', 'ln1_g', 'ln1_b', 'w_up', 'w_down', 'ln2_g', 'ln2_b']
_OUTS = [(1, 1024, 1024), (8, 1, 1024), (1, 1, 1024, 4, 64), (1, 1, 1024, 4, 64), (1, 1, 32, 64, 128),
         (1, 1, 3, 3072), (1, 8, 1, 4, 64), (1, 8, 1, 4, 64), (1, 8, 32, 64, 128), (1, 8, 3, 3072)]


def kernel(**inputs):
    import numpy as _np
    import concourse.bacc as _bacc
    from concourse import mybir as _mybir
    from concourse.bass_utils import run_bass_kernel_spmd as _run

    nc = _bacc.Bacc("TRN2", target_bir_lowering=False, num_devices=1)
    arrays, ins, outs = {}, {}, []
    for name in _INS:
        a = _np.ascontiguousarray(inputs[name])
        arrays[f"in_{name}_dram"] = a
        ins[name] = nc.dram_tensor(f"in_{name}_dram", a.shape, _mybir.dt.from_np(a.dtype), kind="ExternalInput").ap()
    for i, shape in enumerate(_OUTS):
        outs.append(nc.dram_tensor(f"out_{i}_dram", shape, _mybir.dt.float32, kind="ExternalOutput").ap())
    build(nc, ins, outs)
    r = _run(nc, [arrays], core_ids=[0])
    return tuple(r.results[0][f"out_{i}_dram"] for i in range(len(_OUTS)))
```

```python
import concourse.bass as bass
from concourse import mybir
from contextlib import ExitStack

F32 = mybir.dt.float32
I32 = mybir.dt.int32
ACT = mybir.ActivationFunctionType
ALU = mybir.AluOpType
AX_X = mybir.AxisListType.X
ds = bass.ds

D = 1024
SEQ = 1024
NDEC = 8
T = SEQ + NDEC
TN = T // 3
KT = D // 128
D_INNER = 2048
HEADS = 32
GROUPS = 4
NSTATE = 128
CONV_DIM = D_INNER + 2 * GROUPS * NSTATE
CT = CONV_DIM // 128
CHUNK = 128
NCHUNK = SEQ // CHUNK
SB_HEADS = 16
HD = 64
KV = 4
PAGES = 16
PAST = 2048
N_POOL = 160
D_FF = 4096
COL_Z, COL_X = 0, D_INNER
COL_B = COL_X + D_INNER
COL_C = COL_B + GROUPS * NSTATE
COL_DT = COL_C + GROUPS * NSTATE
COL_Q = COL_DT + HEADS
COL_K = COL_Q + SB_HEADS * HD
COL_V = COL_K + KV * HD
COL_GS = COL_V + KV * HD
COL_GA = COL_GS + D
SCALE = HD ** -0.5
ALPHA = 2.0 ** 0.25
EPS = 1e-5
DT_CUM = 13
FAR = 1e30
RAWLEN = 3 + SEQ + 4 * NDEC
ACCLEN = RAWLEN - 3
DEC0 = SEQ + 3
NPAR = 5 + 3 * NDEC

J_X = 0
J_PAR = J_X + NCHUNK + 1
J_QKV = J_PAR + 2
J_KVT = J_QKV + 12
J_ABR = J_KVT + 9
J_DT = J_ABR + 8
J_SSD = J_DT + 2
J_GS = J_SSD + 6 * GROUPS
J_RMS = J_GS + 8
J_SBR = J_RMS + 1
J_OUT = J_SBR + 8
J_LN1 = J_OUT + 8
J_UP = J_LN1 + 2
J_DOWN = J_UP + 32
J_LN2 = J_DOWN + 8
J_TAIL = J_LN2 + 2
J_Y = J_TAIL + 2
J_END = J_Y + 9
U_SBR = J_SBR
U_OUT = U_SBR + 16
U_LN1 = U_OUT + 8
U_UP = U_LN1 + 2
U_DOWN = U_UP + 32
U_LN2 = U_DOWN + 32
U_TAIL = U_LN2 + 2
U_Y = U_TAIL + 2
P_QKV = 0
P_ABR = P_QKV + 12
P_DT = P_ABR
P_SSD = P_DT + 1
P_GS = P_SSD + 6 * GROUPS
P_SBR = P_GS + 8
P_OUT = P_SBR + 16
P_UP = P_OUT + 8
P_DOWN = P_UP + 32


def build(nc, ins, outs):
    y_prompt, y_sample, k_prompt, v_prompt, ssm_prompt, conv_prompt, k_sample, v_sample, ssm_sample, conv_sample = outs
    w_in = ins["w_in"][0].rearrange("(t p) n -> p t n", p=128)
    w_ssm = ins["w_ssm_br"][0].rearrange("(t p) n -> p t n", p=128)
    w_out = ins["w_out"][0].rearrange("(t p) n -> p t n", p=128)
    w_up = ins["w_up"][0].rearrange("(t p) n -> p t n", p=128)
    w_down = ins["w_down"][0].rearrange("(t p) n -> p t n", p=128)
    w_att = ins["w_attn_br"][0].rearrange("(c k i d) n -> k d c i n", c=2, k=2, i=4)
    scr_cum = nc.dram_tensor("scr_cum", [HEADS, SEQ], F32, kind="Internal").ap()
    scr_dec = nc.dram_tensor("scr_dec", [2, HEADS, NDEC], F32, kind="Internal").ap()
    scr_z = nc.dram_tensor("scr_z", [24, 128, T], F32, kind="Internal").ap()
    scr_mix = nc.dram_tensor("scr_mix", [8, 128, T], F32, kind="Internal").ap()
    scr_bc = nc.dram_tensor("scr_bc", [GROUPS, 2, NDEC, NSTATE], F32, kind="Internal").ap()

    with ExitStack() as ctx:
        def sb(name, shape, dt=F32):
            return ctx.enter_context(nc.sbuf_tensor(name, shape, dt))

        def sem(name):
            return ctx.enter_context(nc.semaphore(name))

        res = sb("res", [128, KT, T])
        big = sb("big", [128, 32, T])
        wbuf = sb("wbuf", [128, 2, 8, 128])
        work = sb("work", [128, 7168])
        ident = sb("ident", [128, 128])
        ones = sb("ones", [128, 128])
        keep = sb("keep", [128, 128])
        far = sb("far", [128, 128])
        tri = sb("tri", [128, 128])
        par = sb("par", [128, CT, NPAR])
        vec = sb("vec", [128, KT, 6])
        tail = sb("tail", [128, CT, 3 + NDEC])
        cumtok = sb("cumtok", [128, NCHUNK, HEADS])
        dttok = sb("dttok", [128, NCHUNK, HEADS])
        dtx = sb("dtx", [128, 2, 16, NDEC])
        dskip = sb("dskip", [128, 16])
        sbb = sb("sbb", [128, SB_HEADS])
        sbd = sb("sbd", [128, 1])
        dtb = sb("dtb", [HEADS, 1])
        alog = sb("alog", [HEADS, 1])
        pages = sb("pages", [1, NDEC * PAGES], I32)
        eps = sb("eps", [128, 1])
        small = sb("small", [128, 64])
        PS = ctx.enter_context(nc.psum_tensor("PS", [128, 8, 512], F32))

        flat = big[:, :, :].rearrange("p t n -> p (t n)")

        def carve(base, *shape):
            n = 1
            for s in shape:
                n *= s
            return base[:, 0:n] if len(shape) == 1 else base[:, 0:n].rearrange(
                {2: "p (a b) -> p a b", 3: "p (a b c) -> p a b c"}[len(shape)],
                **dict(zip("abc", shape)))

        def area(off, *shape):
            return carve(flat[:, off:], *shape)

        def wk(off, *shape):
            return carve(work[:, off:], *shape)

        qT = big[:, 0:8, :]
        kvT = big[:, 24:28, :]
        mixT = big[:, 16:24, :]
        hT = big[:, 0:16, :]
        xsT = big[:, 24:28, :]
        bT = big[:, 28, :]
        cT = big[:, 29, :]
        gsT = big[:, 24:32, :]
        hidT = big
        xbuf = area(24 * T, 2, 1024)
        xsam = area(26 * T + 512, 1024)
        prow = area(8 * T, CONV_DIM)
        vrow = area(11 * T + 64, 1024)
        kvtok = area(8 * T, 9, 512)
        o = 8 * T + 9 * 512
        qst = area(o, 1024)
        kst = area(o + 1024, 1024)
        vst = area(o + 2048, 8, 128)
        zb = wk(0, 2, 2, 1024)
        sbuf_s = wk(4096, 2, 1024)
        lb = area(o + 3072, 2, 2, 1024)
        wTb = area(o + 7168, 2, 16, 128)
        kvst = area(28 * T, 2, 4, 128)
        pbuf = area(8 * T, 2, PAGES, 256)
        o = 8 * T + 2 * PAGES * 256
        zd = area(o, PAST)
        ld = area(o + PAST, PAST)
        sd = area(o + 2 * PAST, PAST)
        wTd = area(o + 3 * PAST, PAGES, 128)
        kTst = area(28 * T, 2, 512)
        qbd = area(28 * T + 1032, NDEC, 2, 128)
        qstd = area(28 * T + 3080, 2, 2, 128)
        pst = area(28 * T + 3080, 3, TN)
        w3 = wk(6144, 8, 128)
        raw = wk(0, RAWLEN)
        acc = wk(RAWLEN + 1, ACCLEN)
        sig = wk(RAWLEN + 1 + ACCLEN, ACCLEN)
        cumb = wk(0, 2, 8, 128)
        seg = wk(2048, 8, 128)
        ecm = wk(3072, 8, 128)
        xdt = wk(4096, 8, 64)
        xdte = wk(4608, 8, 64)
        hst = wk(5120, 8, 64)
        btok = wk(5632, 128)
        cbm = wk(5760, 128)
        y1 = wk(5888, 4, 128)
        hout = wk(6400, 4, 128)
        xst = area(30 * T, 2, 4, 128)
        bst = area(30 * T + 1024, 2, 128)
        t8 = small[:, 0:8]
        dte = small[:, 8:16]
        cd = small[:, 16:24]
        xdd = small[:, 24:32]
        yd = small[:, 32:40]
        zsg = wk(3176, T)
        h0b = carve(flat[:, 16 * T:], 4 * NDEC, 128).rearrange("p (q b) n -> p q b n", q=4)
        t2 = area(16 * T + 4096, NDEC, 128)
        bcb = area(16 * T + 5120, 2, NDEC, 128)
        dtr, dte1, dtu, dtl, dtv = [work[0:HEADS, 1040 * n:1040 * n + T] for n in range(5)]
        chm = work[0:HEADS, 5200:5200 + SEQ]
        nacc = wk(0, T)
        nsq = wk(1032, 2, T)
        nbc = wk(3096, T)
        nbc2 = wk(4128, T)
        ytok = area(0, 2, 1024)
        yst = area(3 * T, 2, 8, 128)
        tailrow = area(8 * T, CONV_DIM)

        s_pass = sem("s_pass")
        s_const = sem("s_const")
        s_par = sem("s_par")
        s_small = sem("s_small")
        s_xin = [sem("s_xin0"), sem("s_xin1")]
        s_w = [sem("s_w0"), sem("s_w1")]
        s_unit = sem("s_unit")
        s_psfree = sem("s_psfree")

        block = ctx.enter_context(nc.Block())

        def banks(j, n=3, w=TN):
            return PS[:, 3 * (j % 2):3 * (j % 2) + n, 0:w]

        def tile(t, m):
            return t[:, ds(m, 1), :].rearrange("p o (a b) -> p (o a) b", b=TN)

        s_kst = sem("s_kst")
        s_kvo = sem("s_kvo")
        s_qk = sem("s_qk")
        s_z = sem("s_z")
        s_zs = sem("s_zs")
        s_ab = sem("s_ab")
        s_ex = sem("s_ex")
        s_ln = sem("s_ln")
        s_sp = sem("s_sp")
        s_spm = sem("s_spm")
        s_scan = sem("s_scan")
        s_far = sem("s_far")
        s_d = sem("s_d")
        s_wt = sem("s_wt")
        s_tr = sem("s_tr")
        s_cp = sem("s_cp")
        s_o = sem("s_o")
        s_oc = sem("s_oc")
        s_w3 = [sem("s_w3_0"), sem("s_w3_1"), sem("s_w3_2")]
        s_p3 = sem("s_p3")
        s_pc = sem("s_pc")
        s_pst = [sem("s_pst0"), sem("s_pst1"), sem("s_pst2")]
        s_ga = [sem("s_ga0"), sem("s_ga1"), sem("s_ga2"), sem("s_ga3")]
        s_gas = sem("s_gas")
        s_zl = sem("s_zl")
        s_zm = sem("s_zm")
        s_pt = sem("s_pt")
        s_kp = [sem("s_kp0"), sem("s_kp1")]
        s_wa = [sem("s_wa0"), sem("s_wa1")]
        s_dact = sem("s_dact")
        s_dd = sem("s_dd")
        s_dexp = sem("s_dexp")
        s_tok = sem("s_tok")
        s_nz = sem("s_nz")
        s_nz2 = sem("s_nz2")
        s_cst0 = sem("s_cst0")
        s_yn0 = sem("s_yn0")
        s_rz = sem("s_rz")
        s_yout = [sem("s_yout0"), sem("s_yout1")]
        s_nsum = sem("s_nsum")
        s_dm = sem("s_dm")
        s_rs = sem("s_rs")
        s_yn = sem("s_yn")
        s_qz = sem("s_qz")
        s_qb = sem("s_qb")
        s_qs = sem("s_qs")
        s_dtr = sem("s_dtr")
        s_dcp = sem("s_dcp")
        s_dz = sem("s_dz")
        s_dtw = sem("s_dtw")
        s_dcw = sem("s_dcw")
        s_do = sem("s_do")
        s_doc = sem("s_doc")
        s_dt = sem("s_dt")
        s_dta = sem("s_dta")
        s_scr = sem("s_scr")
        s_dtx = sem("s_dtx")
        s_dtxe = sem("s_dtxe")
        s_zsg = sem("s_zsg")
        s_raw = sem("s_raw")
        s_cv = sem("s_cv")
        s_csg = sem("s_csg")
        s_cout = sem("s_cout")
        s_cb = [sem("s_cb0"), sem("s_cb1")]
        s_stg = sem("s_stg")
        s_tp = sem("s_tp")
        s_bc = sem("s_bc")
        s_t8 = sem("s_t8")
        s_t8e = sem("s_t8e")
        s_dte = sem("s_dte")
        s_cd = sem("s_cd")
        s_xdt = sem("s_xdt")
        s_sg = sem("s_sg")
        s_sg2 = sem("s_sg2")
        s_M = sem("s_M")
        s_Mm = sem("s_Mm")
        s_ec = sem("s_ec")
        s_CE = sem("s_CE")
        s_y = sem("s_y")
        s_st = sem("s_st")
        s_y1 = sem("s_y1")
        s_y2 = sem("s_y2")
        s_hm = sem("s_hm")
        s_hupd = sem("s_hupd")
        s_h0 = sem("s_h0")
        s_ht = sem("s_ht")
        s_hc = sem("s_hc")
        s_ho = sem("s_ho")
        s_bcw = sem("s_bcw")
        s_bcr = sem("s_bcr")
        s_dh = sem("s_dh")
        s_mxo = sem("s_mxo")
        s_mxi = sem("s_mxi")
        s_d1 = sem("s_d1")
        s_d2 = sem("s_d2")
        s_d3 = sem("s_d3")
        s_d4 = sem("s_d4")
        s_d5 = sem("s_d5")
        s_d6 = sem("s_d6")
        s_d7 = sem("s_d7")
        s_d8 = sem("s_d8")
        s_dso = sem("s_dso")
        s_sq = sem("s_sq")
        s_nac = sem("s_nac")
        s_hn = sem("s_hn")
        s_gr = sem("s_gr")
        s_mix = sem("s_mix")
        s_hid = sem("s_hid")
        s_ys = sem("s_ys")
        s_yo = sem("s_yo")
        s_out = sem("s_out")

        def turns(qb):
            return [(k, kb, min(4, qb + 1 - kb)) for k in range(2) for kb in range(0, qb + 1, 4)]

        def turned(qb):
            return sum(len(turns(x)) for x in range(qb))

        def load_pages(eng, cache, r, j, half):
            with eng.Fori(0, PAGES // 8) as i:
                for n in range(4):
                    m = i * 4 + (n + half * PAGES // 2)
                    page = eng.value_load(pages[0:1, ds(r * 2 * PAGES + i * 4 + (n + half * PAGES // 2 + j * PAGES), 1)],
                                          min_val=0, max_val=N_POOL - 1)
                    eng.dma_start(pbuf[:, j, ds(m, 1), :],
                                  ins[cache][0, ds(page, 1)].rearrange("o t g d -> t o (g d)")).then_inc(s_kp[j], 16)

        @block.sync
        def _(sp):
            def load(slot, lo, src_lo, hi, src_hi, unit):
                sp.wait_ge(s_unit, unit - 1)
                sp.dma_start(lo, src_lo).then_inc(s_w[slot], 16)
                sp.dma_start(hi, src_hi).then_inc(s_w[slot], 16)

            def load_cols(P, unit, w, k0, col, n=128):
                b = wbuf[:, P % 2]
                load(P % 2, b[:, 0:4, 0:n], w[:, k0:k0 + 4, ds(col, n)], b[:, 4:8, 0:n], w[:, k0 + 4:k0 + 8, ds(col, n)],
                     unit)

            sp.dma_start(prow[0:4, :], ins["conv_w"][0]).then_inc(s_par, 16)
            sp.dma_start(prow[4:5, :], ins["conv_b"]).then_inc(s_par, 16)
            sp.dma_start(prow[5:NPAR, :], ins["state_conv"][0].rearrange("b k c -> (b k) c")).then_inc(s_par, 16)
            for n, name in enumerate(("ln1_g", "ln1_b", "ln2_g", "ln2_b")):
                sp.dma_start(vrow[n:n + 1, :], ins[name]).then_inc(s_par, 16)
            sp.dma_start(vrow[4:6, :], ins["ssm_norm_w"].rearrange("o (a d) -> (o a) d", a=2)).then_inc(s_par, 16)
            for n in range(2):
                sp.dma_start(xbuf[:, n, :], ins["x_prompt"][0, n * 128:(n + 1) * 128, :]).then_inc(s_xin[n], 16)
            sp.dma_start(xsam[0:NDEC, :], ins["x_sample"].rearrange("b o d -> (b o) d")).then_inc(s_small, 16)
            with nc.allow_non_contiguous_dma("small parameters"):
                for k in range(2):
                    src = ins["d_skip"].rearrange("o (j k) -> o k j", k=2)[:, k, :]
                    sp.dma_start(dskip[64 * k:64 * k + 64, :], src.to_broadcast([64, 16])).then_inc(s_small, 16)
                sp.dma_start(sbb[:], ins["sb_logit_bias"].to_broadcast([128, SB_HEADS])).then_inc(s_small, 16)
                for b in range(NDEC):
                    sp.dma_start(sbd[16 * b:16 * b + 16, :], ins["sb_logit_bias"].rearrange("o h -> h o")).then_inc(s_small, 16)
                sp.dma_start(dtb[:], ins["dt_bias"].rearrange("o h -> h o")).then_inc(s_small, 16)
                sp.dma_start(alog[:], ins["a_log"].rearrange("o h -> h o")).then_inc(s_small, 16)
            sp.dma_start(pages[:], ins["page_table"].rearrange("b n -> (b n)").rearrange("(o n) -> o n", o=1)).then_inc(s_pt, 16)
            with sp.Fori(1, NCHUNK // 2) as r:
                for j in range(2):
                    sp.wait_ge(s_unit, 2 * r + j - 1)
                    sp.dma_start(xbuf[:, j, :], ins["x_prompt"][0, ds(r * 256 + j * 128, 128), :]).then_inc(s_xin[j], 16)

            for c in range(2):
                with sp.Fori(0, 2) as r:
                    for j in range(2):
                        n = 4 * c + j
                        cols = [COL_Q + 512 * c + 256 * k + 64 * j for k in range(2)]
                        b = wbuf[:, n % 2]
                        load(n % 2, b[:, :, 0:64], w_in[:, :, ds(r * 128 + cols[0], 64)],
                             b[:, :, 64:128], w_in[:, :, ds(r * 128 + cols[1], 64)], J_QKV + n + 2 * r)
            with sp.Fori(0, 2) as r:
                for j in range(2):
                    load_cols(P_QKV + 8 + j, J_QKV + 8 + j + 2 * r, w_in, 0, r * 256 + (COL_K + 128 * j))

            sp.wait_ge(s_psfree, J_ABR + 2)
            for t, po, so in ((0, k_prompt, k_sample), (256, v_prompt, v_sample)):
                sp.dma_start(po[0, 0].rearrange("(t p) g d -> p t (g d)", p=128), kvtok[:, 0:8, t:t + 256]).then_inc(s_kvo, 16)
                sp.dma_start(so[0].rearrange("b o g d -> (b o) (g d)"), kvtok[0:NDEC, 8, t:t + 256]).then_inc(s_kvo, 16)

            w3bufs = (wbuf[:, 0], wbuf[:, 1], w3)

            def load3(t, col):
                sp.dma_start(w3bufs[t][:, 0:4], w_in[:, 0:4, ds(col, 128)]).then_inc(s_w3[t], 16)
                sp.dma_start(w3bufs[t][:, 4:8], w_in[:, 4:8, ds(col, 128)]).then_inc(s_w3[t], 16)

            def thirds(pair, cols):
                for m in range(9):
                    t, th = m // 3, m % 3
                    sp.wait_ge(s_pc, pair * 9 + (m + 2))
                    sp.dma_start(scr_z[ds(pair * 3 + t, 1), :, th * TN:th * TN + TN].rearrange("o p n -> p (o n)"),
                                 pst[:, th, :]).then_inc(s_pst[th], 16)
                    if th == 2 and cols:
                        load3(t, cols[t])

            sp.wait_ge(s_unit, J_KVT)
            for t in range(3):
                load3(t, 128 * t)
            with sp.Fori(0, 4) as pair:
                thirds(pair, [pair * 384 + 128 * (3 + t) for t in range(3)])
            thirds(4, [COL_Z + 128 * 15, COL_GA, COL_GA + 128])
            with sp.Fori(5, 7) as pair:
                thirds(pair, [pair * 384 + (COL_GA + 128 * (2 + t - 15)) for t in range(3)])
            thirds(7, None)

            sp.wait_ge(s_pt, 16)
            sp.wait_ge(s_kvo, 64)
            sp.wait_ge(s_oc, 66)
            for j in range(2):
                load_pages(sp, "cache_k", 0, j, 0)
            with sp.Fori(1, NDEC // 2) as r:
                for j in range(2):
                    sp.wait_ge(s_dtr, 16 * r + 8 * (j - 1))
                    sp.sem_inc(s_pass, 1)
                    load_pages(sp, "cache_k", r, j, 0)
            for j in range(2):
                sp.wait_ge(s_dtr, 56 + 8 * j)
                load_pages(sp, "cache_v", 0, j, 0)
            with sp.Fori(1, NDEC // 2) as r:
                for j in range(2):
                    sp.wait_ge(s_do, 2 * r + j - 1)
                    sp.sem_inc(s_pass, 1)
                    load_pages(sp, "cache_v", r, j, 0)

            for k in range(3):
                sp.wait_ge(s_pst[k], 16 * 25)
            sp.wait_ge(s_doc, NDEC + 2)
            for n in range(4):
                sp.dma_start(mixT[:, 2 * n:2 * n + 2, :], scr_z[16 + 2 * n:18 + 2 * n].rearrange("t p n -> p t n")).then_inc(s_ga[n], 16)
            with sp.Fori(0, 4) as r:
                for j in range(2):
                    b = wbuf[:, (P_ABR + j) % 2]
                    sp.wait_ge(s_unit, J_ABR + j - 1 + 2 * r)
                    for k in range(2):
                        for c in range(2):
                            sp.dma_start(b[64 * k:64 * k + 64, 4 * c:4 * c + 4, :],
                                         w_att[k, :, c, :, ds(r * 256 + 128 * j, 128)]).then_inc(s_wa[(P_ABR + j) % 2], 16)

            load_cols(P_DT, J_DT, w_in, 0, COL_DT, HEADS)
            sp.wait_ge(s_psfree, J_DT + 2)
            for n in range(4):
                sp.dma_start(scr_mix[2 * n:2 * n + 2].rearrange("t p n -> p t n"), mixT[:, 2 * n:2 * n + 2, :]).then_inc(s_mxo, 16)
            sp.wait_ge(s_unit, J_DT)
            for n in range(4):
                sp.dma_start(hT[:, 4 * n:4 * n + 4, :], scr_z[4 * n:4 * n + 4].rearrange("t p n -> p t n")).then_inc(s_zl, 16)

            sp.wait_ge(s_dt, DT_CUM)
            sp.dma_start(scr_cum, dtv[:, 0:SEQ]).then_inc(s_scr, 16)
            sp.dma_start(scr_dec[0], dtl[:, SEQ:T]).then_inc(s_scr, 16)
            sp.dma_start(scr_dec[1], dtr[:, SEQ:T]).then_inc(s_scr, 16)
            sp.wait_ge(s_scr, 48)
            for n in range(2):
                for k in range(2):
                    src = scr_dec[n].rearrange("(j k) b -> k j b", k=2)[k:k + 1]
                    sp.dma_start(dtx[64 * k:64 * k + 64, n], src.to_broadcast([64, 16, NDEC])).then_inc(s_dtx, 16)

            def group(g, last):
                for n in (2, 3):
                    load_cols(P_SSD + n, J_SSD + n + 6 * g, w_in, 0, g * 512 + (COL_X + 128 * n))
                load_cols(P_SSD + 4, J_SSD + 4 + 6 * g, w_in, 0, g * 128 + COL_B)
                load_cols(P_SSD + 5, J_SSD + 5 + 6 * g, w_in, 0, g * 128 + COL_C)
                sp.wait_ge(s_cout, 6 * g + 8)
                sp.sem_inc(s_pass, 1)
                with sp.Fori(0, NCHUNK // 2) as r:
                    for j in range(2):
                        sp.wait_ge(s_hupd, g * 8 + 2 * r + (j + 1))
                        src = scr_cum[ds(g * 8, 8), ds(r * 256 + j * 128, 128)]
                        sp.dma_start(cumb[:, j], src.rearrange("(o h) l -> o h l", o=1).to_broadcast([128, 8, 128])).then_inc(s_cb[j], 16)
                sp.wait_ge(s_dso, g * 64 + 16)
                sp.wait_ge(s_d8, g * 4 + 2)
                sp.wait_ge(s_mxo, 64)
                for q in range(4):
                    src = ins["state_ssm"][0].rearrange("b h p n -> (h p) b n")[ds(g * 512 + q * 128, 128)]
                    sp.dma_start(h0b[:, q], src).then_inc(s_dh, 16)
                with nc.allow_non_contiguous_dma("B, C of the decode tokens, token-major"):
                    for n, t in enumerate((bT, cT)):
                        sp.dma_start(scr_bc[ds(g, 1), n].rearrange("o b s -> s (o b)"), t[:, SEQ:T]).then_inc(s_bcw, 16)
                sp.wait_ge(s_bcw, 32 * g + 32)
                sp.sem_inc(s_pass, 1)
                sp.dma_start(bcb[:], scr_bc[ds(g, 1)].to_broadcast([128, 2, NDEC, NSTATE])).then_inc(s_bcr, 16)
                for n in range(2):
                    if last:
                        load_cols(P_GS + n, J_GS + n, w_in, 0, COL_GS + 128 * n)
                    else:
                        load_cols(P_SSD + 6 + n, J_SSD + 6 + n + 6 * g, w_in, 0, g * 512 + (COL_X + 512 + 128 * n))
                sp.wait_ge(s_hc, g + 3)
                sp.dma_start(ssm_prompt[0, 0].rearrange("h p n -> (h p) n")[ds(g * 512, 512), :].rearrange("(j q) n -> q j n", q=128),
                             hout[:]).then_inc(s_ho, 16)

            for n in range(2):
                load_cols(P_SSD + n, J_SSD + n, w_in, 0, COL_X + 128 * n)
            with sp.Fori(0, GROUPS - 1) as g:
                group(g, False)
            group(GROUPS - 1, True)

            with sp.Fori(1, 4) as r:
                for j in range(2):
                    load_cols(P_GS + j, J_GS + j + 2 * r, w_in, 0, r * 256 + (COL_GS + 128 * j))
            sp.wait_ge(s_dso, 64 * GROUPS + 16)
            sp.wait_ge(s_d8, 18)
            for n in range(4):
                sp.dma_start(mixT[:, 2 * n:2 * n + 2, :], scr_mix[2 * n:2 * n + 2].rearrange("t p n -> p t n")).then_inc(s_mxi, 16)
            with sp.Fori(0, 4) as r:
                for j in range(2):
                    for kp in range(2):
                        n = 2 * j + kp
                        load_cols(P_SBR + n, U_SBR + n + 4 * r, w_ssm, 8 * kp, r * 256 + 128 * j)
            with sp.Fori(0, 4) as r:
                for j in range(2):
                    load_cols(P_OUT + j, U_OUT + j + 2 * r, w_out, 0, r * 256 + 128 * j)
            with sp.Fori(0, 16) as r:
                for j in range(2):
                    load_cols(P_UP + j, U_UP + j + 2 * r, w_up, 0, r * 256 + 128 * j)
            with sp.Fori(0, 4) as r:
                for j in range(2):
                    for kp in range(4):
                        n = 4 * j + kp
                        load_cols(P_DOWN + n, U_DOWN + n + 8 * r, w_down, 8 * kp, r * 256 + 128 * j)

            sp.wait_ge(s_psfree, J_Y + 2)
            sp.dma_start(conv_prompt[0, 0], tailrow[0:3, :]).then_inc(s_out, 16)
            sp.dma_start(conv_sample[0, :, 2, :], tailrow[3:3 + NDEC, :]).then_inc(s_out, 16)
            sp.dma_start(conv_sample[0, :, 0:2, :], ins["state_conv"][0, :, 1:3, :]).then_inc(s_out, 16)
            with sp.Fori(0, NCHUNK // 2) as r:
                for j in range(2):
                    sp.wait_ge(s_psfree, J_Y + j + 3 + 2 * r)
                    sp.dma_start(y_prompt[0, ds(r * 256 + 128 * j, 128), :], ytok[:, j, :]).then_inc(s_yout[j], 16)
            sp.wait_ge(s_psfree, J_END + 2)
            sp.dma_start(y_sample.rearrange("b o d -> (b o) d"), ytok[0:NDEC, 0, :]).then_inc(s_yo, 16)
            sp.wait_ge(s_yout[0], 80)
            sp.wait_ge(s_yout[1], 80)
            sp.wait_ge(s_yo, 16)
            sp.wait_ge(s_out, 48)
            sp.wait_ge(s_kvo, 64)
            sp.wait_ge(s_ho, 80)
            sp.wait_ge(s_dso, 64 * GROUPS + 16)

        @block.tensor
        def _(pe):
            def product(j, joff, unit, p, off, kpieces, x, m=128, wa=False):
                pe.wait_ge(s_psfree, j + 1 + joff)
                for kp in range(kpieces):
                    slot = (p + kp) % 2
                    if wa:
                        pe.wait_ge(s_wa[slot], 64 * ((p + kp - P_ABR) // 2 + 1) + 32 * off)
                    else:
                        pe.wait_ge(s_w[slot], 32 * ((p + kp) // 2 + 1) + 16 * off)
                    for n in range(3):
                        for k in range(8):
                            mm = nc.tensor.matmul(PS[0:m, 3 * (j % 2) + n, 0:TN], wbuf[:, slot, k, 0:m],
                                                  x[:, 8 * kp + k, n * TN:(n + 1) * TN],
                                                  start=(kp == 0 and k == 0), stop=(kp == kpieces - 1 and k == 7))
                    mm.then_inc(s_unit, 1)

            def turn(bank, col, src, part=128):
                n = src.shape[1]
                return nc.tensor.transpose(PS[0:n, bank, col:col + part], src, ident[0:part, 0:part])

            pe.wait_ge(s_const, 5)
            with pe.Fori(0, NCHUNK // 2) as r:
                for j in range(2):
                    pe.wait_ge(s_xin[j], 16 * r + 16)
                    pe.wait_ge(s_psfree, J_X + j + 1 + 2 * r)
                    for f in range(KT):
                        mm = turn(3 * ((J_X + j) % 2) + f // 4, 128 * (f % 4), xbuf[:, j, 128 * f:128 * f + 128])
                    mm.then_inc(s_unit, 1)
            pe.wait_ge(s_small, 16 * 14)
            pe.wait_ge(s_psfree, J_PAR)
            for f in range(KT):
                mm = turn(3 * ((J_X + 8) % 2), NDEC * f, xsam[0:NDEC, 128 * f:128 * f + 128], NDEC)
            mm.then_inc(s_unit, 1)
            pe.wait_ge(s_par, 16 * 8)
            pe.wait_ge(s_psfree, J_PAR + 1)
            for t in range(CT):
                mm = turn(3 * (J_PAR % 2) + t // 12, NPAR * (t % 12), prow[0:NPAR, 128 * t:128 * t + 128], NPAR)
            mm.then_inc(s_unit, 1)
            pe.wait_ge(s_psfree, J_PAR + 2)
            for f in range(KT):
                mm = turn(3 * ((J_PAR + 1) % 2), 6 * f, vrow[0:6, 128 * f:128 * f + 128], 6)
            mm.then_inc(s_unit, 1)

            pe.wait_ge(s_psfree, J_PAR + 2)
            with pe.Fori(0, 6) as r:
                for j in range(2):
                    product(J_QKV + j, 2 * r, J_QKV + j, P_QKV + j, 2 * r, 1, res)

            with pe.Fori(0, NCHUNK // 2) as r:
                for j in range(2):
                    pe.wait_ge(s_kst, j + 1 + 2 * r)
                    pe.wait_ge(s_psfree, J_KVT + j + 1 + 2 * r)
                    for f in range(4):
                        mm = turn(3 * ((J_KVT + j) % 2), 128 * f, kvst[:, j, f, :])
                    mm.then_inc(s_unit, 1)
            pe.wait_ge(s_kst, 9)
            pe.wait_ge(s_psfree, J_ABR)
            for f in range(4):
                mm = turn(3 * ((J_KVT + 8) % 2), 128 * f, kvst[:, 0, f, 0:NDEC])
            mm.then_inc(s_unit, 1)

            pe.wait_ge(s_psfree, J_ABR + 2)
            with pe.Fori(0, 2) as c:
                with pe.Fori(0, 4) as i:
                    pair = c * 4 + i
                    pe.wait_ge(s_qk, pair * 3 + 3)
                    for m in range(10):
                        if m < 8:
                            pe.wait_ge(s_ab, pair * 8 + (m + 1))
                            for k in range(2):
                                for s0 in range(0, 128 * (m + 1), 512):
                                    w = min(512, 128 * (m + 1) - s0)
                                    mm = nc.tensor.matmul(PS[:, 2 * k + s0 // 512, 0:w],
                                                          qst[64 * k:64 * k + 64, 128 * m:128 * m + 128],
                                                          kst[64 * k:64 * k + 64, s0:s0 + w], start=True, stop=True)
                            mm.then_inc(s_z, 1)
                        if m >= 2:
                            qb = m - 2
                            pe.wait_ge(s_cp, pair * 24 + (turned(qb + 1) + 2))
                            pe.wait_ge(s_oc, pair * 8 + (m - 1))
                            for k in range(2):
                                for kb in range(qb + 1):
                                    mm = nc.tensor.matmul(PS[64 * k:64 * k + 64, 6, 128 * (m % 2):128 * (m % 2) + 128],
                                                          vst[:, kb, 64 * k:64 * k + 64], wTb[:, m % 2, 8 * k + kb, :],
                                                          start=(kb == 0), stop=(kb == qb))
                            mm.then_inc(s_o, 1)
                        if m < 9:
                            t, th = m // 3, m % 3
                            if th == 0:
                                pe.wait_ge(s_w3[t], pair * 32 + 32)
                            pe.wait_ge(s_pc, pair * 9 + (m + 1))
                            for k in range(8):
                                mm = nc.tensor.matmul(PS[:, 7, 0:TN], (wbuf[:, 0], wbuf[:, 1], w3)[t][:, k, :],
                                                      res[:, k, th * TN:th * TN + TN], start=(k == 0), stop=(k == 7))
                            mm.then_inc(s_p3, 1)
                        if 1 <= m < 9:
                            pe.wait_ge(s_wt, pair * 8 + m)
                            for n, (k, kb0, nb) in enumerate(turns(m - 1)):
                                pe.wait_ge(s_cp, pair * 24 + (turned(m - 1) + n + 1))
                                for b in range(nb):
                                    kb = kb0 + b
                                    mm = turn(4 + n % 2, 128 * b, zb[:, (m - 1) % 2, k, 128 * kb:128 * kb + 128])
                                mm.then_inc(s_tr, 1)

            def decode_keys(b, j, first, last):
                pe.wait_ge(s_kp[j], 16 * PAGES + 8 * PAGES * (b - j))
                pe.wait_ge(s_qs, b + 1)
                for q in range(9):
                    if q < 8:
                        c, jb = q // 4, q % 4
                        pe.wait_ge(s_dcp, b * 8 + (q + 1))
                        for n in range(4):
                            mm = turn(4 + q % 2, 128 * n, pbuf[:, j, 4 * jb + n, 128 * c:128 * c + 128])
                        mm.then_inc(s_dtr, 1)
                    if q >= 1:
                        c, jb = (q - 1) // 4, (q - 1) % 4
                        pe.wait_ge(s_dcp, b * 8 + (q + 2))
                        nc.tensor.matmul(PS[:, jb, :], qstd[:, j, c, :], kTst[:, (q - 1) % 2, :],
                                         start=(first and c == 0), stop=(last and c == 1)).then_inc(s_dz, 1)

            pe.wait_ge(s_oc, 66)
            decode_keys(0, 0, True, False)
            decode_keys(1, 1, False, False)
            with pe.Fori(1, 3) as r:
                for j in range(2):
                    decode_keys(r * 2 + j, j, False, False)
            decode_keys(6, 0, False, False)
            decode_keys(7, 1, False, True)
            pe.wait_ge(s_dexp, 1)
            for n in range(PAGES):
                mm = turn(n // 4, 128 * (n % 4), zd[:, 128 * n:128 * n + 128])
            mm.then_inc(s_dtw, 1)
            pe.wait_ge(s_dcw, 1)
            with pe.Fori(0, NDEC // 2) as r:
                for j in range(2):
                    pe.wait_ge(s_kp[j], 16 * PAGES * 5 + 16 * PAGES * r)
                    pe.wait_ge(s_doc, j + 1 + 2 * r)
                    for c in range(2):
                        for n in range(PAGES):
                            mm = nc.tensor.matmul(PS[:, 4 + j, 8 * c:8 * c + 8], pbuf[:, j, n, 128 * c:128 * c + 128],
                                                  wTd[:, n, ds(r * 32 + (16 * j + 8 * c), 8)],
                                                  start=(n == 0), stop=(n == PAGES - 1))
                    mm.then_inc(s_do, 1)

            pe.wait_ge(s_doc, NDEC + 2)
            with pe.Fori(0, 4) as r:
                for j in range(2):
                    product(J_ABR + j, 2 * r, J_ABR + j, P_ABR + j, 2 * r, 1, qT, wa=True)

            product(J_DT, 0, J_DT, P_DT, 0, 1, res, m=HEADS)
            pe.wait_ge(s_dt, DT_CUM)
            pe.wait_ge(s_psfree, J_DT + 2)
            for n in range(NCHUNK):
                turn(3 * ((J_DT + 1) % 2), 32 * n, dtv[:, 128 * n:128 * n + 128], HEADS)
                mm = turn(3 * ((J_DT + 1) % 2), 256 + 32 * n, dtr[:, 128 * n:128 * n + 128], HEADS)
            mm.then_inc(s_unit, 1)

            with pe.Fori(0, GROUPS) as g:
                pe.wait_ge(s_hupd, g * 8 + 2)
                pe.wait_ge(s_hc, g + 2)
                for n in range(6):
                    product(J_SSD + n, 6 * g, J_SSD + n, P_SSD + n, 6 * g, 1, res)
                pe.wait_ge(s_psfree, g * 6 + (J_SSD + 8))
                pe.sem_inc(s_pass, 1)
                with pe.Fori(0, NCHUNK // 2) as r:
                    for j in range(2):
                        n = g * 8 + 2 * r + j
                        pe.wait_ge(s_stg, 2 * n + 2)
                        pe.wait_ge(s_hupd, n + 1)
                        for f in range(4):
                            turn(3 * j, 128 * f, xst[:, j, f, :])
                        turn(3 * j + 1, 0, bst[:, j, :])
                        nc.tensor.matmul(PS[:, 3 * j + 1, 128:256], bst[:, j, :], cT[:, ds(r * 256 + 128 * j, 128)],
                                         start=True, stop=True).then_inc(s_tp, 1)
                        pe.wait_ge(s_bc, 2 * n + 2)
                        pe.wait_ge(s_xdt, 2 * n + 2)
                        nc.tensor.matmul(PS[:, 6 + j, :], btok, xdte.rearrange("p h d -> p (h d)"),
                                         start=True, stop=True).then_inc(s_st, 1)
                        pe.wait_ge(s_Mm, n + 1)
                        pe.wait_ge(s_CE, n + 1)
                        pe.wait_ge(s_hupd, n + 2)
                        pe.wait_ge(s_h0, g + 1)
                        for h in range(8):
                            y = PS[64 * (h % 2):64 * (h % 2) + 64, 3 * j + 2, 128 * (h // 2):128 * (h // 2) + 128]
                            nc.tensor.matmul(y, xdt[:, h, :], seg[:, h, :], start=True, stop=False)
                            mm = nc.tensor.matmul(y, hst[:, h, :], ecm[:, h, :], start=False, stop=True)
                        mm.then_inc(s_y, 1)
                pe.wait_ge(s_hupd, g * 8 + 10)
                for f in range(4):
                    mm = turn(0, 128 * f, hst[:, 2 * f:2 * f + 2, :].rearrange("p h d -> p (h d)"))
                mm.then_inc(s_ht, 1)

            pe.wait_ge(s_hc, GROUPS + 2)
            with pe.Fori(0, 4) as r:
                for j in range(2):
                    product(J_GS + j, 2 * r, J_GS + j, P_GS + j, 2 * r, 1, res)

            def column_sums(j, ready, value):
                pe.wait_ge(ready, value)
                pe.wait_ge(s_psfree, j + 1)
                for n in range(3):
                    mm = nc.tensor.matmul(PS[:, 3 * (j % 2) + n, 0:TN], ones[:], nacc[:, n * TN:(n + 1) * TN],
                                          start=True, stop=True)
                mm.then_inc(s_unit, 1)

            column_sums(J_RMS, s_nac, 18)
            pe.wait_ge(s_hn, 16)
            with pe.Fori(0, 4) as r:
                for j in range(2):
                    product(J_SBR + j, 2 * r, U_SBR + 2 * j, P_SBR + 2 * j, 4 * r, 2, hT)
            pe.wait_ge(s_mix, 8)
            with pe.Fori(0, 4) as r:
                for j in range(2):
                    product(J_OUT + j, 2 * r, U_OUT + j, P_OUT + j, 2 * r, 1, mixT)
            column_sums(J_LN1, s_nsum, 10)
            column_sums(J_LN1 + 1, s_nac, 26)
            pe.wait_ge(s_yn, 8)
            with pe.Fori(0, 16) as r:
                for j in range(2):
                    product(J_UP + j, 2 * r, U_UP + j, P_UP + j, 2 * r, 1, res)
            pe.wait_ge(s_hid, 32)
            with pe.Fori(0, 4) as r:
                for j in range(2):
                    product(J_DOWN + j, 2 * r, U_DOWN + 4 * j, P_DOWN + 4 * j, 8 * r, 4, hidT)
            column_sums(J_LN2, s_nsum, 18)
            column_sums(J_LN2 + 1, s_nac, 34)
            for n in range(2):
                pe.wait_ge(s_psfree, J_TAIL + n + 1)
                for t in range(12):
                    mm = turn(3 * ((J_TAIL + n) % 2) + t // 4, 128 * (t % 4), tail[:, 12 * n + t, :])
                mm.then_inc(s_unit, 1)
            with pe.Fori(0, NCHUNK // 2) as r:
                for j in range(2):
                    pe.wait_ge(s_ys, j + 1 + 2 * r)
                    pe.wait_ge(s_psfree, J_Y + j + 1 + 2 * r)
                    for f in range(KT):
                        mm = turn(3 * ((J_Y + j) % 2) + f // 4, 128 * (f % 4), yst[:, j, f, :])
                    mm.then_inc(s_unit, 1)
            pe.wait_ge(s_ys, 9)
            pe.wait_ge(s_psfree, J_Y + 9)
            for f in range(KT):
                mm = turn(3 * ((J_Y + 8) % 2) + f // 4, 128 * (f % 4), yst[:, 0, f, 0:NDEC])
            mm.then_inc(s_unit, 1)

        @block.scalar
        def _(act):
            def fn(out, in_, f, **kw):
                return nc.scalar.activation(out, in_, f, **kw)

            with act.Fori(0, NCHUNK // 2) as r:
                for j in range(2):
                    act.wait_ge(s_unit, J_X + j + 1 + 2 * r)
                    act.sem_inc(s_pass, 1)
                    nc.scalar.copy(res[:, :, ds(r * 256 + 128 * j, 128)].rearrange("p (a f) b -> p a f b", a=2),
                                   banks(J_X + j, 2, 512).rearrange("p a (f b) -> p a f b", b=128)).then_inc(s_psfree, 1)
            act.wait_ge(s_unit, J_PAR)
            nc.scalar.copy(res[:, :, SEQ:T], PS[:, 3 * ((J_X + 8) % 2), 0:KT * NDEC].rearrange("p (f b) -> p f b", b=NDEC)).then_inc(s_psfree, 1)
            act.wait_ge(s_unit, J_PAR + 1)
            nc.scalar.copy(par[:, :, :].rearrange("p (a t) n -> p a (t n)", a=2), banks(J_PAR, 2, 12 * NPAR)).then_inc(s_psfree, 1)
            act.wait_ge(s_unit, J_PAR + 2)
            nc.scalar.copy(vec[:, :, :], PS[:, 3 * ((J_PAR + 1) % 2), 0:6 * KT].rearrange("p (f n) -> p f n", n=6)).then_inc(s_psfree, 1)
            for c0, n, t in ((0, 4, qT), (8, 2, kvT)):
                with act.Fori(0, n) as r:
                    for j in range(2):
                        act.wait_ge(s_unit, J_QKV + c0 + j + 1 + 2 * r)
                        act.sem_inc(s_pass, 1)
                        nc.scalar.copy(tile(t, r * 2 + j), banks(J_QKV + c0 + j)).then_inc(s_psfree, 1)
            with act.Fori(0, NCHUNK // 2) as r:
                for j in range(2):
                    act.wait_ge(s_unit, J_KVT + j + 1 + 2 * r)
                    act.sem_inc(s_pass, 1)
                    nc.scalar.copy(kvtok[:, ds(r * 2 + j, 1), :], banks(J_KVT + j, 1, 512)).then_inc(s_psfree, 1)
            act.wait_ge(s_unit, J_ABR)
            nc.scalar.copy(kvtok[0:NDEC, 8:9, :], PS[0:NDEC, 3 * ((J_KVT + 8) % 2):3 * ((J_KVT + 8) % 2) + 1, :]).then_inc(s_psfree, 1)

            act.wait_ge(s_small, 16 * 14)
            act.preload_act_table_set("natural_log_exp_and_others")
            with act.Fori(0, 2) as c:
                with act.Fori(0, 4) as i:
                    pair = c * 4 + i
                    for m in range(10):
                        S = 128 * (m + 1)
                        M = pair * 8 + m
                        if m < 8:
                            z = [PS[:, 2 * k:2 * k + 2, :].rearrange("p a b -> p (a b)")[:, 0:S] for k in range(2)]
                            bias = [sbb[:, ds(c * 8 + i + 4 * k, 1)] for k in range(2)]
                            l = lb[:, m % 2, :, 0:S]
                            act.wait_ge(s_z, M + 1)
                            act.sem_inc(s_pass, 1)
                            fn(zb[:, m % 2, 0, 0:S], z[0], ACT.Identity, bias=bias[0], scale=SCALE)
                            fn(zb[:, m % 2, 1, 0:S], z[1], ACT.Identity, bias=bias[1], scale=SCALE).then_inc(s_zs, 1)
                            act.wait_ge(s_scan, 2 * M + 2)
                            act.sem_inc(s_pass, 1)
                            fn(l[:, 0], z[0], ACT.Abs, bias=bias[0], scale=SCALE)
                            fn(l[:, 1], z[1], ACT.Abs, bias=bias[1], scale=SCALE).then_inc(s_ab, 1)
                            act.wait_ge(s_ab, M + 2)
                            fn(l, l, ACT.Exp, scale=-1.0).then_inc(s_ex, 1)
                        if m >= 1:
                            th = (m - 1) % 3
                            act.wait_ge(s_p3, pair * 9 + m)
                            act.wait_ge(s_pst[th], pair * 48 + (16 * ((m - 1) // 3) + 16))
                            nc.scalar.copy(pst[:, th, :], PS[:, 7, 0:TN]).then_inc(s_pc, 1)
                        if m >= 2:
                            act.wait_ge(s_o, pair * 8 + (m + 1))
                            act.sem_inc(s_pass, 1)
                            nc.scalar.copy(big[:, ds(pair, 1), 128 * (m - 2):128 * (m - 1)],
                                           PS[:, 6:7, 128 * (m % 2):128 * (m % 2) + 128]).then_inc(s_oc, 1)
                        if m < 8:
                            act.wait_ge(s_ex, M + 1)
                            fn(l, l, ACT.Ln, bias=1.0).then_inc(s_ln, 1)
                        if 1 <= m < 9:
                            act.wait_ge(s_d, 2 * pair * 8 + (2 * m + 2))
                            w = zb[:, (m - 1) % 2, :, 0:128 * m]
                            fn(w, w, ACT.Exp).then_inc(s_wt, 1)

            act.wait_ge(s_pt, 16)
            act.wait_ge(s_kvo, 64)
            act.wait_ge(s_oc, 66)
            for j in range(2):
                load_pages(act, "cache_k", 0, j, 1)

            def copy_keys(b):
                for q in range(8):
                    act.wait_ge(s_dtr, b * 8 + (q + 1))
                    act.wait_ge(s_dz, b * 8 + (q + 1))
                    nc.scalar.copy(kTst[:, q % 2, :], PS[:, 4 + q % 2, :]).then_inc(s_dcp, 1)

            with act.Fori(0, NDEC // 2 - 1) as r:
                for j in range(2):
                    copy_keys(r * 2 + j)
                    load_pages(act, "cache_k", r + 1, j, 1)
            for j in range(2):
                copy_keys(6 + j)
                load_pages(act, "cache_v", 0, j, 1)
            zall = PS[:, 0:4, :].rearrange("p a b -> p (a b)")
            act.wait_ge(s_dz, 66)
            fn(zd, zall, ACT.Identity, bias=sbd[:], scale=SCALE).then_inc(s_dact, 1)
            fn(ld, zall, ACT.Abs, bias=sbd[:], scale=SCALE).then_inc(s_dact, 1)
            act.wait_ge(s_dact, 2)
            fn(ld, ld, ACT.Exp, scale=-1.0).then_inc(s_dact, 1)
            act.wait_ge(s_dact, 3)
            fn(ld, ld, ACT.Ln, bias=1.0).then_inc(s_dact, 1)
            act.wait_ge(s_dd, 3)
            fn(zd, zd, ACT.Exp).then_inc(s_dexp, 1)
            with act.Fori(1, NDEC // 2) as r:
                for j in range(2):
                    act.wait_ge(s_do, 2 * r + j - 1)
                    act.sem_inc(s_pass, 1)
                    load_pages(act, "cache_v", r, j, 1)

            for n in range(4):
                act.wait_ge(s_ga[n], 16)
                t = mixT[:, 2 * n:2 * n + 2, :]
                fn(t, t, ACT.Sigmoid).then_inc(s_gas, 2)

            act.wait_ge(s_small, 16 * 14)
            fn(alog[:], alog[:], ACT.Exp).then_inc(s_dta, 1)
            act.wait_ge(s_dt, 2)
            fn(dte1, dtr, ACT.Abs).then_inc(s_dta, 1)
            act.wait_ge(s_dta, 2)
            fn(dte1, dte1, ACT.Exp, scale=-1.0).then_inc(s_dta, 1)
            act.wait_ge(s_dt, 3)
            fn(dtl, dtu, ACT.Ln).then_inc(s_dta, 1)
            act.wait_ge(s_dtx, 64)
            fn(dtx[:, 0], dtx[:, 0], ACT.Exp).then_inc(s_dtxe, 1)

            def out_state(g, q):
                act.wait_ge(s_d4, g * 4 + (q + 1))
                dst = ssm_sample[0].rearrange("b h p n -> (h p) b n")[ds(g * 512 + q * 128, 128)]
                act.dma_start(dst, h0b[:, q]).then_inc(s_dso, 16)

            def conv(g, decode):
                act.wait_ge(s_rz, g + 1)
                for n in range(4):
                    act.wait_ge(s_zm, g * 4 + (n + 1))
                    if n == 0:
                        act.sem_inc(s_pass, 1)
                        act.wait_ge(s_zl, 64)
                    act.sem_inc(s_pass, 1)
                    fn(zsg, hT[:, ds(g * 4 + n, 1), :].rearrange("p o t -> p (o t)"), ACT.Sigmoid).then_inc(s_zsg, 1)
                for n in range(6):
                    ct = g * 4 + n if n < 4 else g + (16 + 4 * (n - 4))
                    J = J_SSD + n
                    act.wait_ge(s_unit, g * 6 + (J + 1))
                    if n == 0:
                        act.wait_ge(s_psfree, g * 6 + (J + 2))
                    act.wait_ge(s_cv, g * 24 + (4 * n + 2))
                    b0 = 3 * (J % 2)
                    nc.scalar.copy(raw[:, 3:3 + 2 * TN].rearrange("p (a b) -> p a b", a=2), PS[:, b0:b0 + 2, 0:TN])
                    nc.scalar.copy(raw[:, 3 + 2 * TN:3 + SEQ], PS[:, b0 + 2, 0:TN - NDEC])
                    nc.scalar.copy(raw[:, 3 + SEQ:RAWLEN].rearrange("p (b k) -> p b k", k=4)[:, :, 0:3],
                                   par[:, ds(ct, 1), 5:NPAR].rearrange("p o (b k) -> p (o b) k", k=3))
                    nc.scalar.copy(raw[:, 3 + SEQ:RAWLEN].rearrange("p (b k) -> p b k", k=4)[:, :, 3:4],
                                   PS[:, b0 + 2, TN - NDEC:TN].rearrange("p (b o) -> p b o", o=1)).then_inc(s_raw, 1)
                    nc.scalar.copy(tail[:, ds(ct, 1), :], PS[:, b0 + 2:b0 + 3, TN - NDEC - 3:TN]).then_inc(s_psfree, 1)
                    act.wait_ge(s_cv, g * 24 + (4 * n + 6))
                    act.wait_ge(s_cout, g * 6 + (n + 2))
                    fn(sig, acc, ACT.Sigmoid).then_inc(s_csg, 1)
                    if decode and n < 4:
                        out_state(g - 1, n)

            def chunks(g):
                with act.Fori(0, NCHUNK // 2) as r:
                    for j in range(2):
                        n = g * 8 + 2 * r + j
                        act.wait_ge(s_cb[j], g * 64 + 16 * r + 16)
                        act.wait_ge(s_y, n + 2)
                        fn(ecm, cumb[:, j], ACT.Exp).then_inc(s_ec, 1)
                        act.wait_ge(s_hupd, n + 2)
                        fn(cd, cumb[:, j, :, 127], ACT.Exp).then_inc(s_cd, 1)
                        act.wait_ge(s_t8, n + 1)
                        fn(t8, t8, ACT.Exp).then_inc(s_t8e, 1)
                        act.wait_ge(s_sg2, n + 1)
                        fn(seg, seg, ACT.Exp).then_inc(s_M, 1)
                act.wait_ge(s_ht, g + 1)
                act.wait_ge(s_ho, g * 16 + 16)
                nc.scalar.copy(hout.rearrange("p j n -> p (j n)"), PS[:, 0, :]).then_inc(s_hc, 1)

            conv(0, False)
            chunks(0)
            with act.Fori(1, GROUPS) as g:
                conv(g, True)
                chunks(g)
            for q in range(4):
                out_state(GROUPS - 1, q)
            act.wait_ge(s_d8, 18)

            with act.Fori(0, 4) as r:
                for j in range(2):
                    act.wait_ge(s_unit, J_GS + j + 1 + 2 * r)
                    act.sem_inc(s_pass, 1)
                    fn(tile(gsT, r * 2 + j), banks(J_GS + j), ACT.Sigmoid).then_inc(s_psfree, 1)

            def squares(t, n, base, nbase):
                with act.Fori(0, n // 2) as r:
                    for j in range(2):
                        if t is res:
                            act.wait_ge(s_dm, nbase + j + 1 + 2 * r)
                        act.wait_ge(s_nac, base + j + 1 + 2 * r)
                        act.sem_inc(s_pass, 1)
                        fn(nsq[:, j], t[:, ds(r * 2 + j, 1), :].rearrange("p o t -> p (o t)"), ACT.Square).then_inc(s_sq, 1)

            squares(hT, 16, 0, 0)
            act.wait_ge(s_unit, J_RMS + 1)
            fn(nbc.rearrange("p (a b) -> p a b", a=3), banks(J_RMS), ACT.Sqrt, bias=eps[:], scale=1.0 / D_INNER).then_inc(s_psfree, 1)

            def norm(n, unit, j):
                squares(res, 8, 16 + 8 * n, 8 * n)
                act.wait_ge(s_unit, unit + 2)
                fn(nbc2.rearrange("p (a b) -> p a b", a=3), banks(j + 1), ACT.Sqrt, bias=eps[:], scale=1.0 / D).then_inc(s_psfree, 1)
                with act.Fori(0, KT) as m:
                    act.wait_ge(s_yn0, m + (8 * n + 1))
                    act.sem_inc(s_pass, 1)
                    fn(res[:, ds(m, 1), :], res[:, ds(m, 1), :], ACT.Identity, bias=vec[:, ds(m, 1), 2 * n + 1],
                       scale=vec[:, ds(m, 1), 2 * n]).then_inc(s_yn, 1)

            norm(0, U_LN1, J_LN1)
            with act.Fori(0, 16) as r:
                for j in range(2):
                    act.wait_ge(s_unit, U_UP + j + 1 + 2 * r)
                    act.sem_inc(s_pass, 1)
                    fn(tile(hidT, r * 2 + j), banks(J_UP + j), ACT.Relu).then_inc(s_psfree, 1)
            norm(1, U_LN2, J_LN2)
            for n in range(2):
                act.wait_ge(s_unit, U_TAIL + n + 1)
                b0 = 3 * ((J_TAIL + n) % 2)
                nc.scalar.copy(tailrow[0:3 + NDEC, 1536 * n:1536 * n + 1536].rearrange("p (a b) -> p a b", a=3),
                               PS[0:3 + NDEC, b0:b0 + 3, :]).then_inc(s_psfree, 1)
            with act.Fori(0, NCHUNK // 2) as r:
                for j in range(2):
                    act.wait_ge(s_unit, U_Y + j + 1 + 2 * r)
                    act.wait_ge(s_yout[j], 16 * r + 16)
                    nc.scalar.copy(ytok[:, j, :].rearrange("p (a b) -> p a b", a=2), banks(J_Y + j, 2, 512)).then_inc(s_psfree, 1)
            act.wait_ge(s_unit, U_Y + 9)
            act.wait_ge(s_yout[0], 80)
            b0 = 3 * ((J_Y + 8) % 2)
            nc.scalar.copy(ytok[0:NDEC, 0, :].rearrange("p (a b) -> p a b", a=2), PS[0:NDEC, b0:b0 + 2, :]).then_inc(s_psfree, 1)

        @block.vector
        def _(dve):
            tt, ts, stt, copy = nc.vector.tensor_tensor, nc.vector.tensor_scalar, nc.vector.scalar_tensor_tensor, nc.vector.tensor_copy
            dve.sem_inc(s_ab, 1)
            dve.sem_inc(s_pc, 1)
            dve.sem_inc(s_zm, 1)
            dve.sem_inc(s_scan, 4)
            for s in (s_psfree, s_d, s_o, s_oc, s_dcp, s_cp, s_dz, s_doc, s_hupd, s_nac, s_hc, s_y, s_cv, s_cout, s_nsum, s_d8):
                dve.sem_inc(s, 2)
            for s in (*s_yout, *s_pst, s_ho, s_dso):
                dve.sem_inc(s, 16)
            nc.vector.memset(eps[:], EPS)
            nc.vector.memset(ones[:], 1.0).then_inc(s_const, 1)

            dve.wait_ge(s_qz, 1)
            dve.wait_ge(s_psfree, J_KVT + 2)
            for b in range(NDEC):
                for c in range(2):
                    for k in range(2):
                        dst = qbd[64 * k:64 * k + 64, b, c, 16 * b + 8 * c + 4 * k:16 * b + 8 * c + 4 * k + 4]
                        copy(dst, big[64 * k:64 * k + 64, 4 * c:4 * c + 4, SEQ + b]).then_inc(s_qb, 1)
            dve.wait_ge(s_const, 5)
            both = lambda v: v[:, :].rearrange("p (o s) -> p o s", o=1).to_broadcast([128, 2, 128])
            with dve.Fori(0, 8) as pair:
                for m in range(9):
                    if m < 8:
                        S = 128 * (m + 1)
                        M = pair * 8 + m
                        l = lb[:, m % 2]
                        dve.wait_ge(s_ln, M + 1)
                        stt(l[:, :, 0:S], zb[:, m % 2, :, 0:S], 0.0, l[:, :, 0:S], ALU.max, ALU.add).then_inc(s_sp, 1)
                        dve.wait_ge(s_sp, M + 1)
                        tt(l[:, :, S - 128:S], l[:, :, S - 128:S], both(keep), ALU.mult).then_inc(s_spm, 1)
                        dve.wait_ge(s_spm, M + 1)
                        back = slice(S - 1, None, -1)
                        for k in range(2):
                            dve.wait_ge(s_d, 2 * M + (k + 1))
                            nc.vector.tensor_tensor_scan(sbuf_s[:, k, back], ones[:, 0:1].to_broadcast([128, S]), l[:, k, back],
                                                         0.0, ALU.mult, ALU.add).then_inc(s_scan, 1)
                        for k in range(2):
                            dve.wait_ge(s_scan, 2 * M + (k + 5))
                            tt(sbuf_s[:, k, S - 128:S], sbuf_s[:, k, S - 128:S], far[:], ALU.add).then_inc(s_far, 1)
                    if m >= 1:
                        dve.wait_ge(s_o, pair * 8 + m)
                        for n, (k, kb0, nb) in enumerate(turns(m - 1)):
                            dve.wait_ge(s_tr, pair * 24 + (turned(m - 1) + n + 1))
                            copy(wTb[:, (m - 1) % 2, 8 * k + kb0:8 * k + kb0 + nb, :].rearrange("p a b -> p (a b)"),
                                 PS[:, 4 + n % 2, 0:128 * nb]).then_inc(s_cp, 1)

            dve.wait_ge(s_dact, 4)
            stt(ld, zd, 0.0, ld, ALU.max, ALU.add).then_inc(s_dd, 1)
            dve.wait_ge(s_dd, 1)
            nc.vector.tensor_tensor_scan(sd[:, ::-1], ones[:, 0:1].to_broadcast([128, PAST]), ld[:, ::-1], 0.0, ALU.mult, ALU.add).then_inc(s_dd, 1)
            dve.wait_ge(s_dd, 2)
            tt(zd, zd, sd, ALU.subtract).then_inc(s_dd, 1)
            dve.wait_ge(s_dtw, 1)
            copy(wTd.rearrange("p a b -> p (a b)"), PS[:, 0:4, :].rearrange("p a b -> p (a b)")).then_inc(s_dcw, 1)
            with dve.Fori(0, NDEC // 2) as r:
                for j in range(2):
                    dve.wait_ge(s_do, 2 * r + j + 1)
                    o = PS[:, 4 + j, 0:16].rearrange("p (c k i) -> p c k i", c=2, k=2)
                    for k in range(2):
                        dst = big[64 * k:64 * k + 64, 0:8, ds(r * 2 + (SEQ + j), 1)].rearrange("p (c i) o -> p c (i o)", c=2)
                        op = copy(dst, o[64 * k:64 * k + 64, :, k, :])
                    op.then_inc(s_doc, 1)

            dve.wait_ge(s_psfree, J_ABR + 2)
            with dve.Fori(0, 4) as r:
                for j in range(2):
                    dve.wait_ge(s_gas, j + 1 + 2 * r)
                    dve.sem_inc(s_pass, 1)
                    dve.wait_ge(s_unit, J_ABR + j + 1 + 2 * r)
                    t = tile(mixT, r * 2 + j)
                    tt(t, banks(J_ABR + j), t, ALU.mult).then_inc(s_psfree, 1)

            dve.wait_ge(s_dta, 1)
            ts(alog[:], alog[:], -1.0, None, ALU.mult).then_inc(s_dt, 1)
            dve.wait_ge(s_unit, J_DT + 1)
            dve.wait_ge(s_psfree, J_DT + 2)
            ts(dtr.rearrange("p (a b) -> p a b", a=3), PS[0:HEADS, 3 * (J_DT % 2):3 * (J_DT % 2) + 3, 0:TN], dtb[:], None,
               ALU.add).then_inc(s_dt, 1)
            dve.wait_ge(s_dta, 3)
            ts(dtu, dte1, 1.0, None, ALU.add).then_inc(s_dt, 1)
            dve.wait_ge(s_dt, 3)
            ts(dtv, dtu, 1.0, None, ALU.subtract).then_inc(s_dt, 1)
            dve.wait_ge(s_dt, 4)
            tt(dtv, dte1, dtv, ALU.subtract).then_inc(s_dt, 1)
            dve.wait_ge(s_dta, 4)
            nc.vector.reciprocal(dtu, dtu).then_inc(s_dt, 1)
            dve.wait_ge(s_dt, 6)
            tt(dtv, dtv, dtu, ALU.mult).then_inc(s_dt, 1)
            dve.wait_ge(s_dt, 7)
            tt(dtl, dtl, dtv, ALU.add).then_inc(s_dt, 1)
            dve.wait_ge(s_dt, 8)
            stt(dtr, dtr, 0.0, dtl, ALU.max, ALU.add).then_inc(s_dt, 1)
            nc.vector.memset(chm, 1.0).then_inc(s_dt, 1)
            dve.wait_ge(s_dt, 10)
            nc.vector.memset(chm.rearrange("p (c l) -> p c l", l=CHUNK)[:, :, 0:1], 0.0).then_inc(s_dt, 1)
            ts(dtl, dtr, alog[:], None, ALU.mult).then_inc(s_dt, 1)
            dve.wait_ge(s_dt, 12)
            nc.vector.tensor_tensor_scan(dtv[:, 0:SEQ], chm, dtl[:, 0:SEQ], 0.0, ALU.mult, ALU.add).then_inc(s_dt, 1)
            dve.wait_ge(s_dt, DT_CUM)
            dve.sem_inc(s_psfree, 1)
            dve.wait_ge(s_unit, J_DT + 2)
            b0 = 3 * ((J_DT + 1) % 2)
            copy(cumtok[:, :, :].rearrange("p c h -> p (c h)"), PS[:, b0, 0:256]).then_inc(s_tok, 1)
            copy(dttok[:, :, :].rearrange("p c h -> p (c h)"), PS[:, b0, 256:512]).then_inc(s_psfree, 1)
            dve.wait_ge(s_tok, 1)
            dve.wait_ge(s_psfree, J_SSD + 2)

            def decode_step(g, q):
                wide8 = lambda v: v.rearrange("p (b o) -> p b o", o=1).to_broadcast([128, NDEC, 128])
                n = g * 4 + q
                if q == 0:
                    dve.wait_ge(s_bcr, g * 16 + 16)
                    dve.sem_inc(s_pass, 1)
                    dve.wait_ge(s_dtxe, 1)
                xcol = xsT[:, q, SEQ:T]
                tt(xdd, xcol, dtx[:, 1, ds(n, 1), :].rearrange("p o b -> p (o b)"), ALU.mult).then_inc(s_d1, 1)
                if q == 0:
                    dve.wait_ge(s_dh, g * 64 + 64)
                tt(h0b[:, q], h0b[:, q], wide8(dtx[:, 0, ds(n, 1), :].rearrange("p o b -> p (o b)")), ALU.mult).then_inc(s_d3, 1)
                dve.wait_ge(s_d2, n + 1)
                dve.wait_ge(s_d3, n + 1)
                tt(h0b[:, q], h0b[:, q], t2, ALU.add).then_inc(s_d4, 1)
                dve.wait_ge(s_d5, n + 1)
                nc.vector.tensor_reduce(yd, t2, AX_X, ALU.add).then_inc(s_d6, 1)
                dve.wait_ge(s_d6, n + 1)
                stt(yd, xcol, dskip[:, ds(n, 1)], yd, ALU.mult, ALU.add).then_inc(s_d7, 1)
                dve.wait_ge(s_d7, n + 1)
                t = hT[:, ds(n, 1), SEQ:T].rearrange("p o b -> p (o b)")
                tt(t, t, yd, ALU.mult).then_inc(s_d8, 1)

            def conv(g, decode):
                dve.wait_ge(s_hc, g + 2)
                dve.wait_ge(s_scr, 48)
                nc.vector.memset(hst, 0.0).then_inc(s_h0, 1)
                nc.vector.memset(raw[:, 0:3], 0.0).then_inc(s_rz, 1)
                dve.wait_ge(s_psfree, g * 6 + (J_SSD + 2))
                for n in range(4):
                    dve.wait_ge(s_zsg, g * 4 + (n + 1))
                    dve.sem_inc(s_pass, 1)
                    t = hT[:, ds(g * 4 + n, 1), :]
                    tt(t, t, zsg.rearrange("p (o t) -> p o t", o=1), ALU.mult).then_inc(s_zm, 1)
                for n in range(6):
                    if decode and n < 4:
                        decode_step(g - 1, n)
                    ct = g * 4 + n if n < 4 else g + (16 + 4 * (n - 4))
                    w = [par[:, ds(ct, 1), k] for k in range(5)]
                    dve.wait_ge(s_raw, g * 6 + (n + 1))
                    dve.wait_ge(s_cout, g * 6 + (n + 2))
                    ts(acc, raw[:, 0:ACCLEN], w[0], w[4], ALU.mult, ALU.add).then_inc(s_cv, 1)
                    for k in range(1, 4):
                        dve.wait_ge(s_cv, g * 24 + (4 * n + k + 2))
                        stt(acc, raw[:, k:k + ACCLEN], w[k], acc, ALU.mult, ALU.add).then_inc(s_cv, 1)
                    dve.wait_ge(s_csg, g * 6 + (n + 1))
                    t = big[:, 24 + n, :]
                    tt(t[:, 0:SEQ], acc[:, 0:SEQ], sig[:, 0:SEQ], ALU.mult)
                    tt(t[:, SEQ:T], acc[:, DEC0:ACCLEN:4], sig[:, DEC0:ACCLEN:4], ALU.mult).then_inc(s_cout, 1)

            def chunks(g):
                with dve.Fori(0, NCHUNK // 2) as r:
                    for j in range(2):
                        n = g * 8 + 2 * r + j
                        c = r * 2 + j
                        cum8 = cumtok[:, ds(c, 1), ds(g * 8, 8)].rearrange("p o h -> p (o h)")
                        dt8 = dttok[:, ds(c, 1), ds(g * 8, 8)].rearrange("p o h -> p (o h)")
                        wide = lambda v, w: v.rearrange("p (h o) -> p h o", o=1).to_broadcast([128, 8, w])
                        dve.wait_ge(s_cb[j], g * 64 + 16 * r + 16)
                        dve.wait_ge(s_hupd, n + 2)
                        tt(t8, cumb[:, j, :, 127], cum8, ALU.subtract).then_inc(s_t8, 1)
                        tt(seg, cumb[:, j], wide(cum8, 128), ALU.subtract).then_inc(s_sg, 1)
                        dve.wait_ge(s_sg, n + 1)
                        ts(seg, seg, 0.0, None, ALU.min).then_inc(s_sg2, 1)
                        dve.wait_ge(s_tp, n + 1)
                        copy(btok, PS[:, 3 * j + 1, 0:128]).then_inc(s_bc, 1)
                        tt(cbm, PS[:, 3 * j + 1, 128:256], tri[:], ALU.mult).then_inc(s_bc, 1)
                        dve.wait_ge(s_t8e, n + 1)
                        tt(dte, t8, dt8, ALU.mult).then_inc(s_dte, 1)
                        x = PS[:, 3 * j, :].rearrange("p (h d) -> p h d", d=64)
                        tt(xdt, x, wide(dt8, 64), ALU.mult).then_inc(s_xdt, 1)
                        dve.wait_ge(s_dte, n + 1)
                        tt(xdte, x, wide(dte, 64), ALU.mult).then_inc(s_xdt, 1)
                        dve.wait_ge(s_ec, n + 1)
                        tt(ecm, ecm, cT[:, ds(r * 256 + 128 * j, 128)].rearrange("p (o l) -> p o l", o=1).to_broadcast([128, 8, 128]),
                           ALU.mult).then_inc(s_CE, 1)
                        dve.wait_ge(s_y, n + 3)
                        for f in range(4):
                            stt(y1[:, f, :], xst[:, j, f, :], dskip[:, ds(g * 4 + f, 1)],
                                PS[:, 3 * j + 2, 128 * f:128 * f + 128], ALU.mult, ALU.add).then_inc(s_y1, 1)
                        dve.wait_ge(s_cd, n + 1)
                        tt(hst, hst, wide(cd, 64), ALU.mult).then_inc(s_hm, 1)
                        dve.wait_ge(s_y1, 4 * n + 4)
                        t = hT[:, ds(g * 4, 4), ds(r * 256 + 128 * j, 128)]
                        tt(t, t, y1, ALU.mult).then_inc(s_y2, 1)
                        dve.wait_ge(s_hm, n + 1)
                        dve.wait_ge(s_st, n + 1)
                        tt(hst, hst, PS[:, 6 + j, :].rearrange("p (h d) -> p h d", d=64), ALU.add).then_inc(s_hupd, 1)

            conv(0, False)
            chunks(0)
            with dve.Fori(1, GROUPS) as g:
                conv(g, True)
                chunks(g)
            for q in range(4):
                decode_step(GROUPS - 1, q)

            def add_squares(n, k):
                with dve.Fori(0, n // 2) as r:
                    for j in range(2):
                        dve.wait_ge(s_sq, k + j + 1 + 2 * r)
                        dve.wait_ge(s_nac, k + j + 2 + 2 * r)
                        tt(nacc, nacc, nsq[:, j], ALU.add).then_inc(s_nac, 1)

            dve.wait_ge(s_d8, 18)
            nc.vector.memset(nacc, 0.0).then_inc(s_nz, 1)
            dve.wait_ge(s_nz, 1)
            add_squares(16, 0)
            for half in range(2):
                with dve.Fori(0, 8) as m:
                    t = hT[:, ds(m + 8 * half, 1), :]
                    ts(t, t, vec[:, ds(m, 1), 4 + half], None, ALU.mult).then_inc(s_hn, 1)
            dve.wait_ge(s_psfree, J_RMS + 3)
            nc.vector.reciprocal(nbc, nbc).then_inc(s_rs, 1)
            dve.wait_ge(s_rs, 1)
            with dve.Fori(0, 8) as m:
                t = gsT[:, ds(m, 1), :]
                tt(t, t, nbc.rearrange("p (o t) -> p o t", o=1), ALU.mult).then_inc(s_gr, 1)
            dve.wait_ge(s_gr, 8)
            dve.wait_ge(s_mxi, 64)
            with dve.Fori(0, 4) as r:
                for j in range(2):
                    dve.wait_ge(s_unit, U_SBR + 2 * j + 2 + 4 * r)
                    u = nsq[:, j].rearrange("p (a b) -> p a b", a=3)
                    tt(u, banks(J_SBR + j), tile(gsT, r * 2 + j), ALU.mult).then_inc(s_psfree, 1)
                    dve.wait_ge(s_psfree, J_SBR + j + 3 + 2 * r)
                    t = tile(mixT, r * 2 + j)
                    tt(t, t, u, ALU.add).then_inc(s_mix, 1)

            def residual(j0, unit, per):
                with dve.Fori(0, 4) as r:
                    for j in range(2):
                        dve.wait_ge(s_unit, unit + per * (j + 1) + 2 * per * r)
                        t = tile(res, r * 2 + j)
                        stt(t, t, ALPHA, banks(j0 + j), ALU.mult, ALU.add).then_inc(s_psfree, 1)

            def norm(n, unit, j):
                dve.wait_ge(s_unit, unit + 1)
                ts(nbc.rearrange("p (a b) -> p a b", a=3), banks(j), 1.0 / D, None, ALU.mult).then_inc(s_psfree, 1)
                nc.vector.memset(nacc, 0.0).then_inc(s_nz, 1)
                dve.wait_ge(s_psfree, j + 3)
                with dve.Fori(0, KT) as m:
                    t = res[:, ds(m, 1), :]
                    tt(t, t, nbc.rearrange("p (o t) -> p o t", o=1), ALU.subtract).then_inc(s_dm, 1)
                dve.wait_ge(s_nz, 2 + n)
                add_squares(8, 16 + 8 * n)
                dve.wait_ge(s_psfree, j + 4)
                nc.vector.reciprocal(nbc2, nbc2).then_inc(s_rs, 1)
                dve.wait_ge(s_rs, 2 + n)
                dve.sem_inc(s_pass, 1)
                with dve.Fori(0, KT) as m:
                    t = res[:, ds(m, 1), :]
                    tt(t, t, nbc2.rearrange("p (o t) -> p o t", o=1), ALU.mult).then_inc(s_yn0, 1)

            residual(J_OUT, U_OUT, 1)
            norm(0, U_LN1, J_LN1)
            dve.wait_ge(s_yn, 8)
            dve.wait_ge(s_psfree, J_DOWN + 2)
            residual(J_DOWN, U_DOWN, 4)
            norm(1, U_LN2, J_LN2)

        @block.gpsimd
        def _(pool):
            tt, ts, copy = nc.gpsimd.tensor_tensor, nc.gpsimd.tensor_scalar, nc.gpsimd.tensor_copy
            nc.gpsimd.memset(ident[:], 0.0).then_inc(s_cst0, 1)
            nc.gpsimd.memset(keep[:], 1.0).then_inc(s_cst0, 1)
            nc.gpsimd.memset(far[:], 0.0).then_inc(s_cst0, 1)
            nc.gpsimd.memset(tri[:], 1.0).then_inc(s_cst0, 1)
            pool.wait_ge(s_cst0, 4)
            for t, op, fill, step, ch in ((ident, ALU.not_equal, 1.0, -1, 1), (keep, ALU.is_gt, 0.0, -1, 1),
                                          (far, ALU.is_gt, FAR, -1, 1), (tri, ALU.is_ge, 0.0, 1, -1)):
                nc.gpsimd.affine_select(out=t[:], in_=t[:], compare_op=op, fill=fill, base=0, pattern=[[step, 128]],
                                        channel_multiplier=ch).then_inc(s_const, 1)
            pool.wait_ge(s_psfree, J_KVT + 2)
            with pool.Fori(0, NCHUNK // 2) as r:
                for j in range(2):
                    pool.wait_ge(s_psfree, J_KVT + j + 1 + 2 * r)
                    copy(kvst[:, j], kvT[:, :, ds(r * 256 + 128 * j, 128)]).then_inc(s_kst, 1)
            pool.wait_ge(s_psfree, J_ABR)
            copy(kvst[:, 0, :, 0:NDEC], kvT[:, :, SEQ:T]).then_inc(s_kst, 1)
            nc.gpsimd.memset(qbd, 0.0).then_inc(s_qz, 1)
            pool.wait_ge(s_psfree, J_ABR + 2)
            with pool.Fori(0, 2) as c:
                with pool.Fori(0, 4) as i:
                    pair = c * 4 + i
                    pool.wait_ge(s_o, pair * 8 + 2)
                    copy(qst, big[:, ds(pair, 1), 0:SEQ].rearrange("p o t -> p (o t)")).then_inc(s_qk, 1)
                    copy(kst, kvT[:, ds(c, 1), 0:SEQ].rearrange("p o t -> p (o t)")).then_inc(s_qk, 1)
                    copy(vst, kvtok[:, 0:8, ds(c * 128 + 256, 128)]).then_inc(s_qk, 1)
                    for m in range(8):
                        S = 128 * (m + 1)
                        for k in range(2):
                            pool.wait_ge(s_far, pair * 16 + (2 * m + k + 1))
                            tt(zb[:, m % 2, k, 0:S], zb[:, m % 2, k, 0:S], sbuf_s[:, k, 0:S], ALU.subtract).then_inc(s_d, 1)
            pool.wait_ge(s_qb, 32)
            for k in range(3):
                pool.wait_ge(s_pst[k], 16 * 25)
            for j in range(2):
                copy(qstd[:, j], qbd[:, j]).then_inc(s_qs, 1)
            with pool.Fori(1, NDEC // 2) as r:
                for j in range(2):
                    pool.wait_ge(s_dz, r * 16 + (8 * j - 6))
                    copy(qstd[:, j], qbd[:, ds(r * 2 + j, 1)].rearrange("p o c n -> p (o c) n")).then_inc(s_qs, 1)

            def chunks(g):
                pool.wait_ge(s_cout, g * 6 + 8)
                pool.sem_inc(s_pass, 1)
                with pool.Fori(0, NCHUNK // 2) as r:
                    for j in range(2):
                        n = g * 8 + 2 * r + j
                        pool.wait_ge(s_hupd, n + 1)
                        copy(xst[:, j], xsT[:, :, ds(r * 256 + 128 * j, 128)]).then_inc(s_stg, 1)
                        copy(bst[:, j], bT[:, ds(r * 256 + 128 * j, 128)]).then_inc(s_stg, 1)
                        pool.wait_ge(s_M, n + 1)
                        pool.wait_ge(s_bc, 2 * n + 2)
                        tt(seg, seg, cbm.rearrange("p (o l) -> p o l", o=1).to_broadcast([128, 8, 128]), ALU.mult).then_inc(s_Mm, 1)

            with pool.Fori(0, GROUPS) as g:
                chunks(g)
                wide8 = lambda v: v.rearrange("p (b o) -> p b o", o=1).to_broadcast([128, NDEC, 128])
                pool.wait_ge(s_bcr, g * 16 + 16)
                pool.sem_inc(s_pass, 1)
                for q in range(4):
                    pool.wait_ge(s_d1, g * 4 + (q + 1))
                    tt(t2, bcb[:, 0], wide8(xdd), ALU.mult).then_inc(s_d2, 1)
                    pool.wait_ge(s_d4, g * 4 + (q + 1))
                    tt(t2, h0b[:, q], bcb[:, 1], ALU.mult).then_inc(s_d5, 1)

            def sums(n, j0):
                nc.gpsimd.memset(nacc, 0.0).then_inc(s_nz2, 1)
                pool.wait_ge(s_nz2, 1 + n)
                pool.sem_inc(s_pass, 1)
                with pool.Fori(0, KT) as m:
                    pool.wait_ge(s_psfree, m + (j0 + 3))
                    pool.wait_ge(s_nsum, m + (8 * n + 2))
                    tt(nacc, nacc, res[:, ds(m, 1), :].rearrange("p o t -> p (o t)"), ALU.add).then_inc(s_nsum, 1)

            pool.wait_ge(s_mix, 8)
            sums(0, J_OUT)
            with pool.Fori(0, 32) as m:
                pool.wait_ge(s_psfree, m + (J_UP + 3))
                t = hidT[:, ds(m, 1), :]
                tt(t, t, t, ALU.mult).then_inc(s_hid, 1)
            sums(1, J_DOWN)
            pool.wait_ge(s_yn, 16)
            with pool.Fori(0, NCHUNK // 2) as r:
                for j in range(2):
                    pool.wait_ge(s_psfree, J_Y + j + 1 + 2 * r)
                    copy(yst[:, j], res[:, :, ds(r * 256 + 128 * j, 128)]).then_inc(s_ys, 1)
            pool.wait_ge(s_psfree, J_Y + 9)
            copy(yst[:, 0, :, 0:NDEC], res[:, :, SEQ:T]).then_inc(s_ys, 1)


_INS = ['x_prompt', 'x_sample', 'cache_k', 'cache_v', 'state_ssm', 'state_conv', 'page_table',
        'w_in', 'conv_w', 'conv_b', 'dt_bias', 'a_log', 'd_skip', 'ssm_norm_w', 'w_ssm_br', 'w_attn_br',
        'sb_logit_bias', 'w_out', 'ln1_g', 'ln1_b', 'w_up', 'w_down', 'ln2_g', 'ln2_b']
_OUTS = [(1, 1024, 1024), (8, 1, 1024), (1, 1, 1024, 4, 64), (1, 1, 1024, 4, 64), (1, 1, 32, 64, 128),
         (1, 1, 3, 3072), (1, 8, 1, 4, 64), (1, 8, 1, 4, 64), (1, 8, 32, 64, 128), (1, 8, 3, 3072)]


def kernel(**inputs):
    import numpy as _np
    import concourse.bacc as _bacc
    from concourse import mybir as _mybir
    from concourse.bass_utils import run_bass_kernel_spmd as _run

    nc = _bacc.Bacc("TRN2", target_bir_lowering=False, num_devices=1)
    arrays, ins, outs = {}, {}, []
    for name in _INS:
        a = _np.ascontiguousarray(inputs[name])
        arrays[f"in_{name}_dram"] = a
        ins[name] = nc.dram_tensor(f"in_{name}_dram", a.shape, _mybir.dt.from_np(a.dtype), kind="ExternalInput").ap()
    for i, shape in enumerate(_OUTS):
        outs.append(nc.dram_tensor(f"out_{i}_dram", shape, _mybir.dt.float32, kind="ExternalOutput").ap())
    build(nc, ins, outs)
    r = _run(nc, [arrays], core_ids=[0])
    return tuple(r.results[0][f"out_{i}_dram"] for i in range(len(_OUTS)))
```

```python
import concourse.bass as bass
from concourse import mybir
from contextlib import ExitStack

F32 = mybir.dt.float32
I32 = mybir.dt.int32
ACT = mybir.ActivationFunctionType
ALU = mybir.AluOpType
AX_X = mybir.AxisListType.X
ds = bass.ds

D = 1024
SEQ = 1024
NDEC = 8
T = SEQ + NDEC
TN = T // 3
KT = D // 128
D_INNER = 2048
HEADS = 32
GROUPS = 4
NSTATE = 128
CONV_DIM = D_INNER + 2 * GROUPS * NSTATE
CT = CONV_DIM // 128
CHUNK = 128
NCHUNK = SEQ // CHUNK
SB_HEADS = 16
HD = 64
KV = 4
PAGES = 16
PAST = 2048
N_POOL = 160
D_FF = 4096
COL_Z, COL_X = 0, D_INNER
COL_B = COL_X + D_INNER
COL_C = COL_B + GROUPS * NSTATE
COL_DT = COL_C + GROUPS * NSTATE
COL_Q = COL_DT + HEADS
COL_K = COL_Q + SB_HEADS * HD
COL_V = COL_K + KV * HD
COL_GS = COL_V + KV * HD
COL_GA = COL_GS + D
SCALE = HD ** -0.5
ALPHA = 2.0 ** 0.25
EPS = 1e-5
DT_CUM = 13
FAR = 1e30
RAWLEN = 3 + SEQ + 4 * NDEC
ACCLEN = RAWLEN - 3
DEC0 = SEQ + 3
NPAR = 5 + 3 * NDEC

J_X = 0
J_PAR = J_X + NCHUNK + 1
J_QKV = J_PAR + 2
J_KVT = J_QKV + 12
J_DT = J_KVT + 9
J_ABR = J_DT + 2
J_SSD = J_ABR + 8
J_GS = J_SSD + 6 * GROUPS
J_RMS = J_GS + 8
J_SBR = J_RMS + 1
J_OUT = J_SBR + 8
J_LN1 = J_OUT + 8
J_UP = J_LN1 + 2
J_DOWN = J_UP + 32
J_LN2 = J_DOWN + 8
J_TAIL = J_LN2 + 2
J_Y = J_TAIL + 2
J_END = J_Y + 9
U_SBR = J_SBR
U_OUT = U_SBR + 16
U_LN1 = U_OUT + 8
U_UP = U_LN1 + 2
U_DOWN = U_UP + 32
U_LN2 = U_DOWN + 32
U_TAIL = U_LN2 + 2
U_Y = U_TAIL + 2
P_QKV = 0
P_DT = P_QKV + 12
P_SSD = P_DT + 1
P_ABR = P_SSD
P_GS = P_SSD + 6 * GROUPS
P_SBR = P_GS + 8
P_OUT = P_SBR + 16
P_UP = P_OUT + 8
P_DOWN = P_UP + 32


def build(nc, ins, outs):
    y_prompt, y_sample, k_prompt, v_prompt, ssm_prompt, conv_prompt, k_sample, v_sample, ssm_sample, conv_sample = outs
    w_in = ins["w_in"][0].rearrange("(t p) n -> p t n", p=128)
    w_ssm = ins["w_ssm_br"][0].rearrange("(t p) n -> p t n", p=128)
    w_out = ins["w_out"][0].rearrange("(t p) n -> p t n", p=128)
    w_up = ins["w_up"][0].rearrange("(t p) n -> p t n", p=128)
    w_down = ins["w_down"][0].rearrange("(t p) n -> p t n", p=128)
    w_att = ins["w_attn_br"][0].rearrange("(c k i d) n -> k d c i n", c=2, k=2, i=4)
    scr_cum = nc.dram_tensor("scr_cum", [HEADS, SEQ], F32, kind="Internal").ap()
    scr_dec = nc.dram_tensor("scr_dec", [2, HEADS, NDEC], F32, kind="Internal").ap()
    scr_z = nc.dram_tensor("scr_z", [24, 128, T], F32, kind="Internal").ap()
    scr_mix = nc.dram_tensor("scr_mix", [8, 128, T], F32, kind="Internal").ap()
    scr_bc = nc.dram_tensor("scr_bc", [GROUPS, 2, NDEC, NSTATE], F32, kind="Internal").ap()

    with ExitStack() as ctx:
        def sb(name, shape, dt=F32):
            return ctx.enter_context(nc.sbuf_tensor(name, shape, dt))

        def sem(name):
            return ctx.enter_context(nc.semaphore(name))

        res = sb("res", [128, KT, T])
        big = sb("big", [128, 32, T])
        wbuf = sb("wbuf", [128, 2, 8, 128])
        work = sb("work", [128, 7168])
        ident = sb("ident", [128, 128])
        ones = sb("ones", [128, 128])
        keep = sb("keep", [128, 128])
        far = sb("far", [128, 128])
        tri = sb("tri", [128, 128])
        par = sb("par", [128, CT, NPAR])
        vec = sb("vec", [128, KT, 6])
        tail = sb("tail", [128, CT, 3 + NDEC])
        cumtok = sb("cumtok", [128, NCHUNK, HEADS])
        dttok = sb("dttok", [128, NCHUNK, HEADS])
        dtx = sb("dtx", [128, 2, 16, NDEC])
        dskip = sb("dskip", [128, 16])
        sbb = sb("sbb", [128, SB_HEADS])
        sbd = sb("sbd", [128, 1])
        dtb = sb("dtb", [HEADS, 1])
        alog = sb("alog", [HEADS, 1])
        pages = sb("pages", [1, NDEC * PAGES], I32)
        eps = sb("eps", [128, 1])
        small = sb("small", [128, 64])
        PS = ctx.enter_context(nc.psum_tensor("PS", [128, 8, 512], F32))

        flat = big[:, :, :].rearrange("p t n -> p (t n)")

        def carve(base, *shape):
            n = 1
            for s in shape:
                n *= s
            return base[:, 0:n] if len(shape) == 1 else base[:, 0:n].rearrange(
                {2: "p (a b) -> p a b", 3: "p (a b c) -> p a b c"}[len(shape)],
                **dict(zip("abc", shape)))

        def area(off, *shape):
            return carve(flat[:, off:], *shape)

        def wk(off, *shape):
            return carve(work[:, off:], *shape)

        qT = big[:, 0:8, :]
        kvT = big[:, 24:28, :]
        mixT = big[:, 16:24, :]
        hT = big[:, 0:16, :]
        xsT = big[:, 24:28, :]
        bT = big[:, 28, :]
        cT = big[:, 29, :]
        gsT = big[:, 24:32, :]
        hidT = big
        xbuf = area(24 * T, 2, 1024)
        xsam = area(26 * T + 512, 1024)
        prow = area(8 * T, CONV_DIM)
        vrow = area(11 * T + 64, 1024)
        kvtok = area(8 * T, 9, 512)
        o = 8 * T + 9 * 512
        qst = area(o, 1024)
        vst = [area(o + 1024 * (c + 1), 8, 128) for c in range(2)]
        zb = wk(0, 2, 2, 1024)
        sbuf_s = wk(4096, 2, 1024)
        lb = area(o + 3072, 2, 2, 1024)
        wTb = area(o + 7168, 2, 16, 128)
        pbuf = area(8 * T, 2, PAGES, 256)
        o = 8 * T + 2 * PAGES * 256
        zd = area(o, PAST)
        ld = area(o + PAST, PAST)
        sd = area(o + 2 * PAST, PAST)
        wTd = area(o + 3 * PAST, PAGES, 128)
        kTst = area(28 * T, 2, 512)
        qbd = area(28 * T + 1032, NDEC, 2, 128)
        qstd = area(28 * T + 3080, 2, 2, 128)
        pst = area(28 * T + 3080, 3, TN)
        w3 = wk(6144, 8, 128)
        raw = wk(0, RAWLEN)
        acc = wk(RAWLEN + 1, ACCLEN)
        sig = wk(RAWLEN + 1 + ACCLEN, ACCLEN)
        cumb = wk(0, 2, 8, 128)
        seg = wk(2048, 2, 8, 128)
        xdt = [wk(4096, 8, 64), area(16 * T + 7168, 8, 64)]
        xdte = [wk(4608, 8, 64), area(16 * T + 7680, 8, 64)]
        hst = wk(5120, 8, 64)
        btok = [wk(5632, 128), wk(6912, 128)]
        cbm = [wk(5760, 128), wk(7040, 128)]
        y1 = wk(5888, 4, 128)
        hout = wk(6400, 4, 128)
        xst = area(30 * T, 2, 4, 128)
        bst = area(30 * T + 1024, 2, 128)
        t8, dte, cd = [[small[:, 16 * n + 8 * j:16 * n + 8 * j + 8] for j in range(2)] for n in range(3)]
        xdd = small[:, 48:56]
        yd = small[:, 56:64]
        zsg = wk(3176, T)
        h0b = carve(flat[:, 16 * T:], 4 * NDEC, 128).rearrange("p (q b) n -> p q b n", q=4)
        t2 = area(16 * T + 4096, NDEC, 128)
        bcb = area(16 * T + 5120, 2, NDEC, 128)
        dtr, dte1, dtu, dtl, dtv = [work[0:HEADS, 1040 * n:1040 * n + T] for n in range(5)]
        chm = work[0:HEADS, 5200:5200 + SEQ]
        nacc = wk(0, T)
        nsq = wk(1032, 2, T)
        nbc = wk(3096, T)
        nbc2 = wk(4128, T)
        ytok = area(0, 2, 1024)
        tailrow = area(8 * T, CONV_DIM)

        s_pass = sem("s_pass")
        s_const = sem("s_const")
        s_par = sem("s_par")
        s_small = sem("s_small")
        s_xin = [sem("s_xin0"), sem("s_xin1")]
        s_w = [sem("s_w0"), sem("s_w1")]
        s_unit = sem("s_unit")
        s_psfree = sem("s_psfree")

        block = ctx.enter_context(nc.Block())

        def banks(j, n=3, w=TN):
            return PS[:, 3 * (j % 2):3 * (j % 2) + n, 0:w]

        def tile(t, m):
            return t[:, ds(m, 1), :].rearrange("p o (a b) -> p (o a) b", b=TN)

        s_kvo = sem("s_kvo")
        s_qst = sem("s_qst")
        s_vst = sem("s_vst")
        s_z = sem("s_z")
        s_ab = sem("s_ab")
        s_ex = sem("s_ex")
        s_ln = sem("s_ln")
        s_sp = sem("s_sp")
        s_spm = sem("s_spm")
        s_scan = sem("s_scan")
        s_far = sem("s_far")
        s_d = sem("s_d")
        s_wt = sem("s_wt")
        s_tr = sem("s_tr")
        s_cp = sem("s_cp")
        s_o = sem("s_o")
        s_oc = sem("s_oc")
        s_w3 = [sem("s_w3_0"), sem("s_w3_1"), sem("s_w3_2")]
        s_p3 = sem("s_p3")
        s_pc = sem("s_pc")
        s_pst = [sem("s_pst0"), sem("s_pst1"), sem("s_pst2")]
        s_ga = [sem("s_ga0"), sem("s_ga1"), sem("s_ga2"), sem("s_ga3")]
        s_gas = sem("s_gas")
        s_zl = [sem("s_zl0"), sem("s_zl1"), sem("s_zl2"), sem("s_zl3")]
        s_zm = sem("s_zm")
        s_pt = sem("s_pt")
        s_kp = [sem("s_kp0"), sem("s_kp1")]
        s_wa = [sem("s_wa0"), sem("s_wa1")]
        s_dact = sem("s_dact")
        s_dd = sem("s_dd")
        s_dexp = sem("s_dexp")
        s_tok = sem("s_tok")
        s_nz = sem("s_nz")
        s_nz2 = sem("s_nz2")
        s_cst0 = sem("s_cst0")
        s_yn0 = sem("s_yn0")
        s_rz = sem("s_rz")
        s_yout = [sem("s_yout0"), sem("s_yout1")]
        s_nsum = sem("s_nsum")
        s_dm = sem("s_dm")
        s_rs = sem("s_rs")
        s_yn = sem("s_yn")
        s_qz = sem("s_qz")
        s_qb = sem("s_qb")
        s_qs = sem("s_qs")
        s_dtr = sem("s_dtr")
        s_dcp = sem("s_dcp")
        s_dz = sem("s_dz")
        s_dtw = sem("s_dtw")
        s_dcw = sem("s_dcw")
        s_do = sem("s_do")
        s_doc = sem("s_doc")
        s_dt = sem("s_dt")
        s_dta = sem("s_dta")
        s_scr = sem("s_scr")
        s_dtx = sem("s_dtx")
        s_dtxe = sem("s_dtxe")
        s_zsg = sem("s_zsg")
        s_raw = sem("s_raw")
        s_cv = sem("s_cv")
        s_csg = sem("s_csg")
        s_cout = sem("s_cout")
        s_cb = [sem("s_cb0"), sem("s_cb1")]
        s_stg = sem("s_stg")
        s_tp = sem("s_tp")
        s_bc = sem("s_bc")
        s_t8 = sem("s_t8")
        s_t8e = sem("s_t8e")
        s_dte = sem("s_dte")
        s_cd = sem("s_cd")
        s_xdt = sem("s_xdt")
        s_sg = sem("s_sg")
        s_sg2 = sem("s_sg2")
        s_M = sem("s_M")
        s_Mm = sem("s_Mm")
        s_ec = sem("s_ec")
        s_CE = sem("s_CE")
        s_y = sem("s_y")
        s_st = sem("s_st")
        s_y1 = sem("s_y1")
        s_hm = sem("s_hm")
        s_hs = sem("s_hs")
        s_hupd = sem("s_hupd")
        s_h0 = sem("s_h0")
        s_ht = sem("s_ht")
        s_hc = sem("s_hc")
        s_ho = sem("s_ho")
        s_bcw = sem("s_bcw")
        s_bcr = sem("s_bcr")
        s_dh = sem("s_dh")
        s_mxo = sem("s_mxo")
        s_mxi = sem("s_mxi")
        s_d1 = sem("s_d1")
        s_d2 = sem("s_d2")
        s_d3 = sem("s_d3")
        s_d4 = sem("s_d4")
        s_d5 = sem("s_d5")
        s_d6 = sem("s_d6")
        s_d7 = sem("s_d7")
        s_d8 = sem("s_d8")
        s_dso = sem("s_dso")
        s_sq = sem("s_sq")
        s_nac = sem("s_nac")
        s_hn = sem("s_hn")
        s_gr = sem("s_gr")
        s_mix = sem("s_mix")
        s_hid = sem("s_hid")
        s_yo = sem("s_yo")
        s_out = sem("s_out")

        def turns(qb):
            return [(k, kb, min(4, qb + 1 - kb)) for k in range(2) for kb in range(0, qb + 1, 4)]

        def turned(qb):
            return sum(len(turns(x)) for x in range(qb))

        def load_pages(eng, cache, r, j, half):
            with eng.Fori(0, PAGES // 8) as i:
                for n in range(4):
                    m = i * 4 + (n + half * PAGES // 2)
                    page = eng.value_load(pages[0:1, ds(r * 2 * PAGES + i * 4 + (n + half * PAGES // 2 + j * PAGES), 1)],
                                          min_val=0, max_val=N_POOL - 1)
                    eng.dma_start(pbuf[:, j, ds(m, 1), :],
                                  ins[cache][0, ds(page, 1)].rearrange("o t g d -> t o (g d)")).then_inc(s_kp[j], 16)

        @block.sync
        def _(sp):
            def load(slot, lo, src_lo, hi, src_hi, unit):
                sp.wait_ge(s_unit, unit - 1)
                sp.dma_start(lo, src_lo).then_inc(s_w[slot], 16)
                sp.dma_start(hi, src_hi).then_inc(s_w[slot], 16)

            def load_cols(P, unit, w, k0, col, n=128):
                b = wbuf[:, P % 2]
                load(P % 2, b[:, 0:4, 0:n], w[:, k0:k0 + 4, ds(col, n)], b[:, 4:8, 0:n], w[:, k0 + 4:k0 + 8, ds(col, n)],
                     unit)

            sp.dma_start(prow[0:4, :], ins["conv_w"][0]).then_inc(s_par, 16)
            sp.dma_start(prow[4:5, :], ins["conv_b"]).then_inc(s_par, 16)
            sp.dma_start(prow[5:NPAR, :], ins["state_conv"][0].rearrange("b k c -> (b k) c")).then_inc(s_par, 16)
            for n, name in enumerate(("ln1_g", "ln1_b", "ln2_g", "ln2_b")):
                sp.dma_start(vrow[n:n + 1, :], ins[name]).then_inc(s_par, 16)
            sp.dma_start(vrow[4:6, :], ins["ssm_norm_w"].rearrange("o (a d) -> (o a) d", a=2)).then_inc(s_par, 16)
            for n in range(2):
                sp.dma_start(xbuf[:, n, :], ins["x_prompt"][0, n * 128:(n + 1) * 128, :]).then_inc(s_xin[n], 16)
            sp.dma_start(xsam[0:NDEC, :], ins["x_sample"].rearrange("b o d -> (b o) d")).then_inc(s_small, 16)
            with nc.allow_non_contiguous_dma("small parameters"):
                for k in range(2):
                    src = ins["d_skip"].rearrange("o (j k) -> o k j", k=2)[:, k, :]
                    sp.dma_start(dskip[64 * k:64 * k + 64, :], src.to_broadcast([64, 16])).then_inc(s_small, 16)
                sp.dma_start(sbb[:], ins["sb_logit_bias"].to_broadcast([128, SB_HEADS])).then_inc(s_small, 16)
                for b in range(NDEC):
                    sp.dma_start(sbd[16 * b:16 * b + 16, :], ins["sb_logit_bias"].rearrange("o h -> h o")).then_inc(s_small, 16)
                sp.dma_start(dtb[:], ins["dt_bias"].rearrange("o h -> h o")).then_inc(s_small, 16)
                sp.dma_start(alog[:], ins["a_log"].rearrange("o h -> h o")).then_inc(s_small, 16)
            sp.dma_start(pages[:], ins["page_table"].rearrange("b n -> (b n)").rearrange("(o n) -> o n", o=1)).then_inc(s_pt, 16)
            with sp.Fori(1, NCHUNK // 2) as r:
                for j in range(2):
                    sp.wait_ge(s_unit, 2 * r + j - 1)
                    sp.dma_start(xbuf[:, j, :], ins["x_prompt"][0, ds(r * 256 + j * 128, 128), :]).then_inc(s_xin[j], 16)

            for c in range(2):
                with sp.Fori(0, 2) as r:
                    for j in range(2):
                        n = 4 * c + j
                        cols = [COL_Q + 512 * c + 256 * k + 64 * j for k in range(2)]
                        b = wbuf[:, n % 2]
                        load(n % 2, b[:, :, 0:64], w_in[:, :, ds(r * 128 + cols[0], 64)],
                             b[:, :, 64:128], w_in[:, :, ds(r * 128 + cols[1], 64)], J_QKV + n + 2 * r)
            with sp.Fori(0, 2) as r:
                for j in range(2):
                    load_cols(P_QKV + 8 + j, J_QKV + 8 + j + 2 * r, w_in, 0, r * 256 + (COL_K + 128 * j))

            sp.wait_ge(s_psfree, J_DT + 2)
            for t, po, so in ((0, k_prompt, k_sample), (256, v_prompt, v_sample)):
                sp.dma_start(po[0, 0].rearrange("(t p) g d -> p t (g d)", p=128), kvtok[:, 0:8, t:t + 256]).then_inc(s_kvo, 16)
                sp.dma_start(so[0].rearrange("b o g d -> (b o) (g d)"), kvtok[0:NDEC, 8, t:t + 256]).then_inc(s_kvo, 16)

            w3bufs = (wbuf[:, 0], wbuf[:, 1], w3)

            def load3(t, col):
                sp.dma_start(w3bufs[t][:, 0:4], w_in[:, 0:4, ds(col, 128)]).then_inc(s_w3[t], 16)
                sp.dma_start(w3bufs[t][:, 4:8], w_in[:, 4:8, ds(col, 128)]).then_inc(s_w3[t], 16)

            def thirds(pair, cols):
                for m in range(9):
                    t, th = m // 3, m % 3
                    sp.wait_ge(s_pc, pair * 9 + (m + 2))
                    sp.dma_start(scr_z[ds(pair * 3 + t, 1), :, th * TN:th * TN + TN].rearrange("o p n -> p (o n)"),
                                 pst[:, th, :]).then_inc(s_pst[th], 16)
                    if th == 2 and cols:
                        load3(t, cols[t])

            sp.wait_ge(s_unit, J_KVT)
            for t in range(3):
                load3(t, 128 * t)
            with sp.Fori(0, 4) as pair:
                thirds(pair, [pair * 384 + 128 * (3 + t) for t in range(3)])
            thirds(4, [COL_Z + 128 * 15, COL_GA, COL_GA + 128])
            with sp.Fori(5, 7) as pair:
                thirds(pair, [pair * 384 + (COL_GA + 128 * (2 + t - 15)) for t in range(3)])
            thirds(7, None)

            load_cols(P_DT, J_DT, w_in, 0, COL_DT, HEADS)

            sp.wait_ge(s_pt, 16)
            sp.wait_ge(s_kvo, 64)
            sp.wait_ge(s_oc, 66)
            for j in range(2):
                load_pages(sp, "cache_k", 0, j, 0)
            with sp.Fori(1, NDEC // 2) as r:
                for j in range(2):
                    sp.wait_ge(s_dtr, 16 * r + 8 * (j - 1))
                    sp.sem_inc(s_pass, 1)
                    load_pages(sp, "cache_k", r, j, 0)
            for j in range(2):
                sp.wait_ge(s_dtr, 56 + 8 * j)
                load_pages(sp, "cache_v", 0, j, 0)
            with sp.Fori(1, NDEC // 2) as r:
                for j in range(2):
                    sp.wait_ge(s_do, 2 * r + j - 1)
                    sp.sem_inc(s_pass, 1)
                    load_pages(sp, "cache_v", r, j, 0)

            sp.wait_ge(s_dt, DT_CUM)
            sp.dma_start(scr_cum, dtv[:, 0:SEQ]).then_inc(s_scr, 16)
            sp.dma_start(scr_dec[0], dtl[:, SEQ:T]).then_inc(s_scr, 16)
            sp.dma_start(scr_dec[1], dtr[:, SEQ:T]).then_inc(s_scr, 16)
            sp.wait_ge(s_scr, 48)
            for n in range(2):
                for k in range(2):
                    src = scr_dec[n].rearrange("(j k) b -> k j b", k=2)[k:k + 1]
                    sp.dma_start(dtx[64 * k:64 * k + 64, n], src.to_broadcast([64, 16, NDEC])).then_inc(s_dtx, 16)

            def load_branch(r, j):
                b = wbuf[:, (P_ABR + j) % 2]
                sp.wait_ge(s_unit, J_ABR + j - 1 + 2 * r)
                for k in range(2):
                    for c in range(2):
                        sp.dma_start(b[64 * k:64 * k + 64, 4 * c:4 * c + 4, :],
                                     w_att[k, :, c, :, ds(r * 256 + 128 * j, 128)]).then_inc(s_wa[(P_ABR + j) % 2], 16)

            for j in range(2):
                load_branch(0, j)
            for k in range(3):
                sp.wait_ge(s_pst[k], 16 * 25)
            sp.wait_ge(s_doc, NDEC + 2)
            for n in range(4):
                sp.dma_start(mixT[:, 2 * n:2 * n + 2, :], scr_z[16 + 2 * n:18 + 2 * n].rearrange("t p n -> p t n")).then_inc(s_ga[n], 16)
            with sp.Fori(1, 4) as r:
                for j in range(2):
                    load_branch(r, j)

            def load_z(n):
                sp.dma_start(hT[:, 4 * n:4 * n + 4, :], scr_z[4 * n:4 * n + 4].rearrange("t p n -> p t n")).then_inc(s_zl[n], 16)

            load_z(2)
            load_z(3)
            for n in range(2):
                load_cols(P_SSD + n, J_SSD + n, w_in, 0, COL_X + 128 * n)
            sp.wait_ge(s_unit, J_SSD)
            load_z(0)
            load_z(1)
            sp.wait_ge(s_psfree, J_SSD + 2)
            for n in range(4):
                sp.dma_start(scr_mix[2 * n:2 * n + 2].rearrange("t p n -> p t n"), mixT[:, 2 * n:2 * n + 2, :]).then_inc(s_mxo, 16)

            def group(g, last):
                for n in (2, 3):
                    load_cols(P_SSD + n, J_SSD + n + 6 * g, w_in, 0, g * 512 + (COL_X + 128 * n))
                load_cols(P_SSD + 4, J_SSD + 4 + 6 * g, w_in, 0, g * 128 + COL_B)
                load_cols(P_SSD + 5, J_SSD + 5 + 6 * g, w_in, 0, g * 128 + COL_C)
                sp.wait_ge(s_cout, 6 * g + 8)
                sp.sem_inc(s_pass, 1)
                with sp.Fori(0, NCHUNK // 2) as r:
                    for j in range(2):
                        sp.wait_ge(s_hupd, g * 8 + 2 * r + (j + 1))
                        src = scr_cum[ds(g * 8, 8), ds(r * 256 + j * 128, 128)]
                        sp.dma_start(cumb[:, j], src.rearrange("(o h) l -> o h l", o=1).to_broadcast([128, 8, 128])).then_inc(s_cb[j], 16)
                sp.wait_ge(s_dso, g * 64 + 16)
                sp.wait_ge(s_d8, g * 4 + 2)
                sp.wait_ge(s_mxo, 64)
                for q in range(4):
                    src = ins["state_ssm"][0].rearrange("b h p n -> (h p) b n")[ds(g * 512 + q * 128, 128)]
                    sp.dma_start(h0b[:, q], src).then_inc(s_dh, 16)
                with nc.allow_non_contiguous_dma("B, C of the decode tokens, token-major"):
                    for n, t in enumerate((bT, cT)):
                        sp.dma_start(scr_bc[ds(g, 1), n].rearrange("o b s -> s (o b)"), t[:, SEQ:T]).then_inc(s_bcw, 16)
                sp.wait_ge(s_bcw, 32 * g + 32)
                sp.sem_inc(s_pass, 1)
                sp.dma_start(bcb[:], scr_bc[ds(g, 1)].to_broadcast([128, 2, NDEC, NSTATE])).then_inc(s_bcr, 16)
                for n in range(2):
                    if last:
                        load_cols(P_GS + n, J_GS + n, w_in, 0, COL_GS + 128 * n)
                    else:
                        load_cols(P_SSD + 6 + n, J_SSD + 6 + n + 6 * g, w_in, 0, g * 512 + (COL_X + 512 + 128 * n))
                sp.wait_ge(s_hc, g + 3)
                sp.dma_start(ssm_prompt[0, 0].rearrange("h p n -> (h p) n")[ds(g * 512, 512), :].rearrange("(j q) n -> q j n", q=128),
                             hout[:]).then_inc(s_ho, 16)

            with sp.Fori(0, GROUPS - 1) as g:
                group(g, False)
            group(GROUPS - 1, True)

            with sp.Fori(1, 4) as r:
                for j in range(2):
                    load_cols(P_GS + j, J_GS + j + 2 * r, w_in, 0, r * 256 + (COL_GS + 128 * j))
            sp.wait_ge(s_dso, 64 * GROUPS + 16)
            sp.wait_ge(s_d8, 18)
            for n in range(4):
                sp.dma_start(mixT[:, 2 * n:2 * n + 2, :], scr_mix[2 * n:2 * n + 2].rearrange("t p n -> p t n")).then_inc(s_mxi, 16)
            with sp.Fori(0, 4) as r:
                for j in range(2):
                    for kp in range(2):
                        n = 2 * j + kp
                        load_cols(P_SBR + n, U_SBR + n + 4 * r, w_ssm, 8 * kp, r * 256 + 128 * j)
            with sp.Fori(0, 4) as r:
                for j in range(2):
                    load_cols(P_OUT + j, U_OUT + j + 2 * r, w_out, 0, r * 256 + 128 * j)
            with sp.Fori(0, 16) as r:
                for j in range(2):
                    load_cols(P_UP + j, U_UP + j + 2 * r, w_up, 0, r * 256 + 128 * j)
            with sp.Fori(0, 4) as r:
                for j in range(2):
                    for kp in range(4):
                        n = 4 * j + kp
                        load_cols(P_DOWN + n, U_DOWN + n + 8 * r, w_down, 8 * kp, r * 256 + 128 * j)

            sp.wait_ge(s_psfree, J_Y + 2)
            sp.dma_start(conv_prompt[0, 0], tailrow[0:3, :]).then_inc(s_out, 16)
            sp.dma_start(conv_sample[0, :, 2, :], tailrow[3:3 + NDEC, :]).then_inc(s_out, 16)
            sp.dma_start(conv_sample[0, :, 0:2, :], ins["state_conv"][0, :, 1:3, :]).then_inc(s_out, 16)
            with sp.Fori(0, NCHUNK // 2) as r:
                for j in range(2):
                    sp.wait_ge(s_psfree, J_Y + j + 3 + 2 * r)
                    sp.dma_start(y_prompt[0, ds(r * 256 + 128 * j, 128), :], ytok[:, j, :]).then_inc(s_yout[j], 16)
            sp.wait_ge(s_psfree, J_END + 2)
            sp.dma_start(y_sample.rearrange("b o d -> (b o) d"), ytok[0:NDEC, 0, :]).then_inc(s_yo, 16)
            sp.wait_ge(s_yout[0], 80)
            sp.wait_ge(s_yout[1], 80)
            sp.wait_ge(s_yo, 16)
            sp.wait_ge(s_out, 48)
            sp.wait_ge(s_kvo, 64)
            sp.wait_ge(s_ho, 80)
            sp.wait_ge(s_dso, 64 * GROUPS + 16)

        @block.tensor
        def _(pe):
            def product(j, joff, unit, p, off, kpieces, x, m=128, wa=False):
                pe.wait_ge(s_psfree, j + 1 + joff)
                for kp in range(kpieces):
                    slot = (p + kp) % 2
                    if wa:
                        pe.wait_ge(s_wa[slot], 64 * ((p + kp - P_ABR) // 2 + 1) + 32 * off)
                    else:
                        pe.wait_ge(s_w[slot], 32 * ((p + kp) // 2 + 1) + 16 * off)
                    for n in range(3):
                        for k in range(8):
                            mm = nc.tensor.matmul(PS[0:m, 3 * (j % 2) + n, 0:TN], wbuf[:, slot, k, 0:m],
                                                  x[:, 8 * kp + k, n * TN:(n + 1) * TN],
                                                  start=(kp == 0 and k == 0), stop=(kp == kpieces - 1 and k == 7))
                    mm.then_inc(s_unit, 1)

            def turn(bank, col, src, part=128):
                n = src.shape[1]
                return nc.tensor.transpose(PS[0:n, bank, col:col + part], src, ident[0:part, 0:part])

            pe.wait_ge(s_const, 5)
            with pe.Fori(0, NCHUNK // 2) as r:
                for j in range(2):
                    pe.wait_ge(s_xin[j], 16 * r + 16)
                    pe.wait_ge(s_psfree, J_X + j + 1 + 2 * r)
                    for f in range(KT):
                        mm = turn(3 * ((J_X + j) % 2) + f // 4, 128 * (f % 4), xbuf[:, j, 128 * f:128 * f + 128])
                    mm.then_inc(s_unit, 1)
            pe.wait_ge(s_small, 16 * 14)
            pe.wait_ge(s_psfree, J_PAR)
            for f in range(KT):
                mm = turn(3 * ((J_X + 8) % 2), NDEC * f, xsam[0:NDEC, 128 * f:128 * f + 128], NDEC)
            mm.then_inc(s_unit, 1)
            pe.wait_ge(s_par, 16 * 8)
            pe.wait_ge(s_psfree, J_PAR + 1)
            for t in range(CT):
                mm = turn(3 * (J_PAR % 2) + t // 12, NPAR * (t % 12), prow[0:NPAR, 128 * t:128 * t + 128], NPAR)
            mm.then_inc(s_unit, 1)
            pe.wait_ge(s_psfree, J_PAR + 2)
            for f in range(KT):
                mm = turn(3 * ((J_PAR + 1) % 2), 6 * f, vrow[0:6, 128 * f:128 * f + 128], 6)
            mm.then_inc(s_unit, 1)

            pe.wait_ge(s_psfree, J_PAR + 2)
            with pe.Fori(0, 6) as r:
                for j in range(2):
                    product(J_QKV + j, 2 * r, J_QKV + j, P_QKV + j, 2 * r, 1, res)

            pe.wait_ge(s_psfree, J_KVT + 2)
            for c in range(NCHUNK + 1):
                n = 128 if c < NCHUNK else NDEC
                pe.wait_ge(s_psfree, J_KVT + c + 1)
                for f in range(4):
                    mm = turn(3 * ((J_KVT + c) % 2), 128 * f, kvT[:, f, 128 * c:128 * c + n])
                mm.then_inc(s_unit, 1)

            pe.wait_ge(s_psfree, J_DT + 2)
            def attend(pair, m, c):
                pe.wait_ge(s_cp, pair * 24 + (turned(m + 1) + 2))
                pe.wait_ge(s_oc, pair * 8 + (m + 1))
                for k in range(2):
                    for kb in range(m + 1):
                        mm = nc.tensor.matmul(PS[64 * k:64 * k + 64, 6, 128 * (m % 2):128 * (m % 2) + 128],
                                              vst[c][:, kb, 64 * k:64 * k + 64], wTb[:, m % 2, 8 * k + kb, :],
                                              start=(kb == 0), stop=(kb == m))
                mm.then_inc(s_o, 1)

            def turn_weights(pair, m):
                pe.wait_ge(s_wt, pair * 8 + (m + 1))
                for n, (k, kb0, nb) in enumerate(turns(m)):
                    pe.wait_ge(s_cp, pair * 24 + (turned(m) + n + 1))
                    for x in range(nb):
                        kb = kb0 + x
                        mm = turn(4 + n % 2, 128 * x, zb[:, m % 2, k, 128 * kb:128 * kb + 128])
                    mm.then_inc(s_tr, 1)

            def third(pair, m):
                t, th = m // 3, m % 3
                if th == 0:
                    pe.wait_ge(s_w3[t], pair * 32 + 32)
                pe.wait_ge(s_pc, pair * 9 + (m + 1))
                for k in range(8):
                    mm = nc.tensor.matmul(PS[:, 7, 0:TN], (wbuf[:, 0], wbuf[:, 1], w3)[t][:, k, :],
                                          res[:, k, th * TN:th * TN + TN], start=(k == 0), stop=(k == 7))
                mm.then_inc(s_p3, 1)

            def steps(pair, c, first=False, c_before=None):
                for m in range(8):
                    pe.wait_ge(s_qst, pair * 8 + (m + 1))
                    pe.wait_ge(s_ab, pair * 8 + (m + 1))
                    for k in range(2):
                        for s0 in range(0, 128 * (m + 1), 512):
                            w = min(512, 128 * (m + 1) - s0)
                            mm = nc.tensor.matmul(PS[:, 2 * k + s0 // 512, 0:w],
                                                  qst[64 * k:64 * k + 64, 128 * m:128 * m + 128],
                                                  kvT[64 * k:64 * k + 64, c, s0:s0 + w], start=True, stop=True)
                    mm.then_inc(s_z, 1)
                    if m >= 2:
                        attend(pair, m - 2, c)
                    elif not first:
                        attend(pair - 1, m + 6, c if c_before is None else c_before)
                    third(pair, m)
                    if m >= 1:
                        turn_weights(pair, m - 1)
                    elif not first:
                        turn_weights(pair - 1, 7)
                third(pair, 8)

            pe.wait_ge(s_vst, 2)
            steps(0, 0, first=True)
            with pe.Fori(1, 4) as pair:
                steps(pair, 0)
            steps(4, 1, c_before=0)
            with pe.Fori(5, 8) as pair:
                steps(pair, 1)
            attend(7, 6, 1)
            turn_weights(7, 7)
            attend(7, 7, 1)

            def decode_keys(b, j, first, last):
                pe.wait_ge(s_kp[j], 16 * PAGES + 8 * PAGES * (b - j))
                pe.wait_ge(s_qs, b + 1)
                for q in range(9):
                    if q < 8:
                        c, jb = q // 4, q % 4
                        pe.wait_ge(s_dcp, b * 8 + (q + 1))
                        for n in range(4):
                            mm = turn(4 + q % 2, 128 * n, pbuf[:, j, 4 * jb + n, 128 * c:128 * c + 128])
                        mm.then_inc(s_dtr, 1)
                    if q >= 1:
                        c, jb = (q - 1) // 4, (q - 1) % 4
                        pe.wait_ge(s_dcp, b * 8 + (q + 2))
                        nc.tensor.matmul(PS[:, jb, :], qstd[:, j, c, :], kTst[:, (q - 1) % 2, :],
                                         start=(first and c == 0), stop=(last and c == 1)).then_inc(s_dz, 1)

            pe.wait_ge(s_oc, 66)
            decode_keys(0, 0, True, False)
            decode_keys(1, 1, False, False)
            with pe.Fori(1, 3) as r:
                for j in range(2):
                    decode_keys(r * 2 + j, j, False, False)
            decode_keys(6, 0, False, False)
            decode_keys(7, 1, False, True)
            pe.wait_ge(s_dact, 2)
            product(J_DT, 0, J_DT, P_DT, 0, 1, res, m=HEADS)
            pe.wait_ge(s_dexp, 1)
            pe.wait_ge(s_pc, 73)
            for n in range(PAGES):
                mm = turn(4 + n // 4, 128 * (n % 4), zd[:, 128 * n:128 * n + 128])
            mm.then_inc(s_dtw, 1)
            pe.wait_ge(s_dcw, 1)
            with pe.Fori(0, NDEC // 2) as r:
                for j in range(2):
                    pe.wait_ge(s_kp[j], 16 * PAGES * 5 + 16 * PAGES * r)
                    pe.wait_ge(s_doc, j + 1 + 2 * r)
                    for c in range(2):
                        for n in range(PAGES):
                            mm = nc.tensor.matmul(PS[:, 4 + j, 8 * c:8 * c + 8], pbuf[:, j, n, 128 * c:128 * c + 128],
                                                  wTd[:, n, ds(r * 32 + (16 * j + 8 * c), 8)],
                                                  start=(n == 0), stop=(n == PAGES - 1))
                    mm.then_inc(s_do, 1)

            pe.wait_ge(s_dt, DT_CUM)
            pe.wait_ge(s_psfree, J_DT + 2)
            for n in range(NCHUNK):
                turn(3 * ((J_DT + 1) % 2), 32 * n, dtv[:, 128 * n:128 * n + 128], HEADS)
                mm = turn(3 * ((J_DT + 1) % 2), 256 + 32 * n, dtr[:, 128 * n:128 * n + 128], HEADS)
            mm.then_inc(s_unit, 1)

            pe.wait_ge(s_doc, NDEC + 2)
            with pe.Fori(0, 4) as r:
                for j in range(2):
                    product(J_ABR + j, 2 * r, J_ABR + j, P_ABR + j, 2 * r, 1, qT, wa=True)

            with pe.Fori(0, GROUPS) as g:
                pe.wait_ge(s_hupd, g * 8 + 2)
                pe.wait_ge(s_hc, g + 2)
                for n in range(6):
                    product(J_SSD + n, 6 * g, J_SSD + n, P_SSD + n, 6 * g, 1, res)
                pe.wait_ge(s_psfree, g * 6 + (J_SSD + 8))
                pe.sem_inc(s_pass, 1)
                def chunk_turn(c, j):
                    n = g * 8 + c
                    pe.wait_ge(s_stg, 2 * n + 2)
                    pe.wait_ge(s_hupd, n + 1)
                    for f in range(4):
                        turn(3 * j, 128 * f, xst[:, j, f, :])
                    turn(3 * j + 1, 0, bst[:, j, :])
                    nc.tensor.matmul(PS[:, 3 * j + 1, 128:256], bst[:, j, :], cT[:, ds(c * 128, 128)],
                                     start=True, stop=True).then_inc(s_tp, 1)

                def chunk_out(c, j):
                    n = g * 8 + c
                    pe.wait_ge(s_bc, 2 * n + 2)
                    pe.wait_ge(s_xdt, 2 * n + 2)
                    nc.tensor.matmul(PS[:, 6 + j, :], btok[j], xdte[j].rearrange("p h d -> p (h d)"),
                                     start=True, stop=True).then_inc(s_st, 1)
                    pe.wait_ge(s_Mm, n + 1)
                    pe.wait_ge(s_CE, n + 1)
                    pe.wait_ge(s_hs, n + 2)
                    pe.wait_ge(s_h0, g + 1)
                    for h in range(8):
                        y = PS[64 * (h % 2):64 * (h % 2) + 64, 3 * j + 2, 128 * (h // 2):128 * (h // 2) + 128]
                        nc.tensor.matmul(y, xdt[j][:, h, :], seg[:, j, h, :], start=True, stop=False)
                        mm = nc.tensor.matmul(y, hst[:, h, :], cumb[:, j, h, :], start=False, stop=True)
                    mm.then_inc(s_y, 1)

                chunk_turn(0, 0)
                with pe.Fori(0, NCHUNK // 2 - 1) as r:
                    for j in range(2):
                        chunk_turn(r * 2 + (j + 1), 1 - j)
                        chunk_out(r * 2 + j, j)
                chunk_turn(7, 1)
                chunk_out(6, 0)
                chunk_out(7, 1)
                pe.wait_ge(s_hupd, g * 8 + 10)
                for f in range(4):
                    mm = turn(0, 128 * f, hst[:, 2 * f:2 * f + 2, :].rearrange("p h d -> p (h d)"))
                mm.then_inc(s_ht, 1)

            pe.wait_ge(s_hc, GROUPS + 2)
            with pe.Fori(0, 4) as r:
                for j in range(2):
                    product(J_GS + j, 2 * r, J_GS + j, P_GS + j, 2 * r, 1, res)

            def column_sums(j, ready, value):
                pe.wait_ge(ready, value)
                pe.wait_ge(s_psfree, j + 1)
                for n in range(3):
                    mm = nc.tensor.matmul(PS[:, 3 * (j % 2) + n, 0:TN], ones[:], nacc[:, n * TN:(n + 1) * TN],
                                          start=True, stop=True)
                mm.then_inc(s_unit, 1)

            column_sums(J_RMS, s_nac, 18)
            pe.wait_ge(s_hn, 16)
            with pe.Fori(0, 4) as r:
                for j in range(2):
                    product(J_SBR + j, 2 * r, U_SBR + 2 * j, P_SBR + 2 * j, 4 * r, 2, hT)
            pe.wait_ge(s_mix, 8)
            with pe.Fori(0, 4) as r:
                for j in range(2):
                    product(J_OUT + j, 2 * r, U_OUT + j, P_OUT + j, 2 * r, 1, mixT)
            column_sums(J_LN1, s_nsum, 10)
            column_sums(J_LN1 + 1, s_nac, 26)
            pe.wait_ge(s_yn, 8)
            with pe.Fori(0, 16) as r:
                for j in range(2):
                    product(J_UP + j, 2 * r, U_UP + j, P_UP + j, 2 * r, 1, res)
            pe.wait_ge(s_hid, 32)
            with pe.Fori(0, 4) as r:
                for j in range(2):
                    product(J_DOWN + j, 2 * r, U_DOWN + 4 * j, P_DOWN + 4 * j, 8 * r, 4, hidT)
            column_sums(J_LN2, s_nsum, 18)
            column_sums(J_LN2 + 1, s_nac, 34)
            for n in range(2):
                pe.wait_ge(s_psfree, J_TAIL + n + 1)
                for t in range(12):
                    mm = turn(3 * ((J_TAIL + n) % 2) + t // 4, 128 * (t % 4), tail[:, 12 * n + t, :])
                mm.then_inc(s_unit, 1)
            pe.wait_ge(s_yn, 16)
            for c in range(NCHUNK + 1):
                n = 128 if c < NCHUNK else NDEC
                pe.wait_ge(s_psfree, J_Y + c + 1)
                for f in range(KT):
                    mm = turn(3 * ((J_Y + c) % 2) + f // 4, 128 * (f % 4), res[:, f, 128 * c:128 * c + n])
                mm.then_inc(s_unit, 1)

        @block.scalar
        def _(act):
            def fn(out, in_, f, **kw):
                return nc.scalar.activation(out, in_, f, **kw)

            with act.Fori(0, NCHUNK // 2) as r:
                for j in range(2):
                    act.wait_ge(s_unit, J_X + j + 1 + 2 * r)
                    act.sem_inc(s_pass, 1)
                    nc.scalar.copy(res[:, :, ds(r * 256 + 128 * j, 128)].rearrange("p (a f) b -> p a f b", a=2),
                                   banks(J_X + j, 2, 512).rearrange("p a (f b) -> p a f b", b=128)).then_inc(s_psfree, 1)
            act.wait_ge(s_unit, J_PAR)
            nc.scalar.copy(res[:, :, SEQ:T], PS[:, 3 * ((J_X + 8) % 2), 0:KT * NDEC].rearrange("p (f b) -> p f b", b=NDEC)).then_inc(s_psfree, 1)
            act.wait_ge(s_unit, J_PAR + 1)
            nc.scalar.copy(par[:, :, :].rearrange("p (a t) n -> p a (t n)", a=2), banks(J_PAR, 2, 12 * NPAR)).then_inc(s_psfree, 1)
            act.wait_ge(s_unit, J_PAR + 2)
            nc.scalar.copy(vec[:, :, :], PS[:, 3 * ((J_PAR + 1) % 2), 0:6 * KT].rearrange("p (f n) -> p f n", n=6)).then_inc(s_psfree, 1)
            for c0, n, t in ((0, 4, qT), (8, 2, kvT)):
                with act.Fori(0, n) as r:
                    for j in range(2):
                        act.wait_ge(s_unit, J_QKV + c0 + j + 1 + 2 * r)
                        act.sem_inc(s_pass, 1)
                        nc.scalar.copy(tile(t, r * 2 + j), banks(J_QKV + c0 + j)).then_inc(s_psfree, 1)
            with act.Fori(0, NCHUNK // 2) as r:
                for j in range(2):
                    act.wait_ge(s_unit, J_KVT + j + 1 + 2 * r)
                    act.sem_inc(s_pass, 1)
                    nc.scalar.copy(kvtok[:, ds(r * 2 + j, 1), :], banks(J_KVT + j, 1, 512)).then_inc(s_psfree, 1)
            act.wait_ge(s_unit, J_DT)
            nc.scalar.copy(kvtok[0:NDEC, 8:9, :], PS[0:NDEC, 3 * ((J_KVT + 8) % 2):3 * ((J_KVT + 8) % 2) + 1, :]).then_inc(s_psfree, 1)

            act.wait_ge(s_small, 16 * 14)
            act.preload_act_table_set("natural_log_exp_and_others")
            def out(pair, m):
                act.wait_ge(s_o, pair * 8 + (m + 3))
                act.sem_inc(s_pass, 1)
                nc.scalar.copy(big[:, ds(pair, 1), 128 * m:128 * m + 128],
                               PS[:, 6:7, 128 * (m % 2):128 * (m % 2) + 128]).then_inc(s_oc, 1)

            def third_out(pair, m):
                th = m % 3
                act.wait_ge(s_p3, pair * 9 + (m + 1))
                act.wait_ge(s_pst[th], pair * 48 + (16 * (m // 3) + 16))
                nc.scalar.copy(pst[:, th, :], PS[:, 7, 0:TN]).then_inc(s_pc, 1)

            def weights(pair, m):
                act.wait_ge(s_d, pair * 16 + (2 * m + 4))
                w = zb[:, m % 2, :, 0:128 * (m + 1)]
                fn(w, w, ACT.Exp).then_inc(s_wt, 1)

            def steps(pair, head, first=False):
                for m in range(8):
                    S = 128 * (m + 1)
                    M = pair * 8 + m
                    z = [PS[:, 2 * k:2 * k + 2, :].rearrange("p a b -> p (a b)")[:, 0:S] for k in range(2)]
                    bias = [sbb[:, ds(head + 4 * k, 1)] for k in range(2)]
                    l = lb[:, m % 2, :, 0:S]
                    act.wait_ge(s_z, M + 1)
                    act.sem_inc(s_pass, 1)
                    fn(zb[:, m % 2, 0, 0:S], z[0], ACT.Identity, bias=bias[0], scale=SCALE)
                    fn(zb[:, m % 2, 1, 0:S], z[1], ACT.Identity, bias=bias[1], scale=SCALE)
                    act.wait_ge(s_scan, 2 * M + 2)
                    act.sem_inc(s_pass, 1)
                    fn(l[:, 0], z[0], ACT.Abs, bias=bias[0], scale=SCALE)
                    fn(l[:, 1], z[1], ACT.Abs, bias=bias[1], scale=SCALE).then_inc(s_ab, 1)
                    act.wait_ge(s_ab, M + 2)
                    fn(l, l, ACT.Exp, scale=-1.0).then_inc(s_ex, 1)
                    if m >= 1:
                        third_out(pair, m - 1)
                    elif not first:
                        third_out(pair - 1, 8)
                    if m >= 2:
                        out(pair, m - 2)
                    elif not first:
                        out(pair - 1, m + 6)
                    act.wait_ge(s_ex, M + 1)
                    fn(l, l, ACT.Ln, bias=1.0).then_inc(s_ln, 1)
                    if m >= 1:
                        weights(pair, m - 1)
                    elif not first:
                        weights(pair - 1, 7)
                third_out(pair, 7)

            steps(0, 0, first=True)
            with act.Fori(1, 4) as i:
                steps(i, i)
            steps(4, 8)
            with act.Fori(1, 4) as i:
                steps(i + 4, i + 8)
            third_out(7, 8)
            out(7, 6)
            weights(7, 7)
            out(7, 7)

            act.wait_ge(s_pt, 16)
            act.wait_ge(s_kvo, 64)
            act.wait_ge(s_oc, 66)
            for j in range(2):
                load_pages(act, "cache_k", 0, j, 1)

            with act.Fori(0, NDEC // 2 - 1) as r:
                for j in range(2):
                    act.wait_ge(s_dtr, 16 * r + 8 * (j + 1))
                    act.sem_inc(s_pass, 1)
                    load_pages(act, "cache_k", r + 1, j, 1)
            for j in range(2):
                act.wait_ge(s_dtr, 56 + 8 * j)
                load_pages(act, "cache_v", 0, j, 1)
            zall = PS[:, 0:4, :].rearrange("p a b -> p (a b)")
            act.wait_ge(s_dz, 66)
            fn(zd, zall, ACT.Identity, bias=sbd[:], scale=SCALE).then_inc(s_dact, 1)
            fn(ld, zall, ACT.Abs, bias=sbd[:], scale=SCALE).then_inc(s_dact, 1)
            act.wait_ge(s_dact, 2)
            fn(ld, ld, ACT.Exp, scale=-1.0).then_inc(s_dact, 1)
            act.wait_ge(s_dact, 3)
            fn(ld, ld, ACT.Ln, bias=1.0).then_inc(s_dact, 1)
            act.wait_ge(s_dd, 3)
            fn(zd, zd, ACT.Exp).then_inc(s_dexp, 1)
            for j in range(2):
                act.wait_ge(s_do, j + 1)
                load_pages(act, "cache_v", 1, j, 1)
            act.wait_ge(s_small, 16 * 14)
            fn(alog[:], alog[:], ACT.Exp).then_inc(s_dta, 1)
            act.wait_ge(s_dt, 2)
            fn(dte1, dtr, ACT.Abs).then_inc(s_dta, 1)
            act.wait_ge(s_dta, 2)
            fn(dte1, dte1, ACT.Exp, scale=-1.0).then_inc(s_dta, 1)
            act.wait_ge(s_dt, 3)
            fn(dtl, dtu, ACT.Ln).then_inc(s_dta, 1)
            with act.Fori(2, NDEC // 2) as r:
                for j in range(2):
                    act.wait_ge(s_do, 2 * r + j - 1)
                    act.sem_inc(s_pass, 1)
                    load_pages(act, "cache_v", r, j, 1)

            for n in range(4):
                act.wait_ge(s_ga[n], 16)
                t = mixT[:, 2 * n:2 * n + 2, :]
                fn(t, t, ACT.Sigmoid).then_inc(s_gas, 2)

            act.wait_ge(s_dtx, 64)
            fn(dtx[:, 0], dtx[:, 0], ACT.Exp).then_inc(s_dtxe, 1)

            def out_state(g, q):
                act.wait_ge(s_d4, g * 4 + (q + 1))
                dst = ssm_sample[0].rearrange("b h p n -> (h p) b n")[ds(g * 512 + q * 128, 128)]
                act.dma_start(dst, h0b[:, q]).then_inc(s_dso, 16)

            def conv(g, decode):
                act.wait_ge(s_rz, g + 1)
                for n in range(4):
                    act.wait_ge(s_zm, g * 4 + (n + 1))
                    if n == 0:
                        act.sem_inc(s_pass, 1)
                        for k in range(1 if not decode else 4):
                            act.wait_ge(s_zl[k], 16)
                    act.sem_inc(s_pass, 1)
                    fn(zsg, hT[:, ds(g * 4 + n, 1), :].rearrange("p o t -> p (o t)"), ACT.Sigmoid).then_inc(s_zsg, 1)
                for n in range(6):
                    ct = g * 4 + n if n < 4 else g + (16 + 4 * (n - 4))
                    J = J_SSD + n
                    act.wait_ge(s_unit, g * 6 + (J + 1))
                    if n == 0:
                        act.wait_ge(s_psfree, g * 6 + (J + 2))
                    act.wait_ge(s_cv, g * 24 + (4 * n + 2))
                    b0 = 3 * (J % 2)
                    nc.scalar.copy(raw[:, 3:3 + 2 * TN].rearrange("p (a b) -> p a b", a=2), PS[:, b0:b0 + 2, 0:TN])
                    nc.scalar.copy(raw[:, 3 + 2 * TN:3 + SEQ], PS[:, b0 + 2, 0:TN - NDEC])
                    nc.scalar.copy(raw[:, 3 + SEQ:RAWLEN].rearrange("p (b k) -> p b k", k=4)[:, :, 0:3],
                                   par[:, ds(ct, 1), 5:NPAR].rearrange("p o (b k) -> p (o b) k", k=3))
                    nc.scalar.copy(raw[:, 3 + SEQ:RAWLEN].rearrange("p (b k) -> p b k", k=4)[:, :, 3:4],
                                   PS[:, b0 + 2, TN - NDEC:TN].rearrange("p (b o) -> p b o", o=1)).then_inc(s_raw, 1)
                    nc.scalar.copy(tail[:, ds(ct, 1), :], PS[:, b0 + 2:b0 + 3, TN - NDEC - 3:TN]).then_inc(s_psfree, 1)
                    act.wait_ge(s_cv, g * 24 + (4 * n + 6))
                    act.wait_ge(s_cout, g * 6 + (n + 2))
                    fn(sig, acc, ACT.Sigmoid).then_inc(s_csg, 1)
                    if decode and n < 4:
                        out_state(g - 1, n)

            def chunks(g):
                with act.Fori(0, NCHUNK // 2) as r:
                    for j in range(2):
                        n = g * 8 + 2 * r + j
                        act.wait_ge(s_cb[j], g * 64 + 16 * r + 16)
                        act.wait_ge(s_hupd, n + 1)
                        fn(cd[j], cumb[:, j, :, 127], ACT.Exp).then_inc(s_cd, 1)
                        act.wait_ge(s_t8, n + 1)
                        fn(t8[j], t8[j], ACT.Exp).then_inc(s_t8e, 1)
                        act.wait_ge(s_sg, n + 1)
                        act.wait_ge(s_cd, n + 1)
                        fn(cumb[:, j], cumb[:, j], ACT.Exp).then_inc(s_ec, 1)
                        act.wait_ge(s_sg2, n + 1)
                        fn(seg[:, j], seg[:, j], ACT.Exp).then_inc(s_M, 1)
                act.wait_ge(s_ht, g + 1)
                act.wait_ge(s_ho, g * 16 + 16)
                nc.scalar.copy(hout.rearrange("p j n -> p (j n)"), PS[:, 0, :]).then_inc(s_hc, 1)

            conv(0, False)
            chunks(0)
            with act.Fori(1, GROUPS) as g:
                conv(g, True)
                chunks(g)
            for q in range(4):
                out_state(GROUPS - 1, q)
            act.wait_ge(s_d8, 18)

            def squares(t, n, base, nbase):
                with act.Fori(0, n // 2) as r:
                    for j in range(2):
                        if t is res:
                            act.wait_ge(s_dm, nbase + j + 1 + 2 * r)
                        act.wait_ge(s_nac, base + j + 1 + 2 * r)
                        act.sem_inc(s_pass, 1)
                        fn(nsq[:, j], t[:, ds(r * 2 + j, 1), :].rearrange("p o t -> p (o t)"), ACT.Square).then_inc(s_sq, 1)

            squares(hT, 16, 0, 0)
            with act.Fori(0, 4) as r:
                for j in range(2):
                    act.wait_ge(s_unit, J_GS + j + 1 + 2 * r)
                    act.sem_inc(s_pass, 1)
                    fn(tile(gsT, r * 2 + j), banks(J_GS + j), ACT.Sigmoid).then_inc(s_psfree, 1)

            act.wait_ge(s_unit, J_RMS + 1)
            fn(nbc.rearrange("p (a b) -> p a b", a=3), banks(J_RMS), ACT.Sqrt, bias=eps[:], scale=1.0 / D_INNER).then_inc(s_psfree, 1)

            def norm(n, unit, j):
                squares(res, 8, 16 + 8 * n, 8 * n)
                act.wait_ge(s_unit, unit + 2)
                fn(nbc2.rearrange("p (a b) -> p a b", a=3), banks(j + 1), ACT.Sqrt, bias=eps[:], scale=1.0 / D).then_inc(s_psfree, 1)
                with act.Fori(0, KT) as m:
                    act.wait_ge(s_yn0, m + (8 * n + 1))
                    act.sem_inc(s_pass, 1)
                    fn(res[:, ds(m, 1), :], res[:, ds(m, 1), :], ACT.Identity, bias=vec[:, ds(m, 1), 2 * n + 1],
                       scale=vec[:, ds(m, 1), 2 * n]).then_inc(s_yn, 1)

            norm(0, U_LN1, J_LN1)
            with act.Fori(0, 16) as r:
                for j in range(2):
                    act.wait_ge(s_unit, U_UP + j + 1 + 2 * r)
                    act.sem_inc(s_pass, 1)
                    fn(tile(hidT, r * 2 + j), banks(J_UP + j), ACT.Relu).then_inc(s_psfree, 1)
            norm(1, U_LN2, J_LN2)
            for n in range(2):
                act.wait_ge(s_unit, U_TAIL + n + 1)
                b0 = 3 * ((J_TAIL + n) % 2)
                nc.scalar.copy(tailrow[0:3 + NDEC, 1536 * n:1536 * n + 1536].rearrange("p (a b) -> p a b", a=3),
                               PS[0:3 + NDEC, b0:b0 + 3, :]).then_inc(s_psfree, 1)
            with act.Fori(0, NCHUNK // 2) as r:
                for j in range(2):
                    act.wait_ge(s_unit, U_Y + j + 1 + 2 * r)
                    act.wait_ge(s_yout[j], 16 * r + 16)
                    nc.scalar.copy(ytok[:, j, :].rearrange("p (a b) -> p a b", a=2), banks(J_Y + j, 2, 512)).then_inc(s_psfree, 1)
            act.wait_ge(s_unit, U_Y + 9)
            act.wait_ge(s_yout[0], 80)
            b0 = 3 * ((J_Y + 8) % 2)
            nc.scalar.copy(ytok[0:NDEC, 0, :].rearrange("p (a b) -> p a b", a=2), PS[0:NDEC, b0:b0 + 2, :]).then_inc(s_psfree, 1)

        @block.vector
        def _(dve):
            tt, ts, stt, copy = nc.vector.tensor_tensor, nc.vector.tensor_scalar, nc.vector.scalar_tensor_tensor, nc.vector.tensor_copy
            dve.sem_inc(s_ab, 1)
            dve.sem_inc(s_pc, 1)
            dve.sem_inc(s_zm, 1)
            dve.sem_inc(s_scan, 4)
            for s in (s_psfree, s_d, s_o, s_oc, s_dcp, s_cp, s_dz, s_doc, s_hs, s_hupd, s_nac, s_hc, s_y, s_cv, s_cout, s_nsum, s_d8):
                dve.sem_inc(s, 2)
            for s in (*s_yout, *s_pst, s_ho, s_dso):
                dve.sem_inc(s, 16)
            nc.vector.memset(eps[:], EPS)
            nc.vector.memset(ones[:], 1.0).then_inc(s_const, 1)

            dve.wait_ge(s_qz, 1)
            dve.wait_ge(s_psfree, J_KVT + 2)
            for b in range(NDEC):
                for c in range(2):
                    for k in range(2):
                        dst = qbd[64 * k:64 * k + 64, b, c, 16 * b + 8 * c + 4 * k:16 * b + 8 * c + 4 * k + 4]
                        copy(dst, big[64 * k:64 * k + 64, 4 * c:4 * c + 4, SEQ + b]).then_inc(s_qb, 1)
            dve.wait_ge(s_const, 5)
            both = lambda v: v[:, :].rearrange("p (o s) -> p o s", o=1).to_broadcast([128, 2, 128])
            def weights_turned(pair, m):
                dve.wait_ge(s_o, pair * 8 + (m + 1))
                for n, (k, kb0, nb) in enumerate(turns(m)):
                    dve.wait_ge(s_tr, pair * 24 + (turned(m) + n + 1))
                    copy(wTb[:, m % 2, 8 * k + kb0:8 * k + kb0 + nb, :].rearrange("p a b -> p (a b)"),
                         PS[:, 4 + n % 2, 0:128 * nb]).then_inc(s_cp, 1)

            def steps(pair, first=False):
                for m in range(8):
                    S = 128 * (m + 1)
                    M = pair * 8 + m
                    l = lb[:, m % 2]
                    dve.wait_ge(s_ln, M + 1)
                    stt(l[:, :, 0:S], zb[:, m % 2, :, 0:S], 0.0, l[:, :, 0:S], ALU.max, ALU.add).then_inc(s_sp, 1)
                    dve.wait_ge(s_sp, M + 1)
                    tt(l[:, :, S - 128:S], l[:, :, S - 128:S], both(keep), ALU.mult).then_inc(s_spm, 1)
                    dve.wait_ge(s_spm, M + 1)
                    back = slice(S - 1, None, -1)
                    for k in range(2):
                        dve.wait_ge(s_d, 2 * M + (k + 1))
                        nc.vector.tensor_tensor_scan(sbuf_s[:, k, back], ones[:, 0:1].to_broadcast([128, S]), l[:, k, back],
                                                     0.0, ALU.mult, ALU.add).then_inc(s_scan, 1)
                    for k in range(2):
                        dve.wait_ge(s_scan, 2 * M + (k + 5))
                        tt(sbuf_s[:, k, S - 128:S], sbuf_s[:, k, S - 128:S], far[:], ALU.add).then_inc(s_far, 1)
                    if m >= 1:
                        weights_turned(pair, m - 1)
                    elif not first:
                        weights_turned(pair - 1, 7)

            steps(0, first=True)
            with dve.Fori(1, 8) as pair:
                steps(pair)
            weights_turned(7, 7)

            dve.wait_ge(s_oc, 66)
            with dve.Fori(0, NDEC) as b:
                for q in range(8):
                    dve.wait_ge(s_dtr, b * 8 + (q + 1))
                    dve.wait_ge(s_dz, b * 8 + (q + 1))
                    copy(kTst[:, q % 2, :], PS[:, 4 + q % 2, :]).then_inc(s_dcp, 1)

            dve.wait_ge(s_dact, 4)
            stt(ld, zd, 0.0, ld, ALU.max, ALU.add).then_inc(s_dd, 1)
            dve.wait_ge(s_dd, 1)
            nc.vector.tensor_tensor_scan(sd[:, ::-1], ones[:, 0:1].to_broadcast([128, PAST]), ld[:, ::-1], 0.0, ALU.mult, ALU.add).then_inc(s_dd, 1)
            dve.wait_ge(s_dd, 2)
            tt(zd, zd, sd, ALU.subtract).then_inc(s_dd, 1)
            dve.wait_ge(s_dtw, 1)
            copy(wTd.rearrange("p a b -> p (a b)"), PS[:, 4:8, :].rearrange("p a b -> p (a b)")).then_inc(s_dcw, 1)
            def decode_out(r, j):
                dve.wait_ge(s_do, 2 * r + j + 1)
                o = PS[:, 4 + j, 0:16].rearrange("p (c k i) -> p c k i", c=2, k=2)
                for k in range(2):
                    dst = big[64 * k:64 * k + 64, 0:8, ds(r * 2 + (SEQ + j), 1)].rearrange("p (c i) o -> p c (i o)", c=2)
                    op = copy(dst, o[64 * k:64 * k + 64, :, k, :])
                op.then_inc(s_doc, 1)

            for j in range(2):
                decode_out(0, j)
            dve.wait_ge(s_dta, 1)
            ts(alog[:], alog[:], -1.0, None, ALU.mult).then_inc(s_dt, 1)
            dve.wait_ge(s_unit, J_DT + 1)
            dve.wait_ge(s_psfree, J_DT + 2)
            ts(dtr.rearrange("p (a b) -> p a b", a=3), PS[0:HEADS, 3 * (J_DT % 2):3 * (J_DT % 2) + 3, 0:TN], dtb[:], None,
               ALU.add).then_inc(s_dt, 1)
            dve.wait_ge(s_dta, 3)
            ts(dtu, dte1, 1.0, None, ALU.add).then_inc(s_dt, 1)
            dve.wait_ge(s_dt, 3)
            ts(dtv, dtu, 1.0, None, ALU.subtract).then_inc(s_dt, 1)
            dve.wait_ge(s_dt, 4)
            tt(dtv, dte1, dtv, ALU.subtract).then_inc(s_dt, 1)
            dve.wait_ge(s_dta, 4)
            nc.vector.reciprocal(dtu, dtu).then_inc(s_dt, 1)
            dve.wait_ge(s_dt, 6)
            tt(dtv, dtv, dtu, ALU.mult).then_inc(s_dt, 1)
            dve.wait_ge(s_dt, 7)
            tt(dtl, dtl, dtv, ALU.add).then_inc(s_dt, 1)
            dve.wait_ge(s_dt, 8)
            stt(dtr, dtr, 0.0, dtl, ALU.max, ALU.add).then_inc(s_dt, 1)
            nc.vector.memset(chm, 1.0).then_inc(s_dt, 1)
            dve.wait_ge(s_dt, 10)
            nc.vector.memset(chm.rearrange("p (c l) -> p c l", l=CHUNK)[:, :, 0:1], 0.0).then_inc(s_dt, 1)
            ts(dtl, dtr, alog[:], None, ALU.mult).then_inc(s_dt, 1)
            dve.wait_ge(s_dt, 12)
            nc.vector.tensor_tensor_scan(dtv[:, 0:SEQ], chm, dtl[:, 0:SEQ], 0.0, ALU.mult, ALU.add).then_inc(s_dt, 1)
            with dve.Fori(1, NDEC // 2) as r:
                for j in range(2):
                    decode_out(r, j)
            dve.wait_ge(s_dt, DT_CUM)
            dve.sem_inc(s_psfree, 1)
            dve.wait_ge(s_unit, J_DT + 2)
            b0 = 3 * ((J_DT + 1) % 2)
            copy(cumtok[:, :, :].rearrange("p c h -> p (c h)"), PS[:, b0, 0:256]).then_inc(s_tok, 1)
            copy(dttok[:, :, :].rearrange("p c h -> p (c h)"), PS[:, b0, 256:512]).then_inc(s_psfree, 1)
            dve.wait_ge(s_tok, 1)

            dve.wait_ge(s_psfree, J_ABR + 2)
            with dve.Fori(0, 4) as r:
                for j in range(2):
                    dve.wait_ge(s_gas, j + 1 + 2 * r)
                    dve.sem_inc(s_pass, 1)
                    dve.wait_ge(s_unit, J_ABR + j + 1 + 2 * r)
                    t = tile(mixT, r * 2 + j)
                    tt(t, banks(J_ABR + j), t, ALU.mult).then_inc(s_psfree, 1)

            dve.wait_ge(s_psfree, J_SSD + 2)

            def decode_step(g, q):
                wide8 = lambda v: v.rearrange("p (b o) -> p b o", o=1).to_broadcast([128, NDEC, 128])
                n = g * 4 + q
                if q == 0:
                    dve.wait_ge(s_bcr, g * 16 + 16)
                    dve.sem_inc(s_pass, 1)
                    dve.wait_ge(s_dtxe, 1)
                xcol = xsT[:, q, SEQ:T]
                tt(xdd, xcol, dtx[:, 1, ds(n, 1), :].rearrange("p o b -> p (o b)"), ALU.mult).then_inc(s_d1, 1)
                if q == 0:
                    dve.wait_ge(s_dh, g * 64 + 64)
                tt(h0b[:, q], h0b[:, q], wide8(dtx[:, 0, ds(n, 1), :].rearrange("p o b -> p (o b)")), ALU.mult).then_inc(s_d3, 1)
                dve.wait_ge(s_d2, n + 1)
                dve.wait_ge(s_d3, n + 1)
                tt(h0b[:, q], h0b[:, q], t2, ALU.add).then_inc(s_d4, 1)
                dve.wait_ge(s_d5, n + 1)
                nc.vector.tensor_reduce(yd, t2, AX_X, ALU.add).then_inc(s_d6, 1)
                dve.wait_ge(s_d6, n + 1)
                stt(yd, xcol, dskip[:, ds(n, 1)], yd, ALU.mult, ALU.add).then_inc(s_d7, 1)
                dve.wait_ge(s_d7, n + 1)
                t = hT[:, ds(n, 1), SEQ:T].rearrange("p o b -> p (o b)")
                tt(t, t, yd, ALU.mult).then_inc(s_d8, 1)

            def conv(g, decode):
                dve.wait_ge(s_hc, g + 2)
                dve.wait_ge(s_scr, 48)
                nc.vector.memset(hst, 0.0).then_inc(s_h0, 1)
                nc.vector.memset(raw[:, 0:3], 0.0).then_inc(s_rz, 1)
                dve.wait_ge(s_psfree, g * 6 + (J_SSD + 2))
                for n in range(4):
                    dve.wait_ge(s_zsg, g * 4 + (n + 1))
                    dve.sem_inc(s_pass, 1)
                    t = hT[:, ds(g * 4 + n, 1), :]
                    tt(t, t, zsg.rearrange("p (o t) -> p o t", o=1), ALU.mult).then_inc(s_zm, 1)
                for n in range(6):
                    if decode and n < 4:
                        decode_step(g - 1, n)
                    ct = g * 4 + n if n < 4 else g + (16 + 4 * (n - 4))
                    w = [par[:, ds(ct, 1), k] for k in range(5)]
                    dve.wait_ge(s_raw, g * 6 + (n + 1))
                    dve.wait_ge(s_cout, g * 6 + (n + 2))
                    ts(acc, raw[:, 0:ACCLEN], w[0], w[4], ALU.mult, ALU.add).then_inc(s_cv, 1)
                    for k in range(1, 4):
                        dve.wait_ge(s_cv, g * 24 + (4 * n + k + 2))
                        stt(acc, raw[:, k:k + ACCLEN], w[k], acc, ALU.mult, ALU.add).then_inc(s_cv, 1)
                    dve.wait_ge(s_csg, g * 6 + (n + 1))
                    t = big[:, 24 + n, :]
                    tt(t[:, 0:SEQ], acc[:, 0:SEQ], sig[:, 0:SEQ], ALU.mult)
                    tt(t[:, SEQ:T], acc[:, DEC0:ACCLEN:4], sig[:, DEC0:ACCLEN:4], ALU.mult).then_inc(s_cout, 1)

            def chunks(g):
                wide = lambda v, w: v.rearrange("p (h o) -> p h o", o=1).to_broadcast([128, 8, w])

                def prepare(c, j, r):
                    n = g * 8 + c
                    cum8 = cumtok[:, ds(c, 1), ds(g * 8, 8)].rearrange("p o h -> p (o h)")
                    dt8 = dttok[:, ds(c, 1), ds(g * 8, 8)].rearrange("p o h -> p (o h)")
                    dve.wait_ge(s_cb[j], g * 64 + 16 * r + 16)
                    dve.wait_ge(s_hupd, n + 1)
                    tt(t8[j], cumb[:, j, :, 127], cum8, ALU.subtract).then_inc(s_t8, 1)
                    tt(seg[:, j], cumb[:, j], wide(cum8, 128), ALU.subtract).then_inc(s_sg, 1)
                    dve.wait_ge(s_sg, n + 1)
                    ts(seg[:, j], seg[:, j], 0.0, None, ALU.min).then_inc(s_sg2, 1)
                    dve.wait_ge(s_tp, n + 1)
                    copy(btok[j], PS[:, 3 * j + 1, 0:128]).then_inc(s_bc, 1)
                    tt(cbm[j], PS[:, 3 * j + 1, 128:256], tri[:], ALU.mult).then_inc(s_bc, 1)
                    dve.wait_ge(s_t8e, n + 1)
                    tt(dte[j], t8[j], dt8, ALU.mult).then_inc(s_dte, 1)
                    x = PS[:, 3 * j, :].rearrange("p (h d) -> p h d", d=64)
                    tt(xdt[j], x, wide(dt8, 64), ALU.mult).then_inc(s_xdt, 1)
                    dve.wait_ge(s_dte, n + 1)
                    tt(xdte[j], x, wide(dte[j], 64), ALU.mult).then_inc(s_xdt, 1)
                    dve.wait_ge(s_ec, n + 1)
                    tt(cumb[:, j], cumb[:, j], cT[:, ds(c * 128, 128)].rearrange("p (o l) -> p o l", o=1).to_broadcast([128, 8, 128]),
                       ALU.mult).then_inc(s_CE, 1)

                def finish(c, j):
                    n = g * 8 + c
                    dve.wait_ge(s_cd, n + 1)
                    dve.wait_ge(s_y, n + 3)
                    tt(hst, hst, wide(cd[j], 64), ALU.mult).then_inc(s_hm, 1)
                    dve.wait_ge(s_hm, n + 1)
                    dve.wait_ge(s_st, n + 1)
                    tt(hst, hst, PS[:, 6 + j, :].rearrange("p (h d) -> p h d", d=64), ALU.add).then_inc(s_hs, 1)
                    dve.wait_ge(s_hupd, n + 2)
                    for f in range(4):
                        stt(y1[:, f, :], xst[:, j, f, :], dskip[:, ds(g * 4 + f, 1)],
                            PS[:, 3 * j + 2, 128 * f:128 * f + 128], ALU.mult, ALU.add).then_inc(s_y1, 1)
                    dve.wait_ge(s_y1, 4 * n + 4)
                    t = hT[:, ds(g * 4, 4), ds(c * 128, 128)]
                    tt(t, t, y1, ALU.mult).then_inc(s_hupd, 1)

                prepare(0, 0, 0)
                with dve.Fori(0, NCHUNK // 2 - 1) as r:
                    prepare(r * 2 + 1, 1, r)
                    finish(r * 2, 0)
                    prepare(r * 2 + 2, 0, r + 1)
                    finish(r * 2 + 1, 1)
                prepare(7, 1, 3)
                finish(6, 0)
                finish(7, 1)

            dve.wait_ge(s_mxo, 64)
            conv(0, False)
            chunks(0)
            with dve.Fori(1, GROUPS) as g:
                conv(g, True)
                chunks(g)
            for q in range(4):
                decode_step(GROUPS - 1, q)

            def add_squares(n, k):
                with dve.Fori(0, n // 2) as r:
                    for j in range(2):
                        dve.wait_ge(s_sq, k + j + 1 + 2 * r)
                        dve.wait_ge(s_nac, k + j + 2 + 2 * r)
                        tt(nacc, nacc, nsq[:, j], ALU.add).then_inc(s_nac, 1)

            dve.wait_ge(s_d8, 18)
            nc.vector.memset(nacc, 0.0).then_inc(s_nz, 1)
            dve.wait_ge(s_nz, 1)
            add_squares(16, 0)
            for half in range(2):
                with dve.Fori(0, 8) as m:
                    t = hT[:, ds(m + 8 * half, 1), :]
                    ts(t, t, vec[:, ds(m, 1), 4 + half], None, ALU.mult).then_inc(s_hn, 1)
            dve.wait_ge(s_psfree, J_RMS + 3)
            nc.vector.reciprocal(nbc, nbc).then_inc(s_rs, 1)
            dve.wait_ge(s_rs, 1)
            with dve.Fori(0, 8) as m:
                t = gsT[:, ds(m, 1), :]
                tt(t, t, nbc.rearrange("p (o t) -> p o t", o=1), ALU.mult).then_inc(s_gr, 1)
            dve.wait_ge(s_gr, 8)
            dve.wait_ge(s_mxi, 64)
            with dve.Fori(0, 4) as r:
                for j in range(2):
                    dve.wait_ge(s_unit, U_SBR + 2 * j + 2 + 4 * r)
                    u = nsq[:, j].rearrange("p (a b) -> p a b", a=3)
                    tt(u, banks(J_SBR + j), tile(gsT, r * 2 + j), ALU.mult).then_inc(s_psfree, 1)
                    dve.wait_ge(s_psfree, J_SBR + j + 3 + 2 * r)
                    t = tile(mixT, r * 2 + j)
                    tt(t, t, u, ALU.add).then_inc(s_mix, 1)

            def residual(j0, unit, per):
                with dve.Fori(0, 4) as r:
                    for j in range(2):
                        dve.wait_ge(s_unit, unit + per * (j + 1) + 2 * per * r)
                        t = tile(res, r * 2 + j)
                        stt(t, t, ALPHA, banks(j0 + j), ALU.mult, ALU.add).then_inc(s_psfree, 1)

            def norm(n, unit, j):
                dve.wait_ge(s_unit, unit + 1)
                ts(nbc.rearrange("p (a b) -> p a b", a=3), banks(j), 1.0 / D, None, ALU.mult).then_inc(s_psfree, 1)
                nc.vector.memset(nacc, 0.0).then_inc(s_nz, 1)
                dve.wait_ge(s_psfree, j + 3)
                with dve.Fori(0, KT) as m:
                    t = res[:, ds(m, 1), :]
                    tt(t, t, nbc.rearrange("p (o t) -> p o t", o=1), ALU.subtract).then_inc(s_dm, 1)
                dve.wait_ge(s_nz, 2 + n)
                add_squares(8, 16 + 8 * n)
                dve.wait_ge(s_psfree, j + 4)
                nc.vector.reciprocal(nbc2, nbc2).then_inc(s_rs, 1)
                dve.wait_ge(s_rs, 2 + n)
                dve.sem_inc(s_pass, 1)
                with dve.Fori(0, KT) as m:
                    t = res[:, ds(m, 1), :]
                    tt(t, t, nbc2.rearrange("p (o t) -> p o t", o=1), ALU.mult).then_inc(s_yn0, 1)

            residual(J_OUT, U_OUT, 1)
            norm(0, U_LN1, J_LN1)
            dve.wait_ge(s_yn, 8)
            dve.wait_ge(s_psfree, J_DOWN + 2)
            residual(J_DOWN, U_DOWN, 4)
            norm(1, U_LN2, J_LN2)

        @block.gpsimd
        def _(pool):
            tt, ts, copy = nc.gpsimd.tensor_tensor, nc.gpsimd.tensor_scalar, nc.gpsimd.tensor_copy
            nc.gpsimd.memset(ident[:], 0.0).then_inc(s_cst0, 1)
            nc.gpsimd.memset(keep[:], 1.0).then_inc(s_cst0, 1)
            nc.gpsimd.memset(far[:], 0.0).then_inc(s_cst0, 1)
            nc.gpsimd.memset(tri[:], 1.0).then_inc(s_cst0, 1)
            pool.wait_ge(s_cst0, 4)
            for t, op, fill, step, ch in ((ident, ALU.not_equal, 1.0, -1, 1), (keep, ALU.is_gt, 0.0, -1, 1),
                                          (far, ALU.is_gt, FAR, -1, 1), (tri, ALU.is_ge, 0.0, 1, -1)):
                nc.gpsimd.affine_select(out=t[:], in_=t[:], compare_op=op, fill=fill, base=0, pattern=[[step, 128]],
                                        channel_multiplier=ch).then_inc(s_const, 1)
            nc.gpsimd.memset(qbd, 0.0).then_inc(s_qz, 1)
            pool.wait_ge(s_psfree, J_DT + 2)
            copy(qst, big[:, 0, 0:SEQ]).then_inc(s_qst, 8)
            for c in range(2):
                copy(vst[c], kvtok[:, 0:8, 256 + 128 * c:384 + 128 * c]).then_inc(s_vst, 1)

            def steps(pair, last=False):
                for m in range(8):
                    S = 128 * (m + 1)
                    for k in range(2):
                        pool.wait_ge(s_far, pair * 16 + (2 * m + k + 1))
                        tt(zb[:, m % 2, k, 0:S], zb[:, m % 2, k, 0:S], sbuf_s[:, k, 0:S], ALU.subtract).then_inc(s_d, 1)
                    if not last:
                        copy(qst[:, 128 * m:128 * m + 128],
                             big[:, ds(pair + 1, 1), 128 * m:128 * m + 128].rearrange("p o t -> p (o t)")).then_inc(s_qst, 1)

            with pool.Fori(0, 7) as pair:
                steps(pair)
            steps(7, last=True)
            pool.wait_ge(s_qb, 32)
            for k in range(3):
                pool.wait_ge(s_pst[k], 16 * 25)
            for j in range(2):
                copy(qstd[:, j], qbd[:, j]).then_inc(s_qs, 1)
            with pool.Fori(1, NDEC // 2) as r:
                for j in range(2):
                    pool.wait_ge(s_dz, r * 16 + (8 * j - 6))
                    copy(qstd[:, j], qbd[:, ds(r * 2 + j, 1)].rearrange("p o c n -> p (o c) n")).then_inc(s_qs, 1)

            def chunks(g):
                pool.wait_ge(s_cout, g * 6 + 8)
                pool.sem_inc(s_pass, 1)
                def stage(c, j):
                    pool.wait_ge(s_hupd, g * 8 + c + 1)
                    pool.sem_inc(s_pass, 1)
                    copy(xst[:, j], xsT[:, :, ds(c * 128, 128)]).then_inc(s_stg, 1)
                    copy(bst[:, j], bT[:, ds(c * 128, 128)]).then_inc(s_stg, 1)

                def weigh(c, j):
                    n = g * 8 + c
                    pool.wait_ge(s_M, n + 1)
                    pool.wait_ge(s_bc, 2 * n + 2)
                    tt(seg[:, j], seg[:, j], cbm[j].rearrange("p (o l) -> p o l", o=1).to_broadcast([128, 8, 128]), ALU.mult).then_inc(s_Mm, 1)

                stage(0, 0)
                stage(1, 1)
                with pool.Fori(0, NCHUNK // 2 - 1) as r:
                    for j in range(2):
                        weigh(r * 2 + j, j)
                        stage(r * 2 + (j + 2), j)
                weigh(6, 0)
                weigh(7, 1)

            with pool.Fori(0, GROUPS) as g:
                chunks(g)
                wide8 = lambda v: v.rearrange("p (b o) -> p b o", o=1).to_broadcast([128, NDEC, 128])
                pool.wait_ge(s_bcr, g * 16 + 16)
                pool.sem_inc(s_pass, 1)
                for q in range(4):
                    pool.wait_ge(s_d1, g * 4 + (q + 1))
                    tt(t2, bcb[:, 0], wide8(xdd), ALU.mult).then_inc(s_d2, 1)
                    pool.wait_ge(s_d4, g * 4 + (q + 1))
                    tt(t2, h0b[:, q], bcb[:, 1], ALU.mult).then_inc(s_d5, 1)

            def sums(n, j0):
                nc.gpsimd.memset(nacc, 0.0).then_inc(s_nz2, 1)
                pool.wait_ge(s_nz2, 1 + n)
                pool.sem_inc(s_pass, 1)
                with pool.Fori(0, KT) as m:
                    pool.wait_ge(s_psfree, m + (j0 + 3))
                    pool.wait_ge(s_nsum, m + (8 * n + 2))
                    tt(nacc, nacc, res[:, ds(m, 1), :].rearrange("p o t -> p (o t)"), ALU.add).then_inc(s_nsum, 1)

            pool.wait_ge(s_mix, 8)
            sums(0, J_OUT)
            with pool.Fori(0, 32) as m:
                pool.wait_ge(s_psfree, m + (J_UP + 3))
                t = hidT[:, ds(m, 1), :]
                tt(t, t, t, ALU.mult).then_inc(s_hid, 1)
            sums(1, J_DOWN)


_INS = ['x_prompt', 'x_sample', 'cache_k', 'cache_v', 'state_ssm', 'state_conv', 'page_table',
        'w_in', 'conv_w', 'conv_b', 'dt_bias', 'a_log', 'd_skip', 'ssm_norm_w', 'w_ssm_br', 'w_attn_br',
        'sb_logit_bias', 'w_out', 'ln1_g', 'ln1_b', 'w_up', 'w_down', 'ln2_g', 'ln2_b']
_OUTS = [(1, 1024, 1024), (8, 1, 1024), (1, 1, 1024, 4, 64), (1, 1, 1024, 4, 64), (1, 1, 32, 64, 128),
         (1, 1, 3, 3072), (1, 8, 1, 4, 64), (1, 8, 1, 4, 64), (1, 8, 32, 64, 128), (1, 8, 3, 3072)]


def kernel(**inputs):
    import numpy as _np
    import concourse.bacc as _bacc
    from concourse import mybir as _mybir
    from concourse.bass_utils import run_bass_kernel_spmd as _run

    nc = _bacc.Bacc("TRN2", target_bir_lowering=False, num_devices=1)
    arrays, ins, outs = {}, {}, []
    for name in _INS:
        a = _np.ascontiguousarray(inputs[name])
        arrays[f"in_{name}_dram"] = a
        ins[name] = nc.dram_tensor(f"in_{name}_dram", a.shape, _mybir.dt.from_np(a.dtype), kind="ExternalInput").ap()
    for i, shape in enumerate(_OUTS):
        outs.append(nc.dram_tensor(f"out_{i}_dram", shape, _mybir.dt.float32, kind="ExternalOutput").ap())
    build(nc, ins, outs)
    r = _run(nc, [arrays], core_ids=[0])
    return tuple(r.results[0][f"out_{i}_dram"] for i in range(len(_OUTS)))
```
